# Optimizing a Trainium2 kernel written in Bass

```python
import math
import jax, jax.numpy as jnp
from jax import lax
import numpy as np

D_MODEL = 1024
BATCH = 1
SEQ = 512
DEPTH = 2

GRID_W = 64
CTX_LEN = 256
D_MIX = D_MODEL
MLSTM_HEADS = 4
MLSTM_WIDTH = D_MIX // 2
MLSTM_HD = MLSTM_WIDTH // MLSTM_HEADS
MLSTM_CHUNK = 64
SHORT_CONV = 3
N_GATES = 4 * MLSTM_HEADS
FOURIER_HEADS = 4
FOURIER_WIDTH = D_MIX // 4
FOURIER_HD = FOURIER_WIDTH // FOURIER_HEADS
CONV_WIDTH = D_MIX - MLSTM_WIDTH - FOURIER_WIDTH
CONV_K = 31
D_FF = 4 * D_MODEL
Q_OFF = 0
K_OFF = MLSTM_WIDTH
V_OFF = 2 * MLSTM_WIDTH
O_OFF = 3 * MLSTM_WIDTH
G_OFF = 4 * MLSTM_WIDTH
MLSTM_COLS = 4 * MLSTM_WIDTH + N_GATES
F_OFF = MLSTM_COLS
C_OFF = F_OFF + FOURIER_WIDTH
P_IN = C_OFF + 2 * CONV_WIDTH
EPS = 1e-6
POS_BASE = 10000.0


def rmsnorm(x, g):
    xf = x.astype(jnp.float32)
    y = xf * lax.rsqrt(jnp.mean(xf * xf, axis=-1, keepdims=True) + EPS)
    return (y * g.astype(jnp.float32)).astype(x.dtype)

def layernorm(x, g, b):
    xf = x.astype(jnp.float32)
    mu = jnp.mean(xf, axis=-1, keepdims=True)
    var = jnp.mean(jnp.square(xf - mu), axis=-1, keepdims=True)
    y = (xf - mu) * lax.rsqrt(var + EPS)
    return (y * g.astype(jnp.float32) + b.astype(jnp.float32)).astype(x.dtype)

def modulate(h, shift, scale):
    return h * (1 + scale) + shift

def grid_sincos(rows, d):
    quarter = d // 4
    freq = jnp.exp(-math.log(POS_BASE) * jnp.arange(quarter, dtype=jnp.float32) / quarter)
    r = jnp.broadcast_to(jnp.arange(rows, dtype=jnp.float32)[:, None], (rows, GRID_W)).reshape(-1)
    col = jnp.broadcast_to(jnp.arange(GRID_W, dtype=jnp.float32)[None, :], (rows, GRID_W)).reshape(-1)
    ar = r[:, None] * freq
    ac = col[:, None] * freq
    return jnp.concatenate([jnp.sin(ar), jnp.cos(ar), jnp.sin(ac), jnp.cos(ac)], axis=-1)

def dwconv(u, w):
    k = w.shape[0]
    ch = u.shape[-1]
    return lax.conv_general_dilated(u, w[:, None, :], window_strides=(1,), padding=[(k // 2, k // 2)],
                                    dimension_numbers=('NWC', 'WIO', 'NWC'), feature_group_count=ch)

def mlstm_chunked(q, k, v, li, lf, state):
    b_, h_, t_, hd = q.shape
    nc = t_ // MLSTM_CHUNK
    L = MLSTM_CHUNK

    def to_chunks(a):
        return jnp.moveaxis(a.reshape(a.shape[:2] + (nc, L) + a.shape[3:]), 2, 0)

    tri = jnp.tril(jnp.ones((L, L), dtype=bool))

    def step(carry, inp):
        C, n, m = carry
        qc, kc, vc, lic, lfc = inp
        bcum = jnp.cumsum(lfc, axis=-1)
        a = bcum + m[..., None]
        D = bcum[..., :, None] - bcum[..., None, :] + lic[..., None, :]
        D = jnp.where(tri, D, -jnp.inf)
        m_t = jnp.maximum(a, jnp.max(D, axis=-1))
        w_inter = jnp.exp(a - m_t)
        S = jnp.einsum('bhld,bhsd->bhls', qc, kc) * jnp.exp(D - m_t[..., None])
        num = w_inter[..., None] * jnp.einsum('bhed,bhld->bhle', C, qc) + jnp.einsum('bhls,bhse->bhle', S, vc)
        den = w_inter * jnp.einsum('bhd,bhld->bhl', n, qc) + jnp.sum(S, axis=-1)
        h = num / jnp.maximum(jnp.abs(den), jnp.exp(-m_t))[..., None]
        bl = bcum[..., -1]
        g = bl[..., None] - bcum + lic
        m_new = jnp.maximum(bl + m, jnp.max(g, axis=-1))
        decay = jnp.exp(bl + m - m_new)
        ws = jnp.exp(g - m_new[..., None])
        C_new = decay[..., None, None] * C + jnp.einsum('bhs,bhse,bhsd->bhed', ws, vc, kc)
        n_new = decay[..., None] * n + jnp.einsum('bhs,bhsd->bhd', ws, kc)
        return (C_new, n_new, m_new), h

    final, hs = lax.scan(step, state, (to_chunks(q), to_chunks(k), to_chunks(v), to_chunks(li), to_chunks(lf)))
    h = jnp.moveaxis(hs, 0, 2).reshape(b_, h_, t_, hd)
    return h, final

def mlstm_heads(z, w_qk_conv, b_gate):
    b_, t_, _ = z.shape
    qk = dwconv(z[..., Q_OFF:V_OFF], w_qk_conv)

    def heads(a):
        return a.reshape(b_, t_, MLSTM_HEADS, MLSTM_HD).transpose(0, 2, 1, 3).astype(jnp.float32)

    q = heads(qk[..., :MLSTM_WIDTH])
    k = heads(qk[..., MLSTM_WIDTH:]) * (MLSTM_HD ** -0.5)
    v = heads(z[..., V_OFF:O_OFF])
    gates = (z[..., G_OFF:G_OFF + N_GATES].reshape(b_, t_, 4, MLSTM_HEADS) + b_gate).astype(jnp.float32)
    gates = gates.transpose(2, 0, 3, 1)
    fwd = (gates[0], jax.nn.log_sigmoid(gates[1]))
    bwd = (gates[2], jax.nn.log_sigmoid(gates[3]))
    return q, k, v, fwd, bwd

def mlstm_out(h, o_pre, g):
    b_, h_, t_, hd = h.shape
    mu = jnp.mean(h, axis=-1, keepdims=True)
    var = jnp.mean(jnp.square(h - mu), axis=-1, keepdims=True)
    hn = ((h - mu) * lax.rsqrt(var + EPS)).transpose(0, 2, 1, 3).reshape(b_, t_, h_ * hd)
    return (hn * g.astype(jnp.float32) * jax.nn.sigmoid(o_pre.astype(jnp.float32))).astype(o_pre.dtype)

def mlstm_mixer(zx, zc, w_qk_conv, b_gate, g_norm, need_ctx):
    qx, kx, vx, fx, bx = mlstm_heads(zx, w_qk_conv, b_gate)
    qc, kc, vc, fc, bc = mlstm_heads(zc, w_qk_conv, b_gate)
    bsz = zx.shape[0]
    zero = (jnp.zeros((bsz, MLSTM_HEADS, MLSTM_HD, MLSTM_HD), jnp.float32),
            jnp.zeros((bsz, MLSTM_HEADS, MLSTM_HD), jnp.float32),
            jnp.zeros((bsz, MLSTM_HEADS), jnp.float32))

    def fl(a):
        return jnp.flip(a, axis=2)

    hc_f, st_f = mlstm_chunked(qc, kc, vc, fc[0], fc[1], zero)
    hx_f, _ = mlstm_chunked(qx, kx, vx, fx[0], fx[1], st_f)
    hc_b, st_b = mlstm_chunked(fl(qc), fl(kc), fl(vc), fl(bc[0]), fl(bc[1]), zero)
    hx_b, _ = mlstm_chunked(fl(qx), fl(kx), fl(vx), fl(bx[0]), fl(bx[1]), st_b)
    yx = mlstm_out(hx_f + fl(hx_b), zx[..., O_OFF:G_OFF], g_norm)
    yc = mlstm_out(hc_f + fl(hc_b), zc[..., O_OFF:G_OFF], g_norm) if need_ctx else None
    return yx, yc

def fourier_mix(u):
    b_, t_, _ = u.shape
    uh = u.reshape(b_, t_, FOURIER_HEADS, FOURIER_HD).astype(jnp.float32)
    y = jnp.real(jnp.fft.fftn(uh, axes=(1, 3), norm='ortho'))
    return y.reshape(b_, t_, FOURIER_WIDTH).astype(u.dtype)

def conv_module(z, w_dw, b_dw, g_ln, b_ln):
    a, gt = z[..., :CONV_WIDTH], z[..., CONV_WIDTH:]
    u = a * jax.nn.sigmoid(gt)
    u = dwconv(u, w_dw) + b_dw
    return jax.nn.silu(layernorm(u, g_ln, b_ln))

def token_mixers(hx, hc, w_in, w_out, b_gate, w_qk_conv, g_mlstm_norm, w_dw, b_dw, g_conv_ln, b_conv_ln, need_ctx):
    zx = hx @ w_in
    zc = hc @ (w_in if need_ctx else w_in[:, :MLSTM_COLS])
    ym_x, ym_c = mlstm_mixer(zx, zc, w_qk_conv, b_gate, g_mlstm_norm, need_ctx)

    def merge(z, ym):
        yf = fourier_mix(z[..., F_OFF:C_OFF])
        yv = conv_module(z[..., C_OFF:P_IN], w_dw, b_dw, g_conv_ln, b_conv_ln)
        return jnp.concatenate([ym, yf, yv], axis=-1) @ w_out

    out_x = merge(zx, ym_x)
    out_c = merge(zc, ym_c) if need_ctx else None
    return out_x, out_c

def sq_relu_mlp(h, w1, w2):
    return jnp.square(jax.nn.relu(h @ w1)) @ w2

def first_inputs(seed: int = 0) -> dict:
    key = jax.random.key(seed)
    ks = jax.random.split(key, 24)
    f32 = jnp.float32
    L = DEPTH

    def nrm(k, shape, scale):
        return jax.random.normal(k, shape, f32) * scale

    def gain(k, shape):
        return 1.0 + nrm(k, shape, 0.05)

    return {
        'x': nrm(ks[0], (BATCH, SEQ, D_MODEL), 1.0),
        'c': nrm(ks[1], (BATCH, D_MODEL), 1.0),
        'ctx': nrm(ks[2], (BATCH, CTX_LEN, D_MODEL), 1.0),
        'c_ctx': nrm(ks[3], (D_MODEL,), 1.0),
        'w_ada': nrm(ks[4], (L, D_MODEL, 6 * D_MODEL), D_MODEL ** -0.5),
        'b_ada': nrm(ks[5], (L, 6 * D_MODEL), 0.02),
        'g_pre_mix': gain(ks[6], (L, D_MODEL)),
        'g_post_mix': gain(ks[7], (L, D_MODEL)),
        'g_pre_mlp': gain(ks[8], (L, D_MODEL)),
        'g_post_mlp': gain(ks[9], (L, D_MODEL)),
        'w_in': nrm(ks[10], (L, D_MODEL, P_IN), D_MODEL ** -0.5),
        'b_gate': jnp.array([0.0, 3.0, 0.0, 3.0], f32)[None, :, None] + nrm(ks[11], (L, 4, MLSTM_HEADS), 0.1),
        'w_qk_conv': nrm(ks[12], (L, SHORT_CONV, 2 * MLSTM_WIDTH), SHORT_CONV ** -0.5),
        'g_mlstm_norm': gain(ks[13], (L, MLSTM_WIDTH)),
        'w_dw': nrm(ks[14], (L, CONV_K, CONV_WIDTH), CONV_K ** -0.5),
        'b_dw': nrm(ks[15], (L, CONV_WIDTH), 0.02),
        'g_conv_ln': gain(ks[16], (L, CONV_WIDTH)),
        'b_conv_ln': nrm(ks[17], (L, CONV_WIDTH), 0.02),
        'w_out': nrm(ks[18], (L, D_MIX, D_MODEL), D_MIX ** -0.5),
        'w_mlp1': nrm(ks[19], (L, D_MODEL, D_FF), D_MODEL ** -0.5),
        'w_mlp2': nrm(ks[20], (L, D_FF, D_MODEL), D_FF ** -0.5),
    }

def first_block(x, c, ctx, c_ctx, w_ada, b_ada, g_pre_mix, g_post_mix, g_pre_mlp, g_post_mlp, w_in, b_gate,
              w_qk_conv, g_mlstm_norm, w_dw, b_dw, g_conv_ln, b_conv_ln, w_out, w_mlp1, w_mlp2):
    n_tok = x.shape[1]
    rows = n_tok // GRID_W
    x = x + grid_sincos(rows, x.shape[-1]).astype(x.dtype)[None]
    for l in range(DEPTH):
        need_ctx = l < DEPTH - 1
        mx = jnp.split((jax.nn.silu(c) @ w_ada[l] + b_ada[l])[:, None, :], 6, axis=-1)
        mc = jnp.split((jax.nn.silu(c_ctx) @ w_ada[l] + b_ada[l])[None, None, :], 6, axis=-1)
        hx = modulate(rmsnorm(x, g_pre_mix[l]), mx[0], mx[1])
        hc = modulate(rmsnorm(ctx, g_pre_mix[l]), mc[0], mc[1])
        out_x, out_c = token_mixers(hx, hc, w_in[l], w_out[l], b_gate[l], w_qk_conv[l], g_mlstm_norm[l],
                                    w_dw[l], b_dw[l], g_conv_ln[l], b_conv_ln[l], need_ctx)
        x = x + mx[2] * rmsnorm(out_x, g_post_mix[l])
        hx = modulate(rmsnorm(x, g_pre_mlp[l]), mx[3], mx[4])
        x = x + mx[5] * rmsnorm(sq_relu_mlp(hx, w_mlp1[l], w_mlp2[l]), g_post_mlp[l])
        if need_ctx:
            ctx = ctx + mc[2] * rmsnorm(out_c, g_post_mix[l])
            hc = modulate(rmsnorm(ctx, g_pre_mlp[l]), mc[3], mc[4])
            ctx = ctx + mc[5] * rmsnorm(sq_relu_mlp(hc, w_mlp1[l], w_mlp2[l]), g_post_mlp[l])
    return x


DEPTH_2 = 1

HEAD_DIM = 64
NSA_HEADS = 8
NSA_KV_HEADS = 2
NSA_GROUP = NSA_HEADS // NSA_KV_HEADS
NSA_WIDTH = NSA_HEADS * HEAD_DIM
KV_WIDTH = NSA_KV_HEADS * HEAD_DIM
N_BRANCH = 3
CMP_LEN = 32
CMP_STRIDE = 16
SEL_BLOCK = 64
SEL_TOPK = 16
WINDOW = 512
FORCE_SCORE = 1e4
POOL_WINDOWS = (2, 4, 8, 16)
POOL_GROUPS = 4
POOL_GROUP_DIM = 64
POOL_WIDTH = POOL_GROUPS * POOL_GROUP_DIM
MEM_HEADS = 4
MEM_LEN = 256
MEM_WIDTH = MEM_HEADS * HEAD_DIM
MIX_WIDTH = NSA_WIDTH + POOL_WIDTH + MEM_WIDTH
ROPE_THETA = 500000.0
ROPE_DIM = HEAD_DIM // 4
Q_BLOCK = 32
IN_SPLITS = (NSA_WIDTH, 6 * KV_WIDTH, NSA_HEADS * N_BRANCH, NSA_WIDTH,
             POOL_WIDTH, POOL_WIDTH, MEM_WIDTH, MEM_WIDTH)
IN_WIDTH = sum(IN_SPLITS)


def rms_norm(x, g):
    x32 = x.astype(jnp.float32)
    y = x32 * lax.rsqrt(jnp.mean(x32 * x32, axis=-1, keepdims=True) + EPS)
    return (y * g.astype(jnp.float32)).astype(x.dtype)

def partial_rope(x, pos):
    half = ROPE_DIM // 2
    inv_freq = ROPE_THETA ** (-jnp.arange(half, dtype=jnp.float32) / half)
    ang = pos.astype(jnp.float32)[:, None, :, None] * inv_freq
    cos, sin = jnp.cos(ang), jnp.sin(ang)
    x32 = x.astype(jnp.float32)
    x1, x2 = x32[..., :half], x32[..., half:ROPE_DIM]
    out = jnp.concatenate([x1 * cos - x2 * sin, x1 * sin + x2 * cos, x32[..., ROPE_DIM:]], axis=-1)
    return out.astype(x.dtype)

def masked_softmax(s, mask):
    s = jnp.where(mask, s, -jnp.inf)
    m = jnp.max(s, axis=-1, keepdims=True)
    m = jnp.where(jnp.isfinite(m), m, 0.0)
    e = jnp.where(mask, jnp.exp(s - m), 0.0)
    return e / jnp.maximum(jnp.sum(e, axis=-1, keepdims=True), jnp.finfo(jnp.float32).tiny)

def compress_blocks(kv_raw, pos_emb, w1, w2):
    S = kv_raw.shape[1]
    nc = (S - CMP_LEN) // CMP_STRIDE + 1
    idx = np.arange(nc)[:, None] * CMP_STRIDE + np.arange(CMP_LEN)[None, :]
    blocks = kv_raw[:, idx] + pos_emb[None, None, :, None, :]
    hid = jax.nn.gelu(jnp.einsum('bnlgd,lde->bgne', blocks, w1))
    return jnp.einsum('bgne,ef->bgnf', hid, w2)

def cmp_to_sel_map(nc, ns):
    c0 = np.arange(nc) * CMP_STRIDE
    c1 = c0 + CMP_LEN
    s0 = np.arange(ns) * SEL_BLOCK
    s1 = s0 + SEL_BLOCK
    ov = np.clip(np.minimum(c1[:, None], s1[None, :]) - np.maximum(c0[:, None], s0[None, :]), 0, None)
    return (ov / CMP_LEN).astype(np.float32)

def nsa_mixer(q_n, kv_n, gate_n, positions, g_q_nsa, g_k_cmp, g_k_slc, g_k_win,
              cmp_pos_k, w_cmp_k1, w_cmp_k2, cmp_pos_v, w_cmp_v1, w_cmp_v2):
    B, S, _ = q_n.shape
    G, R, hd = NSA_KV_HEADS, NSA_GROUP, HEAD_DIM
    dt = q_n.dtype
    scale = HEAD_DIM ** -0.5
    nc = (S - CMP_LEN) // CMP_STRIDE + 1
    ns = S // SEL_BLOCK
    top_n = min(SEL_TOPK, ns)

    q = q_n.reshape(B, S, NSA_HEADS, hd).transpose(0, 2, 1, 3)
    q = partial_rope(rms_norm(q, g_q_nsa), positions)
    kv = kv_n.reshape(B, S, 6, G, hd)
    kc_raw, vc_raw = kv[:, :, 0], kv[:, :, 1]
    k_s, v_s = kv[:, :, 2].transpose(0, 2, 1, 3), kv[:, :, 3].transpose(0, 2, 1, 3)
    k_w, v_w = kv[:, :, 4].transpose(0, 2, 1, 3), kv[:, :, 5].transpose(0, 2, 1, 3)

    end_idx = np.arange(nc) * CMP_STRIDE + CMP_LEN - 1
    k_c = compress_blocks(kc_raw, cmp_pos_k, w_cmp_k1, w_cmp_k2)
    k_c = partial_rope(rms_norm(k_c, g_k_cmp), positions[:, end_idx])
    v_c = compress_blocks(vc_raw, cmp_pos_v, w_cmp_v1, w_cmp_v2)

    k_s = partial_rope(rms_norm(k_s, g_k_slc), positions)
    kb = k_s.reshape(B, G, ns, SEL_BLOCK, hd)
    vb = v_s.reshape(B, G, ns, SEL_BLOCK, hd)

    k_w = partial_rope(rms_norm(k_w, g_k_win), positions)
    pad = ((0, 0), (0, 0), (WINDOW, 0), (0, 0))
    kw_pad, vw_pad = jnp.pad(k_w, pad), jnp.pad(v_w, pad)

    gates = jax.nn.sigmoid(gate_n.astype(jnp.float32)).reshape(B, S, NSA_HEADS, N_BRANCH)
    gates = gates.transpose(0, 2, 1, 3).astype(dt)

    sel_map = jnp.asarray(cmp_to_sel_map(nc, ns))
    end_idx_j = jnp.asarray(end_idx)
    blk = jnp.arange(ns)
    b_ix = jnp.arange(B)[:, None, None, None]
    g_ix = jnp.arange(G)[None, :, None, None]

    def query_block(i):
        start = i * Q_BLOCK
        t = start + jnp.arange(Q_BLOCK)
        qb = lax.dynamic_slice_in_dim(q, start, Q_BLOCK, axis=2).reshape(B, G, R, Q_BLOCK, hd)

        s_c = jnp.einsum('bgrqd,bgnd->bgrqn', qb, k_c, preferred_element_type=jnp.float32) * scale
        c_mask = end_idx_j[None, :] <= t[:, None]
        p_c = masked_softmax(s_c, c_mask)
        o_c = jnp.einsum('bgrqn,bgnd->bgrqd', p_c.astype(dt), v_c)

        imp = jnp.einsum('bgqn,nj->bgqj', jnp.sum(p_c, axis=2), sel_map)
        cur = t // SEL_BLOCK
        forced = (blk[None, :] == 0) | (blk[None, :] == cur[:, None]) | (blk[None, :] == cur[:, None] - 1)
        valid = blk[None, :] <= cur[:, None]
        imp = jnp.where(forced, FORCE_SCORE, jnp.where(valid, imp, -1.0))
        _, sel = lax.top_k(imp, top_n)
        ks_g = kb[b_ix, g_ix, sel]
        vs_g = vb[b_ix, g_ix, sel]
        s_pos = (sel[..., None] * SEL_BLOCK + jnp.arange(SEL_BLOCK)).reshape(B, G, Q_BLOCK, top_n * SEL_BLOCK)
        s_mask = (s_pos <= t[None, None, :, None])[:, :, None]
        s_s = jnp.einsum('bgrqd,bgqkld->bgrqkl', qb, ks_g, preferred_element_type=jnp.float32)
        s_s = s_s.reshape(B, G, R, Q_BLOCK, top_n * SEL_BLOCK) * scale
        p_s = masked_softmax(s_s, s_mask).reshape(B, G, R, Q_BLOCK, top_n, SEL_BLOCK)
        o_s = jnp.einsum('bgrqkl,bgqkld->bgrqd', p_s.astype(dt), vs_g)

        kw_blk = lax.dynamic_slice_in_dim(kw_pad, start, WINDOW + Q_BLOCK, axis=2)
        vw_blk = lax.dynamic_slice_in_dim(vw_pad, start, WINDOW + Q_BLOCK, axis=2)
        kpos = start - WINDOW + jnp.arange(WINDOW + Q_BLOCK)
        w_mask = (kpos[None, :] <= t[:, None]) & (kpos[None, :] > t[:, None] - WINDOW) & (kpos[None, :] >= 0)
        s_w = jnp.einsum('bgrqd,bgkd->bgrqk', qb, kw_blk, preferred_element_type=jnp.float32) * scale
        p_w = masked_softmax(s_w, w_mask)
        o_w = jnp.einsum('bgrqk,bgkd->bgrqd', p_w.astype(dt), vw_blk)

        gb = lax.dynamic_slice_in_dim(gates, start, Q_BLOCK, axis=2).reshape(B, G, R, Q_BLOCK, N_BRANCH)
        o = gb[..., 0:1] * o_c + gb[..., 1:2] * o_s + gb[..., 2:3] * o_w
        return o.reshape(B, NSA_HEADS, Q_BLOCK, hd)

    o_blocks = lax.map(query_block, jnp.arange(S // Q_BLOCK))
    return o_blocks.transpose(1, 0, 3, 2, 4).reshape(B, S, NSA_WIDTH)

def pool_mixer(v_p, w_pool, pool_scale):
    B, S, _ = v_p.shape
    v32 = v_p.reshape(B, S, POOL_GROUPS, POOL_GROUP_DIM).astype(jnp.float32)
    cs = jnp.cumsum(v32, axis=1)
    count_base = jnp.arange(1, S + 1, dtype=jnp.float32)
    pooled = []
    for g, w in enumerate(POOL_WINDOWS):
        c = cs[:, :, g]
        lower = jnp.pad(c[:, :S - w], ((0, 0), (w, 0), (0, 0)))
        cnt = jnp.minimum(count_base, float(w))[None, :, None]
        pooled.append((c - lower) / cnt - v32[:, :, g])
    pooled = jnp.stack(pooled, axis=2).astype(v_p.dtype)
    out = jnp.einsum('bsgc,gce->bsge', pooled, w_pool).reshape(B, S, POOL_WIDTH)
    return out * pool_scale

def memory_mixer(q_m, mem, g_mem, w_mem_kv, g_q_mem, g_k_mem):
    B, S, _ = q_m.shape
    M = mem.shape[1]
    scale = HEAD_DIM ** -0.5
    m_h = rms_norm(mem, g_mem)
    mkv = jnp.einsum('bmd,de->bme', m_h, w_mem_kv).reshape(B, M, 2, MEM_HEADS, HEAD_DIM)
    mk = rms_norm(mkv[:, :, 0], g_k_mem)
    mv = mkv[:, :, 1]
    mq = rms_norm(q_m.reshape(B, S, MEM_HEADS, HEAD_DIM), g_q_mem)
    s_m = jnp.einsum('bshd,bmhd->bhsm', mq, mk, preferred_element_type=jnp.float32) * scale
    p_m = jax.nn.softmax(s_m, axis=-1)
    return jnp.einsum('bhsm,bmhd->bshd', p_m.astype(q_m.dtype), mv).reshape(B, S, MEM_WIDTH)

def hybrid_layer(x, mem, positions, g_norm, w_in, g_q_nsa, g_k_cmp, g_k_slc, g_k_win,
                 cmp_pos_k, w_cmp_k1, w_cmp_k2, cmp_pos_v, w_cmp_v1, w_cmp_v2,
                 w_pool, pool_scale, g_mem, w_mem_kv, g_q_mem, g_k_mem, w_out):
    h = rms_norm(x, g_norm)
    proj = jnp.einsum('bsd,de->bse', h, w_in)
    split_at = np.cumsum(IN_SPLITS)[:-1].tolist()
    q_n, kv_n, gate_n, z_n, v_p, z_p, q_m, z_m = jnp.split(proj, split_at, axis=-1)
    o_nsa = nsa_mixer(q_n, kv_n, gate_n, positions, g_q_nsa, g_k_cmp, g_k_slc, g_k_win,
                      cmp_pos_k, w_cmp_k1, w_cmp_k2, cmp_pos_v, w_cmp_v1, w_cmp_v2)
    o_pool = pool_mixer(v_p, w_pool, pool_scale)
    o_mem = memory_mixer(q_m, mem, g_mem, w_mem_kv, g_q_mem, g_k_mem)
    y = jnp.concatenate([o_nsa * jax.nn.silu(z_n),
                         o_pool * jax.nn.silu(z_p),
                         o_mem * jax.nn.silu(z_m)], axis=-1)
    return x + jnp.einsum('bse,ed->bsd', y, w_out)

def second_inputs(seed: int = 0) -> dict:
    key = jax.random.key(seed)
    ks = jax.random.split(key, 24)
    f32 = jnp.float32
    L = DEPTH_2

    def nrm(k, shape, s):
        return jax.random.normal(k, shape, f32) * s

    def gain(k, shape):
        return 1.0 + 0.01 * jax.random.normal(k, shape, f32)

    x = nrm(ks[0], (BATCH, SEQ, D_MODEL), 1.0)
    mem = nrm(ks[1], (BATCH, MEM_LEN, D_MODEL), 1.0)
    positions = (jnp.arange(SEQ, dtype=jnp.int32)[None, :]
                 + jax.random.randint(ks[2], (BATCH, 1), 0, 1024, dtype=jnp.int32))
    return {
        "x": x,
        "mem": mem,
        "positions": positions,
        "g_norm": gain(ks[3], (L, D_MODEL)),
        "w_in": nrm(ks[4], (L, D_MODEL, IN_WIDTH), D_MODEL ** -0.5),
        "g_q_nsa": gain(ks[5], (L, HEAD_DIM)),
        "g_k_cmp": gain(ks[6], (L, HEAD_DIM)),
        "g_k_slc": gain(ks[7], (L, HEAD_DIM)),
        "g_k_win": gain(ks[8], (L, HEAD_DIM)),
        "cmp_pos_k": nrm(ks[9], (L, CMP_LEN, HEAD_DIM), 0.1),
        "w_cmp_k1": nrm(ks[10], (L, CMP_LEN, HEAD_DIM, HEAD_DIM), (CMP_LEN * HEAD_DIM) ** -0.5),
        "w_cmp_k2": nrm(ks[11], (L, HEAD_DIM, HEAD_DIM), HEAD_DIM ** -0.5),
        "cmp_pos_v": nrm(ks[12], (L, CMP_LEN, HEAD_DIM), 0.1),
        "w_cmp_v1": nrm(ks[13], (L, CMP_LEN, HEAD_DIM, HEAD_DIM), (CMP_LEN * HEAD_DIM) ** -0.5),
        "w_cmp_v2": nrm(ks[14], (L, HEAD_DIM, HEAD_DIM), HEAD_DIM ** -0.5),
        "w_pool": nrm(ks[15], (L, POOL_GROUPS, POOL_GROUP_DIM, POOL_GROUP_DIM), POOL_GROUP_DIM ** -0.5),
        "pool_scale": gain(ks[16], (L, POOL_WIDTH)),
        "g_mem": gain(ks[17], (L, D_MODEL)),
        "w_mem_kv": nrm(ks[18], (L, D_MODEL, 2 * MEM_WIDTH), D_MODEL ** -0.5),
        "g_q_mem": gain(ks[19], (L, HEAD_DIM)),
        "g_k_mem": gain(ks[20], (L, HEAD_DIM)),
        "w_out": nrm(ks[21], (L, MIX_WIDTH, D_MODEL), MIX_WIDTH ** -0.5),
    }

def second_block(x, mem, positions, g_norm, w_in, g_q_nsa, g_k_cmp, g_k_slc, g_k_win,
              cmp_pos_k, w_cmp_k1, w_cmp_k2, cmp_pos_v, w_cmp_v1, w_cmp_v2,
              w_pool, pool_scale, g_mem, w_mem_kv, g_q_mem, g_k_mem, w_out):
    for l in range(DEPTH_2):
        x = hybrid_layer(x, mem, positions, g_norm[l], w_in[l], g_q_nsa[l], g_k_cmp[l],
                         g_k_slc[l], g_k_win[l], cmp_pos_k[l], w_cmp_k1[l], w_cmp_k2[l],
                         cmp_pos_v[l], w_cmp_v1[l], w_cmp_v2[l], w_pool[l], pool_scale[l],
                         g_mem[l], w_mem_kv[l], g_q_mem[l], g_k_mem[l], w_out[l])
    return x


_first_inputs = second_inputs


def second_inputs(seed=0):
    import zlib

    import numpy as np

    out = dict(_first_inputs(seed))
    spreads = {}
    factors = {'g_norm': 8.0,
     'g_q_nsa': 8.0,
     'g_k_cmp': 8.0,
     'g_k_slc': 8.0,
     'g_k_win': 8.0,
     'cmp_pos_k': 8.0,
     'cmp_pos_v': 4.918,
     'pool_scale': 8.0,
     'g_mem': 8.0,
     'g_q_mem': 8.0,
     'g_k_mem': 8.0}
    for name, (base, spread) in spreads.items():
        noise = np.random.default_rng([zlib.crc32(name.encode()), seed]).standard_normal(out[name].shape)
        drawn = base * np.exp(spread * noise) if base else spread * noise
        out[name] = __import__('jax').numpy.asarray(drawn.astype(out[name].dtype))
    for name, factor in factors.items():
        out[name] = (out[name] * factor).astype(out[name].dtype)
    return out


_narrow_inputs = second_inputs


def second_inputs(seed=0):

    out = dict(_narrow_inputs(seed))
    wider = {'g_q_nsa': 4.42,
     'g_k_cmp': 12.0,
     'g_k_slc': 7.29,
     'g_k_win': 6.74,
     'cmp_pos_v': 11.69,
     'pool_scale': 6.33,
     'g_mem': 6.85,
     'g_q_mem': 6.99,
     'g_k_mem': 6.48}
    for name, times in wider.items():
        mean = out[name].mean()
        out[name] = (mean + times * (out[name] - mean)).astype(out[name].dtype)
    return out


def setup_inputs(seed=0):
    out = dict(first_inputs(seed))
    for name, value in second_inputs(seed + 1).items():
        if name != "x":
            out[name + "_2"] = value
    return out


def reference(
    x, c, ctx, c_ctx, w_ada, b_ada, g_pre_mix, g_post_mix, g_pre_mlp, g_post_mlp, w_in, b_gate,
    w_qk_conv, g_mlstm_norm, w_dw, b_dw, g_conv_ln, b_conv_ln, w_out, w_mlp1, w_mlp2, mem_2,
    positions_2, g_norm_2, w_in_2, g_q_nsa_2, g_k_cmp_2, g_k_slc_2, g_k_win_2, cmp_pos_k_2,
    w_cmp_k1_2, w_cmp_k2_2, cmp_pos_v_2, w_cmp_v1_2, w_cmp_v2_2, w_pool_2, pool_scale_2,
    g_mem_2, w_mem_kv_2, g_q_mem_2, g_k_mem_2, w_out_2,
):
    x = first_block(
        x, c, ctx, c_ctx, w_ada, b_ada, g_pre_mix, g_post_mix, g_pre_mlp, g_post_mlp, w_in,
        b_gate, w_qk_conv, g_mlstm_norm, w_dw, b_dw, g_conv_ln, b_conv_ln, w_out, w_mlp1,
        w_mlp2,
    )
    return second_block(
        x, mem_2, positions_2, g_norm_2, w_in_2, g_q_nsa_2, g_k_cmp_2, g_k_slc_2, g_k_win_2,
        cmp_pos_k_2, w_cmp_k1_2, w_cmp_k2_2, cmp_pos_v_2, w_cmp_v1_2, w_cmp_v2_2, w_pool_2,
        pool_scale_2, g_mem_2, w_mem_kv_2, g_q_mem_2, g_k_mem_2, w_out_2,
    )


_drawn_inputs = setup_inputs


def setup_inputs(seed=0):
    import zlib

    import numpy as np

    out = dict(_drawn_inputs(seed))
    spreads = {}
    factors = {'b_conv_ln': 2.997, 'cmp_pos_k_2': 2.774}
    for name, (base, spread) in spreads.items():
        noise = np.random.default_rng([zlib.crc32(name.encode()), seed]).standard_normal(out[name].shape)
        drawn = base * np.exp(spread * noise) if base else spread * noise
        out[name] = __import__('jax').numpy.asarray(drawn.astype(out[name].dtype))
    for name, factor in factors.items():
        out[name] = (out[name] * factor).astype(out[name].dtype)
    return out
```

```python
from contextlib import ExitStack

import numpy as np

import concourse.bass as bass
from concourse import mybir

F32 = mybir.dt.float32
I32 = mybir.dt.int32
ALU = mybir.AluOpType
ACT = mybir.ActivationFunctionType
AXX = mybir.AxisListType.X

P = 128
D = 1024
KC = D // P
TX, TC = 512, 256
T = TX + TC
LAYERS = 2
EPS = 1e-6
HEADS = 4
HD = 128
FF = 4096
W_IN = 2832
W_IN2 = 2840
CONV_K = 31
NCMP = (TX - 32) // 16 + 1
SCALE = 64 ** -0.5
UNITS = [("nsa", c, g, tb) for c in range(4) for tb in range(4) for g in range(2)]
UNITS += [("mem", c, g, tb) for c in range(2) for tb in range(4) for g in range(2)]
PAD = CONV_K // 2
BIG = 1e30
TINY = float(np.finfo(np.float32).tiny)
X_COLS, C_COLS = (0, TX), (TX, TC)

LAYER_COLS = [("b_ada", 48), ("g_pre_mix", 8), ("g_post_mix", 8), ("g_pre_mlp", 8), ("g_post_mlp", 8),
              ("g_mlstm_norm", 4), ("w_qk_conv", 24), ("w_dw", 62), ("b_dw", 2), ("g_conv_ln", 2),
              ("b_conv_ln", 2), ("b_gate", 1)]
LAST_COLS = [("g_norm_2", 8), ("g_q_nsa_2", 1), ("g_k_cmp_2", 1), ("g_k_slc_2", 1), ("g_k_win_2", 1),
             ("g_q_mem_2", 1), ("g_k_mem_2", 1), ("pool_scale_2", 2), ("g_mem_2", 8), ("cmp_pos_k_2", 32),
             ("cmp_pos_v_2", 32)]


def column_offsets():
    at, n = {}, 0
    for layer in range(LAYERS):
        for name, k in LAYER_COLS:
            at[name, layer] = n
            n += k
    for name, k in LAST_COLS:
        at[name] = n
        n += k
    return at, n


COL, NCOL = column_offsets()

PANELS = {"conv": (2320, 512), "gates": (2048, 272), "q": (0, 512), "k": (512, 512), "v": (1024, 512),
          "o": (1536, 512)}
PANELS2 = [(0, 512), (512, 512), (1024, 280), (1304, 512), (1816, 512), (2328, 512)]

TWO_PI = 2 * np.pi
ROUND = 1.5 * 2 ** 23
PI_BELOW = 3.1415925


def split_two_pi():
    parts, rest = [], float(TWO_PI)
    for bits in (9, 21):
        part = np.floor(rest * 2.0 ** bits) / 2.0 ** bits
        parts.append(part)
        rest -= part
    return parts + [rest]


TWO_PI_PARTS = split_two_pi()
SLOTS = 3
SLOT = 4096

CONSTS = [("ident", P), ("ones", P), ("ones64", P), ("rope_turn", P), ("dft_chan", 256), ("hide_t_lt_s", P),
          ("hide_t_gt_s", P), ("hide_s_gt_t", P), ("cmp_hide", 128), ("head_rows", 512), ("rope_freq", 1),
          ("eps", 1), ("pool_inv", 2), ("pool_first", 32)]


def const_offsets():
    at, n = {}, 0
    for name, k in CONSTS:
        at[name] = (n, k)
        n += k
    return at, n


CONST, NCONST = const_offsets()


class Signal:

    def __init__(self, sem):
        self.sem, self.made = sem, 0


class Worker:

    def __init__(self, step):
        self.step, self.seen, self.last = step, {}, None

    def up(self, signal=None):
        signal = signal or self.step
        signal.made += 1
        self.last = (signal.sem, signal.made)
        return signal.sem, 1

    def own(self):
        return self.last

    def next(self, signal, n=1):
        self.seen[signal] = self.seen.get(signal, 0) + n
        return signal.sem, self.seen[signal]


def pt_layout():
    at, n = {}, 0
    for d in range(2):
        for s in range(6):
            for group in ((0, 1, 2, 3), (4, 5)):
                for tb in group:
                    if s >= 4 and tb < 4:
                        seen = True
                    elif (s >= 4) != (tb >= 4):
                        seen = False
                    else:
                        seen = tb >= s if d == 0 else tb <= s
                    if seen:
                        at[d, s, tb] = n
                        n += P
    return at, n


PT_AT, PT_SIZE = pt_layout()


def pt_at(d, s, tb):
    return PT_AT.get((d, s, tb))


def build(nc, a):
    with ExitStack() as ctx:
        def sb(name, shape, dt=F32):
            return ctx.enter_context(nc.sbuf_tensor(name, shape, dt))

        def signal(name):
            return Signal(ctx.enter_context(nc.semaphore(name)))

        X = sb("X", [P, KC, T])
        H = sb("H", [P, KC * T])
        R = sb("R", [P, 21504])
        ring = sb("ring", [P, SLOTS, SLOT])
        cols = sb("cols", [P, NCOL])
        con = sb("con", [P, NCONST])
        cvec = sb("cvec", [P, KC, 2])
        mod = sb("mod", [P, LAYERS, 48, 2])
        gsc = sb("gsc", [P, 4, KC, 2])
        rs = sb("rs", [P, T])
        tmp = sb("tmp", [P, 2 * T])
        sq = sb("sq", [P, T])
        acol = sb("acol", [P, 96])
        small = sb("small", [P, 96])
        psum = ctx.enter_context(nc.psum_tensor("psum", [P, 8, 512], F32))

        def part(buf, at, *shape):
            n = int(np.prod(shape))
            v = buf[:, at:at + n]
            if len(shape) == 2:
                return v.rearrange("p (a b) -> p a b", a=shape[0])
            if len(shape) == 3:
                return v.rearrange("p (a b c) -> p a b c", a=shape[0], b=shape[1])
            if len(shape) == 4:
                return v.rearrange("p (a b c d) -> p a b c d", a=shape[0], b=shape[1], c=shape[2])
            return v

        Hc = part(H, 0, KC, T)
        Q = part(R, 0, 4, T)
        K = part(R, 3072, 4, T)
        V = part(R, 6144, 6, 4, 129)
        O = part(R, 9240, 4, T)
        ROWS = part(R, 12312, 4, T)
        FZ = part(R, 15384, 2, T)
        PT = part(R, 12312, PT_SIZE)
        HS = part(R, 17688, 6, 4, 128)
        UPAD = part(R, 17688, 2, 828)
        CV = part(R, 19344, 2, T)
        FA = part(R, 17688, 6, 2, 2, 128)
        HID = part(R, 0, 16, T)
        ACC = part(R, 12288, KC, T)
        GR = part(tmp, 0, 2, T)
        Q2, KS, KW = part(R, 0, 4, TX), part(R, 2048, TX), part(R, 2560, TX)
        KRAW, VRAW = part(R, 3072, TX), part(R, 3584, TX)
        VS, VW = part(R, 4096, 4, P), part(R, 4608, 4, P)
        ZN, VP, ZP = part(R, 5120, 4, TX), part(R, 7168, 2, TX), part(R, 8192, 2, TX)
        QM, ZM = part(R, 9216, 2, TX), part(R, 10240, 2, TX)
        MK, MV = part(R, 11264, 2, TC), part(R, 11776, 2, TC)
        MEM = part(R, 12288, KC, TC)
        KWIN, VWIN = part(R, 14336, NCMP, 32), part(R, 15360, NCMP, 32)
        COS, SIN = part(R, 16384, TX), part(R, 16896, TX)
        PROB = part(R, 17408, 2, 1152)
        GATE = part(R, 19712, 4, 24)
        KCMP, VCMP = part(R, 19808, NCMP), part(R, 19840, P)
        HIDK, HIDV = part(R, 19968, NCMP), part(R, 20000, NCMP)
        POOLT = part(R, 20032, 2, TX)
        PROBT = part(R, 12288, 2, 9, P)
        Y = part(H, 0, KC, TX)

        def const(name):
            at, n = CONST[name]
            return con[:, at:at + n]

        def col(name, i=0, layer=None, n=1):
            at = COL[name if layer is None else (name, layer)] + i
            return cols[:, at:at + n]

        ident, ones, ones64, rope_turn = (const(n) for n in ("ident", "ones", "ones64", "rope_turn"))
        eps = const("eps")

        pe_step, dve_step, act_step = signal("pe_step"), signal("dve_step"), signal("act_step")
        pe_tile_for = {"dve": signal("pe_tile_for_dve"), "act": signal("pe_tile_for_act")}
        dve_bank_free, act_bank_free = signal("dve_bank_free"), signal("act_bank_free")
        bank_free = {"dve": dve_bank_free, "act": act_bank_free}
        dve_ready_pe, act_ready_pe = signal("dve_ready_for_pe"), signal("act_ready_for_pe")
        dve_ready_act, act_ready_dve = signal("dve_ready_for_act"), signal("act_ready_for_dve")
        dve_ready_sp = signal("dve_ready_for_sp")
        slot_loaded = [ctx.enter_context(nc.semaphore(f"slot{i}_loaded")) for i in range(SLOTS)]
        s_first = ctx.enter_context(nc.semaphore("vectors_loaded"))
        s_x = ctx.enter_context(nc.semaphore("x_loaded"))
        s_pos = ctx.enter_context(nc.semaphore("grid_loaded"))
        s_rows = ctx.enter_context(nc.semaphore("gate_rows_moved"))
        s_mem = ctx.enter_context(nc.semaphore("mem_loaded"))
        s_tok = ctx.enter_context(nc.semaphore("positions_loaded"))
        s_out = ctx.enter_context(nc.semaphore("out_stored"))

        panels = []
        marks = {}
        tiles = {"dve": [], "act": []}
        shared = []
        frees = {"dve": 0, "act": 0}
        history = []
        rows_after = {}
        memory_after = []

        block = ctx.enter_context(nc.Block())

        def prob_blocks(u):
            kind, _, _, tb = UNITS[u]
            if kind == "mem":
                return [P, 2 * P]
            n = tb + 1
            return [0] + [P * (1 + i) for i in range(2 * n)]

        heads = [(MK[:, c, :], TC, "g_k_mem_2", None) for c in range(2)]
        heads += [(Q2[:, c, :], TX, "g_q_nsa_2", slice(0, TX)) for c in range(4)]
        heads += [(KS, TX, "g_k_slc_2", slice(0, TX)), (KW, TX, "g_k_win_2", slice(0, TX))]
        heads += [(QM[:, c, :], TX, "g_q_mem_2", None) for c in range(2)]
        heads += [(KCMP, NCMP, "g_k_cmp_2", slice(31, TX, 16))]

        def prob_at(u, j, n):
            return P if UNITS[u][0] == "mem" else (0, P, P + n)[j]

        def Hs_gate(s, n):
            return rs[:, 0:n] if s == 0 else rs[:, TX:TX + n]

        def weights(w, dve, s, d, hd, lo, hi, t0, wv, av):
            if t0 == 0 and s >= 4:
                dve.wait_ge(*w.next(act_ready_dve))
                return
            g = sq_gb(d)[:, t0 + lo:t0 + hi]
            dve.tensor_scalar(wv, g, av[:, s, d, hd:hd + 1], 0.0, ALU.subtract, ALU.max).then_inc(*w.up())
            dve.wait_ge(*w.own())
            o = 0 if d == 0 else hi - lo - P
            hide = const("hide_t_lt_s" if d == 0 else "hide_t_gt_s")
            dve.tensor_tensor(wv[:, o:o + P], wv[:, o:o + P], hide, ALU.add).then_inc(*w.up(dve_ready_act))
            dve.wait_ge(*w.next(act_ready_dve))

        def sq_gb(d):
            return sq if d == 1 else rs

        @block.tensor
        def _(pe):
            w = Worker(pe_step)

            def panel(src, kc, width):
                n = len(panels)
                panels.append([src, kc, width, None])
                pe.wait_ge(slot_loaded[n % SLOTS], 16 * (n // SLOTS + 1))
                return part(ring[:, n % SLOTS], 0, kc, width)

            def panel_done():
                panels[-1][3] = w.last

            def tile(reader, last=None):
                last = last or reader
                n = len(history)
                if n >= 8:
                    r, i = history[n - 8]
                    pe.wait_ge(bank_free[r].sem, i)
                tiles[reader].append(n % 8)
                if last != reader:
                    shared.append(n % 8)
                frees[last] += 1
                history.append((last, frees[last]))
                return psum[:, n % 8]

            def norm_sum(streams, chunks, stationary):
                t = [tile("act") for _ in streams]
                for k in range(chunks):
                    pe.wait_ge(*w.next(act_ready_pe))
                    for (c0, n), b in zip(streams, t):
                        mm = pe.matmul(b[:, 0:n], stationary, Hc[:, k, c0:c0 + n], start=k == 0, stop=k == chunks - 1)
                        if k == chunks - 1:
                            mm.then_inc(*w.up(pe_tile_for["act"]))

            def project(wt, chunk, streams, src, kc, reader):
                for c0, n in streams:
                    b = tile(reader)
                    for k in range(kc):
                        mm = pe.matmul(b[:, 0:n], wt[:, k, chunk * P:chunk * P + P], src(k)[:, c0:c0 + n],
                                       start=k == 0, stop=k == kc - 1)
                    mm.then_inc(*w.up(pe_tile_for[reader]))

            def by_token(wt, blocks, w0, width, src, reader):
                for tb in blocks:
                    b = tile(reader)
                    for k in range(KC):
                        mm = pe.matmul(b[:, 0:width], src(k)[:, tb * P:tb * P + P], wt[:, k, w0:w0 + width],
                                       start=k == 0, stop=k == KC - 1)
                    mm.then_inc(*w.up(pe_tile_for[reader]))

            def ada(layer, first, last):
                for n in range(first, last):
                    wt = panel(a["w_ada"][layer, :, n * 512:(n + 1) * 512], KC, 512)
                    b = tile("dve")
                    for j in range(4):
                        for k in range(KC):
                            mm = pe.matmul(b[:, 2 * j:2 * j + 2], wt[:, k, j * P:j * P + P], cvec[:, k, :],
                                           start=k == 0, stop=k == KC - 1)
                    mm.then_inc(*w.up(pe_tile_for["dve"]))
                    panel_done()

            def layer_program(layer):
                both = layer < LAYERS - 1
                streams = [X_COLS, C_COLS] if both else [X_COLS]
                all_streams = [X_COLS, C_COLS]
                w_in = a["w_in"]

                def win(name):
                    c0, n = PANELS[name]
                    return panel(w_in[layer, :, c0:c0 + n], KC, n)

                def h(k):
                    return Hc[:, k, :]

                norm_sum(all_streams, KC, ones)
                pe.wait_ge(*w.next(act_ready_pe, KC))
                wt = win("conv")
                for m in (2, 0, 3, 1):
                    project(wt, m, streams, h, KC, "act" if m >= 2 else "dve")
                panel_done()
                wt = win("gates")
                for c0, n in all_streams:
                    b = tile("dve")
                    for k in range(KC):
                        mm = pe.matmul(b[0:16, 0:n], wt[:, k, 0:16], h(k)[:, c0:c0 + n], start=k == 0, stop=k == KC - 1)
                    mm.then_inc(*w.up(pe_tile_for["dve"]))
                for m in range(2):
                    for c0, n in streams:
                        b = tile("act")
                        for k in range(KC):
                            mm = pe.matmul(b[:, 0:n], wt[:, k, 16 + m * P:16 + m * P + P], h(k)[:, c0:c0 + n],
                                           start=k == 0, stop=k == KC - 1)
                        mm.then_inc(*w.up(pe_tile_for["act"]))
                panel_done()
                for name, st in (("q", streams), ("k", all_streams)):
                    wt = win(name)
                    for m in range(4):
                        project(wt, m, st, h, KC, "dve")
                    panel_done()
                wt = win("v")
                rows_after[layer] = len(panels)
                by_token(wt, range(6), 0, 512, h, "act")
                panel_done()
                wt = win("o")
                for m in range(4):
                    project(wt, m, streams, h, KC, "act")
                panel_done()
                marks["h_read", layer] = w.last
                ada(layer, 4, 12)
                if both:
                    ada(layer + 1, 0, 4)

                pe.wait_ge(*w.next(dve_ready_pe))
                b = tile("dve")
                for i in range(6):
                    for d in range(2):
                        for e in range(2):
                            o = ((e * 6 + i) * 2 + d) * 4
                            mm = pe.matmul(b[:, o:o + 4], ROWS[0:4, 2 * d + e, i * P:i * P + P], ident[0:4, 0:4],
                                           start=True, stop=True)
                mm.then_inc(*w.up(pe_tile_for["dve"]))
                pe.wait_ge(*w.next(dve_ready_pe))
                for c0, n in streams:
                    b = tile("dve")
                    for k in range(2):
                        mm = pe.matmul(b[:, 0:n], ones, CV[:, k, c0:c0 + n], start=k == 0, stop=k == 1)
                    mm.then_inc(*w.up(pe_tile_for["dve"]))
                t = [tile("act") for _ in streams]
                for k in range(2):
                    pe.wait_ge(*w.next(act_ready_pe))
                    for (c0, n), b in zip(streams, t):
                        mm = pe.matmul(b[:, 0:n], ones, Hc[:, k, c0:c0 + n], start=k == 0, stop=k == 1)
                        if k == 1:
                            mm.then_inc(*w.up(pe_tile_for["act"]))
                pe.wait_ge(*w.next(dve_ready_pe))
                for i in range(6 if both else 4):
                    b = tile("act")
                    for c in range(2):
                        mm = pe.matmul(b[:, c * 256:c * 256 + 256], FZ[:, c, i * P:i * P + P], const("dft_chan"),
                                       start=True, stop=True)
                    mm.then_inc(*w.up(pe_tile_for["act"]))
                pe.wait_ge(*w.next(act_ready_pe, 6 if both else 4))
                for s, (c0, n) in enumerate(streams):
                    nb = n // P
                    wt = part(panel_raw(a["dft_x" if s == 0 else "dft_c"], 2 * nb * n), 0, 2, nb, n)
                    for c in range(2):
                        b = tile("dve")
                        for i in range(nb):
                            for cs in range(2):
                                mm = pe.matmul(b[:, 0:n], FA[:, c0 // P + i, c, cs, :], wt[:, cs, i, :],
                                               start=i == 0 and cs == 0, stop=i == nb - 1 and cs == 1)
                        mm.then_inc(*w.up(pe_tile_for["dve"]))
                    panel_done()

                for hd in range(HEADS):
                    for d in range(2):
                        for c0, n in streams:
                            b = tile("act")
                            mm = pe.matmul(b[:, 0:n], const("head_rows")[0:4, hd * P:hd * P + P], GR[0:4, d, c0:c0 + n],
                                           start=True, stop=True)
                            mm.then_inc(*w.up(pe_tile_for["act"]))
                    for s in (4, 5, 0, 1, 2, 3):
                        b = tile("dve")
                        mm = pe.matmul(b[:, 0:TX], K[:, hd, s * P:s * P + P], Q[:, hd, 0:TX], start=True, stop=True)
                        mm.then_inc(*w.up(pe_tile_for["dve"]))
                    if both:
                        b = tile("dve")
                        for j in range(2):
                            mm = pe.matmul(b[:, j * TC:j * TC + TC], K[:, hd, TX + j * P:TX + j * P + P],
                                           Q[:, hd, TX:T], start=True, stop=True)
                        mm.then_inc(*w.up(pe_tile_for["dve"]))
                    pe.wait_ge(*w.next(dve_ready_pe))
                    for d in range(2):
                        for g in ((0, 1, 2), (3, 4, 5)) if both else ((0, 1, 2), (3,)):
                            b = tile("dve")
                            for i, tb in enumerate(g):
                                keys = [s for s in (4, 5, 0, 1, 2, 3) if pt_at(d, s, tb) is not None]
                                for n, s in enumerate(keys):
                                    at = pt_at(d, s, tb)
                                    mm = pe.matmul(b[:, i * 129:i * 129 + 129], PT[:, at:at + P], V[:, s, hd, :],
                                                   start=n == 0, stop=n == len(keys) - 1)
                            mm.then_inc(*w.up(pe_tile_for["dve"]))
                pe.wait_ge(*w.next(dve_ready_pe))
                for hd in range(HEADS):
                    for g in ((0, 1, 2, 3), (4, 5)) if both else ((0, 1, 2, 3),):
                        b = tile("dve")
                        for i, tb in enumerate(g):
                            mm = pe.transpose(b[:, i * P:i * P + P], HS[:, tb, hd, :], ident)
                        mm.then_inc(*w.up(pe_tile_for["dve"]))
                pe.wait_ge(*w.next(dve_ready_pe))
                for half in range(2):
                    wt = panel(a["w_out"][layer, :, half * 512:(half + 1) * 512], KC, 512)
                    for m in range(4):
                        project(wt, m, streams, h, KC, "dve")
                    panel_done()
                norm_sum(streams, KC, ones)
                norm_sum(streams, KC, ones)
                pe.wait_ge(*w.next(act_ready_pe, KC))
                for half in range(2):
                    for n in range(4):
                        c0 = half * 2048 + n * 512
                        wt = panel(a["w_mlp1"][layer, :, c0:c0 + 512], KC, 512)
                        for m in range(4):
                            project(wt, m, streams, h, KC, "act")
                        panel_done()
                    pe.wait_ge(*w.next(dve_ready_pe, 16))
                    for n in range(4):
                        wt = panel(a["w_mlp2"][layer, half * 2048:half * 2048 + 2048, n * 256:n * 256 + 256], 16, 256)
                        for m in range(2):
                            project(wt, m, streams, lambda k: HID[:, k, :], 16, "dve")
                        panel_done()
                    marks["hid_read", layer, half] = w.last
                norm_sum(streams, KC, ones)

            def panel_raw(src, width):
                n = len(panels)
                panels.append([src, 0, width, None])
                pe.wait_ge(slot_loaded[n % SLOTS], 16 * (n // SLOTS + 1))
                return ring[:, n % SLOTS]

            pe.wait_ge(s_first, 48)
            pe.wait_ge(*w.next(act_ready_pe))
            ada(0, 0, 4)
            for layer in range(LAYERS):
                layer_program(layer)

            memory_after.append(len(panels))
            norm_sum([(0, TC)], KC, ones)
            pe.wait_ge(*w.next(dve_ready_pe, KC))
            wt = panel(a["w_mem_kv_2"][0], KC, 512)
            for m in range(2):
                project(wt, m, [(0, TC)], lambda k: MEM[:, k, :], KC, "act")
            by_token(wt, range(2), 256, 256, lambda k: MEM[:, k, :], "act")
            panel_done()
            norm_sum([X_COLS], KC, ones)
            pe.wait_ge(*w.next(dve_ready_pe, KC))

            def h(k):
                return Hc[:, k, :]

            for i, (c0, n) in enumerate(PANELS2):
                wt = panel(a["w_in_2"][0, :, c0:c0 + n], KC, n)
                for m in range({1: 3, 2: 1}.get(i, 4)):
                    project(wt, m, [X_COLS], h, KC, "act")
                if i == 1:
                    by_token(wt, range(4), 384, 128, h, "act")
                if i == 2:
                    by_token(wt, range(4), 128, 152, h, "act")
                panel_done()
            for i, win in enumerate((KWIN, VWIN)):
                pe.wait_ge(*w.next(dve_ready_pe))
                wt = part(panel_raw(a["w_cmp1"][i], SLOT), 0, 32, P)
                b = tile("act")
                for j in range(32):
                    mm = pe.matmul(b[:, 0:NCMP], wt[:, j, :], win[:, :, j], start=j == 0, stop=j == 31)
                mm.then_inc(*w.up(pe_tile_for["act"]))
                panel_done()
            wt = part(panel_raw(a["w_small"], 512), 0, 4, P)
            pe.wait_ge(*w.next(act_ready_pe))
            b = tile("act")
            pe.matmul(b[:, 0:NCMP], wt[:, 0, :], HIDK, start=True, stop=True).then_inc(*w.up(pe_tile_for["act"]))
            b = tile("act")
            pe.matmul(b[0:NCMP, 0:P], HIDV, wt[:, 1, :], start=True, stop=True).then_inc(*w.up(pe_tile_for["act"]))
            for c in range(2):
                pe.wait_ge(*w.next(dve_ready_pe))
                b = tile("dve")
                pe.matmul(b[:, 0:TX], wt[:, 2 + c, :], VP[:, c, :], start=True, stop=True).then_inc(*w.up(pe_tile_for["dve"]))
            panel_done()
            for i in range(len(heads) + 1):
                if i < len(heads):
                    pe.wait_ge(*w.next(act_ready_pe))
                    n = heads[i][1]
                    b = tile("act")
                    pe.matmul(b[:, 0:n], ones64, tmp[:, (i % 2) * TX:(i % 2) * TX + n], start=True,
                                        stop=True).then_inc(*w.up(pe_tile_for["act"]))
                if i and heads[i - 1][3]:
                    pe.wait_ge(*w.next(dve_ready_pe))
                    z, n = heads[i - 1][0:2]
                    b = tile("dve")
                    pe.matmul(b[:, 0:n], rope_turn, z, start=True, stop=True).then_inc(*w.up(pe_tile_for["dve"]))

            def scores(u):
                kind, c, g, tb = UNITS[u]
                lo, hi = 64 * g, 64 * g + 64
                if kind == "mem":
                    q, keys = QM[lo:hi, c, tb * P:tb * P + P], [MK[lo:hi, c, :]]
                else:
                    n = (tb + 1) * P
                    q, keys = Q2[lo:hi, c, tb * P:tb * P + P], [KCMP[lo:hi, :], KS[lo:hi, 0:n], KW[lo:hi, 0:n]]
                for k in keys:
                    b = tile("dve", "act")
                    pe.matmul(b[:, 0:k.shape[1]], q, k, start=True, stop=True).then_inc(*w.up(pe_tile_for["dve"]))

            def turn(u):
                pe.wait_ge(*w.next(dve_ready_pe))
                blocks = prob_blocks(u)
                for i in range(0, len(blocks), 4):
                    b = tile("act")
                    for j, at in enumerate(blocks[i:i + 4]):
                        mm = pe.transpose(b[:, j * P:j * P + P], PROB[:, u % 2, at:at + P], ident)
                    mm.then_inc(*w.up(pe_tile_for["act"]))

            def values(u):
                pe.wait_ge(*w.next(act_ready_pe))
                kind, c, g, tb = UNITS[u]
                lo, hi = 64 * g, 64 * g + 64
                if kind == "mem":
                    v = [MV[:, i, (2 * c + g) * 64:(2 * c + g) * 64 + 64] for i in range(2)]
                else:
                    v = [VCMP[:, lo:hi]] + [VS[:, i, lo:hi] for i in range(tb + 1)]
                    v += [VW[:, i, lo:hi] for i in range(tb + 1)]
                b = tile("dve")
                for i, vi in enumerate(v):
                    mm = pe.matmul(b[lo:hi, 0:P], vi, PROBT[:, u % 2, i, :], start=i == 0, stop=i == len(v) - 1)
                mm.then_inc(*w.up(pe_tile_for["dve"]))

            pe.wait_ge(*w.next(dve_ready_pe))
            scores(0)
            for u in range(len(UNITS)):
                if u + 1 < len(UNITS):
                    scores(u + 1)
                if u:
                    values(u - 1)
                turn(u)
            values(len(UNITS) - 1)
            pe.wait_ge(*w.next(dve_ready_pe))
            for half in range(2):
                wt = panel(a["w_out_2"][0, :, half * 512:(half + 1) * 512], KC, 512)
                for m in range(4):
                    project(wt, m, [X_COLS], lambda k: Y[:, k, :], KC, "dve")
                panel_done()

        @block.vector
        def _(dve):
            w = Worker(dve_step)
            st = iter(tiles["dve"])

            def tile():
                return psum[:, next(st)]

            def recip_rs(c0, n):
                dve.wait_ge(*w.next(act_ready_dve))
                dve.reciprocal(rs[:, c0:c0 + n], rs[:, c0:c0 + n]).then_inc(*w.up())

            def apply_norm(streams, gslot, dst):
                for c0, n in streams:
                    recip_rs(c0, n)
                dve.wait_ge(*w.own())
                for k in range(KC):
                    for s, (c0, n) in enumerate(streams):
                        ins = dve.scalar_tensor_tensor(out=dst[:, k, c0:c0 + n], in0=X[:, k, c0:c0 + n],
                                                       scalar=gsc[:, gslot, k, s:s + 1], in1=rs[:, c0:c0 + n],
                                                       op0=ALU.mult, op1=ALU.mult)
                        ins.then_inc(*w.up(dve_ready_act if s == len(streams) - 1 else None))

            def ada(layer, first, last):
                for n in range(first, last):
                    dve.wait_ge(*w.next(pe_tile_for["dve"]))
                    b = tile()
                    for s in range(2):
                        ins = dve.tensor_tensor(mod[:, layer, 4 * n:4 * n + 4, s],
                                                b[:, 0:8].rearrange("p (j s) -> p j s", s=2)[:, :, s],
                                                col("b_ada", 4 * n, layer, 4), ALU.add)
                        if s == 0:
                            ins.then_inc(*w.up())
                    ins.then_inc(*w.up(dve_bank_free))

            def gains(layer, gslot, name, section, plus_one):
                dve.wait_ge(*w.own())
                for s in range(2):
                    m = mod[:, layer, section * 8:section * 8 + 8, s]
                    dve.scalar_tensor_tensor(out=gsc[:, gslot, :, s], in0=m, scalar=1.0 if plus_one else 0.0,
                                                   in1=col(name, 0, layer, 8), op0=ALU.add, op1=ALU.mult).then_inc(*w.up())
                dve.wait_ge(*w.own())

            def residual(streams, gslot):
                for c0, n in streams:
                    recip_rs(c0, n)
                dve.wait_ge(*w.own())
                for k in range(KC):
                    for s, (c0, n) in enumerate(streams):
                        dve.scalar_tensor_tensor(out=ACC[:, k, c0:c0 + n], in0=ACC[:, k, c0:c0 + n],
                                                       scalar=gsc[:, gslot, k, s:s + 1], in1=rs[:, c0:c0 + n],
                                                       op0=ALU.mult, op1=ALU.mult).then_inc(*w.up())
                    dve.wait_ge(*w.own())
                    n = sum(q[1] for q in streams)
                    dve.tensor_tensor(X[:, k, 0:n], X[:, k, 0:n], ACC[:, k, 0:n], ALU.add).then_inc(*w.up(dve_ready_act))

            def layer_program(layer):
                both = layer < LAYERS - 1
                streams = [X_COLS, C_COLS] if both else [X_COLS]
                all_streams = [X_COLS, C_COLS]
                tn = T if both else TX

                gains(layer, 0, "g_pre_mix", 1, True)
                apply_norm(all_streams, 0, Hc)
                dve.memset(R[:, 17688:17688 + 1656], 0.0).then_inc(*w.up())
                dve.wait_ge(*w.own())
                for m in range(2):
                    for s, (c0, n) in enumerate(streams):
                        u0 = PAD + (0 if s == 0 else TX + 2 * PAD)
                        dve.wait_ge(*w.next(act_ready_dve))
                        dve.wait_ge(*w.next(pe_tile_for["dve"]))
                        b = tile()
                        dve.tensor_tensor(UPAD[:, m, u0:u0 + n], b[:, 0:n], Hs_gate(s, n), ALU.mult).then_inc(*w.up(dve_bank_free))
                        dve.wait_ge(*w.own())
                        dve.wait_ge(*w.own())
                        dve.sem_inc(*w.up(dve_ready_act))
                for c0, n in all_streams:
                    dve.wait_ge(*w.next(pe_tile_for["dve"]))
                    b = tile()
                    dve.tensor_scalar(sq[0:16, c0:c0 + n], b[0:16, 0:n], col("b_gate", 0, layer)[0:16, :], None,
                                           ALU.add).then_inc(*w.up(dve_bank_free))
                dve.wait_ge(*w.own())
                dve.sem_inc(*w.up(dve_ready_sp))
                for name, dst, st_, j in (("q", Q, streams, 0), ("k", K, all_streams, 4)):
                    for m in range(4):
                        for c0, n in st_:
                            dve.wait_ge(*w.next(pe_tile_for["dve"]))
                            b = tile()
                            tap = [col("w_qk_conv", 8 * i + j + m, layer) for i in range(3)]
                            dve.tensor_scalar(dst[:, m, c0:c0 + n], b[:, 0:n], tap[1], None, ALU.mult).then_inc(*w.up())
                            dve.wait_ge(*w.own())
                            dve.scalar_tensor_tensor(out=dst[:, m, c0 + 1:c0 + n], in0=b[:, 0:n - 1], scalar=tap[0],
                                                           in1=dst[:, m, c0 + 1:c0 + n], op0=ALU.mult, op1=ALU.add).then_inc(*w.up())
                            dve.wait_ge(*w.own())
                            dve.scalar_tensor_tensor(out=dst[:, m, c0:c0 + n - 1], in0=b[:, 1:n], scalar=tap[2],
                                                          in1=dst[:, m, c0:c0 + n - 1], op0=ALU.mult, op1=ALU.add).then_inc(*w.up(dve_bank_free))
                dve.memset(V[:, :, :, 128:129], 1.0).then_inc(*w.up())
                ada(layer, 4, 12)
                if both:
                    ada(layer + 1, 0, 4)
                for m in range(2):
                    for s, (c0, n) in enumerate(streams):
                        u0 = 0 if s == 0 else TX + 2 * PAD
                        cv = CV[:, m, c0:c0 + n]
                        for i in range(CONV_K):
                            u = UPAD[:, m, u0 + i:u0 + i + n]
                            tap = col("w_dw", 2 * i + m, layer)
                            dve.wait_ge(*w.own())
                            if i == 0:
                                dve.tensor_scalar(cv, u, tap, col("b_dw", m, layer), ALU.mult, ALU.add).then_inc(*w.up())
                            else:
                                dve.scalar_tensor_tensor(out=cv, in0=u, scalar=tap, in1=cv, op0=ALU.mult,
                                                               op1=ALU.add).then_inc(*w.up())

                dve.wait_ge(*w.next(act_ready_dve))
                for d in range(2):
                    i_row, f_row = ROWS[0:4, 2 * d, :], ROWS[0:4, 2 * d + 1, :]
                    ln = (rs if d == 0 else sq)[0:4, :]
                    dve.scalar_tensor_tensor(out=f_row, in0=f_row, scalar=0.0, in1=ln, op0=ALU.min,
                                                   op1=ALU.subtract).then_inc(*w.up())
                    dve.wait_ge(*w.own())

                    def scan(dst, src, kind):
                        parts = [(TX, T), (0, TX)]
                        carry = 0.0
                        for lo, hi in parts:
                            o, i = dst[:, lo:hi], src[:, lo:hi]
                            if d == 1:
                                o, i = o[:, ::-1], i[:, ::-1]
                            dve.tensor_tensor_scan(o, i, i, carry, kind, ALU.bypass).then_inc(*w.up())
                            dve.wait_ge(*w.own())
                            carry = dst[:, hi - 1:hi] if d == 0 else dst[:, lo:lo + 1]

                    scan(f_row, f_row, ALU.add)
                    dve.tensor_tensor(i_row, i_row, f_row, ALU.subtract).then_inc(*w.up())
                    dve.wait_ge(*w.own())
                    scan(GR[0:4, d, :], i_row, ALU.max)
                    dve.tensor_tensor(f_row, f_row, GR[0:4, d, :], ALU.add).then_inc(*w.up(dve_ready_act if d == 1 else None))
                dve.wait_ge(*w.next(act_ready_dve))
                dve.wait_ge(*w.own())
                dve.sem_inc(*w.up(dve_ready_pe))
                dve.wait_ge(*w.next(pe_tile_for["dve"]))
                b = tile()
                dve.tensor_copy(acol[:, :], b[:, 0:96]).then_inc(*w.up(dve_bank_free))
                dve.wait_ge(*w.own())
                dve.sem_inc(*w.up(dve_ready_pe))
                for c0, n in streams:
                    dve.wait_ge(*w.next(pe_tile_for["dve"]))
                    b = tile()
                    for k in range(2):
                        cv = CV[:, k, c0:c0 + n]
                        ins = dve.scalar_tensor_tensor(out=cv, in0=b[:, 0:n], scalar=-1.0 / 256, in1=cv, op0=ALU.mult,
                                                       op1=ALU.add)
                        if k == 0:
                            ins.then_inc(*w.up())
                    ins.then_inc(*w.up(dve_bank_free))
                dve.wait_ge(*w.own())
                dve.sem_inc(*w.up(dve_ready_act))
                for c0, n in streams:
                    recip_rs(c0, n)
                dve.wait_ge(*w.own())
                for k in range(2):
                    dve.tensor_tensor(Hc[:, 6 + k, 0:tn], CV[:, k, 0:tn], rs[:, 0:tn], ALU.mult).then_inc(*w.up(dve_ready_act))
                dve.wait_ge(*w.own())
                dve.sem_inc(*w.up(dve_ready_pe))
                for c0, n in streams:
                    for c in range(2):
                        dve.wait_ge(*w.next(pe_tile_for["dve"]))
                        b = tile()
                        dve.tensor_copy(Hc[:, 4 + c, c0:c0 + n], b[:, 0:n]).then_inc(*w.up(dve_bank_free))

                en = acol[:, 48:96].rearrange("p (i d h) -> p i d h", i=6, d=2)
                av = acol[:, 0:48].rearrange("p (i d h) -> p i d h", i=6, d=2)
                for hd in range(HEADS):
                    dve.wait_ge(*w.next(act_ready_dve, 2 * len(streams)))
                    for s in (4, 5, 0, 1, 2, 3):
                        dve.wait_ge(*w.next(pe_tile_for["dve"]))
                        b = tile()
                        for d in range(2):
                            at = pt_at(d, s, 0 if d == 1 or s >= 4 else s)
                            lo, hi = (0, TX) if s >= 4 else ((s * P, TX) if d == 0 else (0, (s + 1) * P))
                            wv = PT[:, at:at + hi - lo]
                            weights(w, dve, s, d, hd, lo, hi, 0, wv, av)
                            ins = dve.scalar_tensor_tensor(out=wv, in0=b[:, lo:hi], scalar=HD ** -0.5, in1=wv,
                                                           op0=ALU.mult, op1=ALU.mult)
                            if d == 0:
                                ins.then_inc(*w.up())
                            else:
                                ins.then_inc(*w.up(dve_bank_free))
                    if both:
                        dve.wait_ge(*w.next(pe_tile_for["dve"]))
                        b = tile()
                        for j in range(2):
                            for d in range(2):
                                s = 4 + j
                                at = pt_at(d, s, 4 if d == 1 else s)
                                lo, hi = (j * P, TC) if d == 0 else (0, (j + 1) * P)
                                wv = PT[:, at:at + hi - lo]
                                weights(w, dve, s, d, hd, lo, hi, TX, wv, av)
                                ins = dve.scalar_tensor_tensor(out=wv, in0=b[:, j * TC + lo:j * TC + hi],
                                                               scalar=HD ** -0.5, in1=wv, op0=ALU.mult, op1=ALU.mult)
                                if (j, d) != (1, 1):
                                    ins.then_inc(*w.up())
                                else:
                                    ins.then_inc(*w.up(dve_bank_free))
                    dve.wait_ge(*w.own())
                    dve.sem_inc(*w.up(dve_ready_pe))
                    for d in range(2):
                        for g in ((0, 1, 2), (3, 4, 5)) if both else ((0, 1, 2), (3,)):
                            dve.wait_ge(*w.next(pe_tile_for["dve"]))
                            b = tile()
                            ng = len(g)
                            bv = b[:, 0:ng * 129].rearrange("p (i e) -> p i e", e=129)
                            den = small[:, 0:ng]
                            dve.tensor_tensor(den, bv[:, :, 128], en[:, g[0]:g[0] + ng, d, hd], ALU.max).then_inc(*w.up())
                            dve.wait_ge(*w.own())
                            dve.scalar_tensor_tensor(out=den, in0=bv[:, :, 128], scalar=-1.0, in1=den,
                                                           op0=ALU.mult, op1=ALU.max).then_inc(*w.up())
                            dve.wait_ge(*w.own())
                            dve.reciprocal(den, den).then_inc(*w.up())
                            dve.wait_ge(*w.own())
                            for i, tb in enumerate(g):
                                if d == 0:
                                    ins = dve.tensor_scalar(HS[:, tb, hd, :], bv[:, i, 0:128], den[:, i:i + 1], None,
                                                            ALU.mult)
                                else:
                                    ins = dve.scalar_tensor_tensor(out=HS[:, tb, hd, :], in0=bv[:, i, 0:128],
                                                                   scalar=den[:, i:i + 1], in1=HS[:, tb, hd, :],
                                                                   op0=ALU.mult, op1=ALU.add)
                                if i < ng - 1:
                                    ins.then_inc(*w.up())
                            ins.then_inc(*w.up(dve_bank_free))
                            dve.wait_ge(*w.own())
                    dve.sem_inc(*w.up(dve_ready_act))
                nb = 6 if both else 4
                for tb in range(nb):
                    for hd in range(HEADS):
                        dve.bn_stats(small[:, 0:6], HS[:, tb, hd, :]).then_inc(*w.up())
                        dve.wait_ge(*w.own())
                        dve.bn_aggr(tmp[:, 2 * (tb * 4 + hd):2 * (tb * 4 + hd) + 2], small[:, 0:6]).then_inc(*w.up())
                        dve.wait_ge(*w.own())
                dve.sem_inc(*w.up(dve_ready_act))
                dve.wait_ge(*w.next(act_ready_dve))
                dve.reciprocal(tmp[:, 64:64 + nb * 4], tmp[:, 64:64 + nb * 4]).then_inc(*w.up())
                dve.wait_ge(*w.own())
                for tb in range(nb):
                    for hd in range(HEADS):
                        i = tb * 4 + hd
                        dve.tensor_scalar(HS[:, tb, hd, :], HS[:, tb, hd, :], tmp[:, 2 * i:2 * i + 1],
                                                tmp[:, 64 + i:65 + i], ALU.subtract, ALU.mult).then_inc(*w.up())
                dve.wait_ge(*w.own())
                dve.sem_inc(*w.up(dve_ready_pe))
                for hd in range(HEADS):
                    for c0, n in streams:
                        dve.wait_ge(*w.next(pe_tile_for["dve"]))
                        b = tile()
                        dve.scalar_tensor_tensor(out=Hc[:, hd, c0:c0 + n], in0=b[:, 0:n],
                                                      scalar=col("g_mlstm_norm", hd, layer), in1=O[:, hd, c0:c0 + n],
                                                      op0=ALU.mult, op1=ALU.mult).then_inc(*w.up(dve_bank_free))
                dve.wait_ge(*w.own())
                dve.wait_ge(*w.next(act_ready_dve))
                dve.wait_ge(*w.own())
                dve.sem_inc(*w.up(dve_ready_pe))
                gains(layer, 1, "g_post_mix", 2, False)
                gains(layer, 2, "g_pre_mlp", 4, True)
                gains(layer, 3, "g_post_mlp", 5, False)
                for k in range(KC):
                    for c0, n in streams:
                        dve.wait_ge(*w.next(pe_tile_for["dve"]))
                        b = tile()
                        dve.tensor_copy(ACC[:, k, c0:c0 + n], b[:, 0:n]).then_inc(*w.up(dve_bank_free))
                dve.wait_ge(*w.own())
                dve.sem_inc(*w.up(dve_ready_act))
                residual(streams, 1)
                apply_norm(streams, 2, Hc)
                for half in range(2):
                    for k in range(16):
                        dve.wait_ge(*w.next(act_ready_dve))
                        dve.tensor_tensor(HID[:, k, 0:tn], HID[:, k, 0:tn], HID[:, k, 0:tn], ALU.mult).then_inc(*w.up(dve_ready_pe))
                    for k in range(KC):
                        for c0, n in streams:
                            dve.wait_ge(*w.next(pe_tile_for["dve"]))
                            b = tile()
                            acc = ACC[:, k, c0:c0 + n]
                            if half == 0:
                                dve.tensor_copy(acc, b[:, 0:n]).then_inc(*w.up(dve_bank_free))
                            else:
                                dve.wait_ge(*w.own())
                                dve.tensor_tensor(acc, b[:, 0:n], acc, ALU.add).then_inc(*w.up(dve_bank_free))
                dve.wait_ge(*w.own())
                dve.sem_inc(*w.up(dve_ready_act))
                residual(streams, 3)

            dve.wait_ge(s_first, 48)
            dve.memset(small[:, :], 0.0).then_inc(*w.up())
            dve.wait_ge(*w.own())
            dve.wait_ge(s_x, 32)
            dve.wait_ge(s_pos, 16)
            for k in range(KC):
                dve.tensor_tensor(X[:, k, 0:TX], X[:, k, 0:TX], Hc[:, k, 0:TX], ALU.add).then_inc(*w.up())
            dve.wait_ge(*w.own())
            dve.sem_inc(*w.up(dve_ready_act))
            ada(0, 0, 4)
            for layer in range(LAYERS):
                layer_program(layer)
            dve.wait_ge(*w.own())
            dve.sem_inc(*w.up(dve_ready_sp))
            recip_rs(0, TC)
            dve.wait_ge(*w.own())
            for k in range(KC):
                dve.scalar_tensor_tensor(out=MEM[:, k, :], in0=MEM[:, k, :], scalar=col("g_mem_2", k),
                                               in1=rs[:, 0:TC], op0=ALU.mult, op1=ALU.mult).then_inc(*w.up(dve_ready_pe))
            dve.wait_ge(*w.own())
            dve.sem_inc(*w.up(dve_ready_act))
            dve.wait_ge(s_tok, 16)
            kk = POOLT[:, 0, :]
            dve.tensor_scalar(SIN, COS.bitcast(I32), const("rope_freq"), None, ALU.mult).then_inc(*w.up())
            dve.wait_ge(*w.own())
            dve.tensor_scalar(kk, SIN, 1.0 / TWO_PI, ROUND, ALU.mult, ALU.add).then_inc(*w.up())
            dve.wait_ge(*w.own())
            dve.tensor_scalar(kk, kk, ROUND, None, ALU.subtract).then_inc(*w.up())
            for c in TWO_PI_PARTS:
                dve.wait_ge(*w.own())
                dve.scalar_tensor_tensor(out=SIN, in0=kk, scalar=-c, in1=SIN, op0=ALU.mult, op1=ALU.add).then_inc(*w.up())
            dve.wait_ge(*w.own())
            dve.tensor_scalar(SIN, SIN, PI_BELOW, -PI_BELOW, ALU.min, ALU.max).then_inc(*w.up(dve_ready_act))
            dve.wait_ge(*w.next(act_ready_dve))
            dve.tensor_tensor(COS, COS, COS, ALU.mult).then_inc(*w.up())
            dve.wait_ge(*w.own())
            dve.tensor_scalar(COS, COS, -2.0, 1.0, ALU.mult, ALU.add).then_inc(*w.up())
            dve.memset(VCMP, 0.0).then_inc(*w.up())
            dve.memset(PROB[:, :, 0:P], 0.0).then_inc(*w.up())
            recip_rs(*X_COLS)
            dve.wait_ge(*w.own())
            for k in range(KC):
                dve.scalar_tensor_tensor(out=Hc[:, k, 0:TX], in0=X[:, k, 0:TX], scalar=col("g_norm_2", k),
                                               in1=rs[:, 0:TX], op0=ALU.mult, op1=ALU.mult).then_inc(*w.up(dve_ready_pe))
            dve.wait_ge(*w.next(act_ready_dve))
            for raw, win, pos in ((KRAW, KWIN, "cmp_pos_k_2"), (VRAW, VWIN, "cmp_pos_v_2")):
                for part_ in range(2):
                    src = raw[:, 16 * part_:16 * part_ + 16 * NCMP].rearrange("p (n j) -> p n j", j=16)
                    dve.tensor_tensor(win[:, :, 16 * part_:16 * part_ + 16], src,
                                            col(pos, 16 * part_, n=16).unsqueeze(1).to_broadcast([P, NCMP, 16]),
                                            ALU.add).then_inc(*w.up())
                dve.wait_ge(*w.own())
                dve.sem_inc(*w.up(dve_ready_pe))
            dve.wait_ge(*w.next(act_ready_dve))
            for c in range(2):
                cur, lo = VP[:, c, :], 0
                where = {0: cur}
                for i, sh in enumerate((1, 2) if c == 0 else (1, 2, 4, 8)):
                    if sh == (2, 8)[c]:
                        where[0], lo = cur, 64
                    nxt = POOLT[:, i % 2, :]
                    dve.wait_ge(*w.own())
                    dve.tensor_tensor(nxt[lo:, sh:TX], cur[lo:, sh:TX], cur[lo:, 0:TX - sh], ALU.add).then_inc(*w.up())
                    dve.tensor_copy(nxt[lo:, 0:sh], cur[lo:, 0:sh]).then_inc(*w.up())
                    cur = nxt
                for lo, res in ((0, where[0]), (64, cur)):
                    r = res[lo:lo + 64, :]
                    dve.wait_ge(*w.own())
                    dve.tensor_tensor(r[:, 0:16], r[:, 0:16], const("pool_first")[lo:lo + 64, 16 * c:16 * c + 16],
                                            ALU.mult).then_inc(*w.up())
                    dve.wait_ge(*w.own())
                    vp = VP[lo:lo + 64, c, :]
                    dve.scalar_tensor_tensor(out=vp, in0=r, scalar=const("pool_inv")[lo:lo + 64, c:c + 1],
                                                   in1=vp, op0=ALU.mult, op1=ALU.subtract).then_inc(*w.up())
                dve.wait_ge(*w.own())
                dve.sem_inc(*w.up(dve_ready_pe))
            for c in range(2):
                dve.wait_ge(*w.next(pe_tile_for["dve"]))
                b = tile()
                dve.scalar_tensor_tensor(out=Y[:, 4 + c, :], in0=b[:, 0:TX], scalar=col("pool_scale_2", c),
                                              in1=ZP[:, c, :], op0=ALU.mult, op1=ALU.mult).then_inc(*w.up(dve_bank_free))
            for i in range(len(heads) + 1):
                if i < len(heads):
                    z, n, gain, _ = heads[i]
                    r = (rs, sq)[i % 2][:, 0:n]
                    dve.wait_ge(*w.next(act_ready_dve))
                    dve.reciprocal(r, r).then_inc(*w.up())
                    dve.wait_ge(*w.own())
                    dve.scalar_tensor_tensor(out=z, in0=z, scalar=col(gain), in1=r, op0=ALU.mult, op1=ALU.mult).then_inc(*w.up())
                    dve.wait_ge(*w.own())
                    dve.sem_inc(*w.up(dve_ready_act))
                    if heads[i][3]:
                        dve.wait_ge(*w.own())
                        dve.sem_inc(*w.up(dve_ready_pe))
                if i and heads[i - 1][3]:
                    z, n, _, sl = heads[i - 1]
                    dve.wait_ge(*w.next(pe_tile_for["dve"]))
                    b = tile()
                    t0, t1 = POOLT[:, 0, 0:n], POOLT[:, 1, 0:n]
                    dve.wait_ge(*w.own())
                    dve.tensor_tensor(t0, z, COS[:, sl], ALU.mult).then_inc(*w.up())
                    dve.tensor_tensor(t1, b[:, 0:n], SIN[:, sl], ALU.mult).then_inc(*w.up(dve_bank_free))
                    dve.wait_ge(*w.own())
                    dve.tensor_tensor(z, t0, t1, ALU.add).then_inc(*w.up())
            dve.wait_ge(*w.own())
            dve.sem_inc(*w.up(dve_ready_pe))

            def parts_of(u):
                kind, c, g, tb = UNITS[u]
                if kind == "mem":
                    return [(TC, 0, None)]
                n = (tb + 1) * P
                return [(NCMP, 0, const("cmp_hide")[:, tb * NCMP:(tb + 1) * NCMP]), (n, tb * P, const("hide_s_gt_t")),
                        (n, tb * P, const("hide_s_gt_t"))]

            def highest(u):
                o = 16 * (u % 2)
                ps = parts_of(u)
                for j, (n, h0, hide) in enumerate(ps):
                    dve.wait_ge(*w.next(pe_tile_for["dve"]))
                    b = tile()
                    if hide is not None:
                        m = hide.shape[1]
                        dve.tensor_tensor(b[:, h0:h0 + m], b[:, h0:h0 + m], hide, ALU.add).then_inc(*w.up())
                        dve.wait_ge(*w.own())
                    dve.tensor_reduce(small[:, o + j:o + j + 1], b[:, 0:n], AXX, ALU.max).then_inc(*w.up())
                dve.wait_ge(*w.own())
                dve.tensor_scalar(small[:, o + 4:o + 4 + len(ps)], small[:, o:o + len(ps)], -BIG / 10, -SCALE,
                                        ALU.max, ALU.mult).then_inc(*w.up(dve_ready_act))

            def normalise(u):
                kind, c, g, tb = UNITS[u]
                o = 16 * (u % 2) + 8
                ps = parts_of(u)
                dve.wait_ge(*w.next(act_ready_dve))
                den = small[:, o:o + len(ps)]
                dve.tensor_scalar(den, den, TINY, None, ALU.max).then_inc(*w.up())
                dve.wait_ge(*w.own())
                dve.reciprocal(den, den).then_inc(*w.up())
                dve.wait_ge(*w.own())
                if kind == "nsa":
                    hd = 4 * g + c
                    dve.tensor_tensor(den, den, GATE[:, tb, 3 * hd:3 * hd + 3], ALU.mult).then_inc(*w.up())
                    dve.wait_ge(*w.own())
                for j, (n, _, _) in enumerate(ps):
                    at = prob_at(u, j, n)
                    pr = PROB[:, u % 2, at:at + n]
                    dve.tensor_scalar(pr, pr, den[:, j:j + 1], None, ALU.mult).then_inc(*w.up())
                dve.wait_ge(*w.own())
                dve.sem_inc(*w.up(dve_ready_pe))

            def gated(u):
                kind, c, g, tb = UNITS[u]
                lo, hi = 64 * g, 64 * g + 64
                z, k = (ZN, c) if kind == "nsa" else (ZM, 6 + c)
                dve.wait_ge(*w.next(pe_tile_for["dve"]))
                b = tile()
                dve.tensor_tensor(Y[lo:hi, k, tb * P:tb * P + P], b[lo:hi, 0:P], z[lo:hi, c, tb * P:tb * P + P],
                                       ALU.mult).then_inc(*w.up(dve_bank_free))

            highest(0)
            for u in range(len(UNITS)):
                normalise(u)
                if u + 1 < len(UNITS):
                    highest(u + 1)
                if u:
                    gated(u - 1)
            gated(len(UNITS) - 1)
            dve.wait_ge(*w.own())
            dve.sem_inc(*w.up(dve_ready_pe))
            for k in range(KC):
                dve.wait_ge(*w.next(pe_tile_for["dve"]))
                b = tile()
                dve.tensor_tensor(X[:, k, 0:TX], b[:, 0:TX], X[:, k, 0:TX], ALU.add).then_inc(*w.up(dve_bank_free))
            dve.wait_ge(*w.own())
            dve.sem_inc(*w.up(dve_ready_sp))

        @block.scalar
        def _(act):
            w = Worker(act_step)
            st = iter(tiles["act"])

            def tile():
                return psum[:, next(st)]

            def squares(src, streams, chunks=KC, each=None):
                n = sum(q[1] for q in streams)
                for k in range(chunks):
                    if each:
                        act.wait_ge(*w.next(dve_ready_act))
                    act.activation(Hc[:, k, 0:n], src[:, k, 0:n], ACT.Square).then_inc(*w.up(act_ready_pe))

            def roots(streams, count):
                for c0, n in streams:
                    act.wait_ge(*w.next(pe_tile_for["act"]))
                    b = tile()
                    act.activation(rs[:, c0:c0 + n], b[:, 0:n], ACT.Sqrt, scale=1.0 / count, bias=eps).then_inc(*w.up(act_bank_free))
                    act.wait_ge(*w.own())
                    act.sem_inc(*w.up(act_ready_dve))

            def shifts(streams, layer, section):
                for k in range(KC):
                    act.wait_ge(*w.next(dve_ready_act))
                    for s, (c0, n) in enumerate(streams):
                        m = mod[:, layer, section * 8 + k, s:s + 1]
                        act.activation(Hc[:, k, c0:c0 + n], Hc[:, k, c0:c0 + n], ACT.Identity, bias=m).then_inc(*w.up(act_ready_pe if s == len(streams) - 1 else None))

            def layer_program(layer):
                both = layer < LAYERS - 1
                streams = [X_COLS, C_COLS] if both else [X_COLS]
                all_streams = [X_COLS, C_COLS]
                tn = T if both else TX
                squares(X, all_streams)
                roots(all_streams, D)
                shifts(all_streams, layer, 0)
                for m in range(2):
                    for s, (c0, n) in enumerate(streams):
                        if m:
                            act.wait_ge(*w.next(dve_ready_act))
                        act.wait_ge(*w.next(pe_tile_for["act"]))
                        b = tile()
                        act.activation(Hs_gate(s, n), b[:, 0:n], ACT.Sigmoid).then_inc(*w.up(act_bank_free))
                        act.wait_ge(*w.own())
                        act.sem_inc(*w.up(act_ready_dve))
                for _ in range(len(streams)):
                    act.wait_ge(*w.next(dve_ready_act))
                for m in range(2):
                    for c0, n in streams:
                        act.wait_ge(*w.next(pe_tile_for["act"]))
                        b = tile()
                        act.copy(FZ[:, m, c0:c0 + n], b[:, 0:n]).then_inc(*w.up(act_bank_free))
                for i in range(6):
                    act.wait_ge(*w.next(pe_tile_for["act"]))
                    b = tile()
                    act.copy(V[:, i, :, 0:128], b[:, 0:512].rearrange("p (h e) -> p h e", h=4)).then_inc(*w.up(act_bank_free))
                for m in range(4):
                    for c0, n in streams:
                        act.wait_ge(*w.next(pe_tile_for["act"]))
                        b = tile()
                        act.activation(O[:, m, c0:c0 + n], b[:, 0:n], ACT.Sigmoid).then_inc(*w.up(act_bank_free))
                act.wait_ge(*w.own())
                act.wait_ge(s_rows, 64 * (layer + 1))
                for d in range(2):
                    t = (rs if d == 0 else sq)[0:4, :]
                    act.activation(t, ROWS[0:4, 2 * d + 1, :], ACT.Abs).then_inc(*w.up())
                    act.wait_ge(*w.own())
                    act.activation(t, t, ACT.Exp, scale=-1.0).then_inc(*w.up())
                    act.wait_ge(*w.own())
                    act.activation(t, t, ACT.Ln, bias=1.0).then_inc(*w.up(act_ready_dve if d == 1 else None))
                    act.wait_ge(*w.own())
                act.wait_ge(*w.next(dve_ready_act))
                act.activation(ROWS[0:4, 1:4:2, :], ROWS[0:4, 1:4:2, :], ACT.Exp, scale=-1.0).then_inc(*w.up(act_ready_dve))
                act.wait_ge(*w.next(dve_ready_act))
                for k in range(2):
                    act.activation(Hc[:, k, 0:tn], CV[:, k, 0:tn], ACT.Square).then_inc(*w.up(act_ready_pe))
                roots(streams, 256)
                for k in range(2):
                    act.wait_ge(*w.next(dve_ready_act))
                    act.activation(Hc[:, 6 + k, 0:tn], Hc[:, 6 + k, 0:tn], ACT.Silu,
                                         scale=col("g_conv_ln", k, layer), bias=col("b_conv_ln", k, layer)).then_inc(*w.up())
                for i in range(6 if both else 4):
                    act.wait_ge(*w.next(pe_tile_for["act"]))
                    b = tile()
                    act.copy(FA[:, i], b[:, 0:512].rearrange("p (c s e) -> p c s e", c=2, s=2)).then_inc(*w.up(bank_free["act"]))
                    act.wait_ge(*w.own())
                    act.sem_inc(*w.up(act_ready_pe))
                av = acol[:, 0:48].rearrange("p (i d h) -> p i d h", i=6, d=2)
                for hd in range(HEADS):
                    if hd:
                        act.wait_ge(*w.next(dve_ready_act))
                    for d in range(2):
                        for c0, n in streams:
                            act.wait_ge(*w.next(pe_tile_for["act"]))
                            b = tile()
                            act.copy(sq_gb(d)[:, c0:c0 + n], b[:, 0:n]).then_inc(*w.up(act_bank_free))
                            act.wait_ge(*w.own())
                            act.sem_inc(*w.up(act_ready_dve))
                    for s in (4, 5, 0, 1, 2, 3):
                        for d in range(2):
                            at = pt_at(d, s, 0 if d == 1 or s >= 4 else s)
                            lo, hi = (0, TX) if s >= 4 else ((s * P, TX) if d == 0 else (0, (s + 1) * P))
                            wv = PT[:, at:at + hi - lo]
                            if s >= 4:
                                act.activation(wv, sq_gb(d)[:, 0:TX], ACT.Exp, scale=-1.0,
                                                     bias=av[:, s, d, hd:hd + 1]).then_inc(*w.up(act_ready_dve))
                            else:
                                act.wait_ge(*w.next(dve_ready_act))
                                act.activation(wv, wv, ACT.Exp, scale=-1.0).then_inc(*w.up(act_ready_dve))
                    if both:
                        for j in range(2):
                            for d in range(2):
                                s = 4 + j
                                at = pt_at(d, s, 4 if d == 1 else s)
                                lo, hi = (j * P, TC) if d == 0 else (0, (j + 1) * P)
                                wv = PT[:, at:at + hi - lo]
                                act.wait_ge(*w.next(dve_ready_act))
                                act.activation(wv, wv, ACT.Exp, scale=-1.0).then_inc(*w.up(act_ready_dve))
                act.wait_ge(*w.next(dve_ready_act))
                act.wait_ge(*w.next(dve_ready_act))
                nb = 6 if both else 4
                act.activation(tmp[:, 64:64 + nb * 4], tmp[:, 0:nb * 8].rearrange("p (i t) -> p i t", t=2)[:, :, 1],
                                     ACT.Sqrt, bias=eps).then_inc(*w.up(act_ready_dve))
                act.wait_ge(*w.own())
                act.sem_inc(*w.up(act_ready_dve))
                act.wait_ge(*w.next(dve_ready_act))
                squares(ACC, streams)
                roots(streams, D)
                squares(X, streams, each=True)
                roots(streams, D)
                shifts(streams, layer, 3)
                for half in range(2):
                    if half:
                        act.wait_ge(*marks["hid_read", layer, 0])
                    for k in range(16):
                        for c0, n in streams:
                            act.wait_ge(*w.next(pe_tile_for["act"]))
                            b = tile()
                            act.activation(HID[:, k, c0:c0 + n], b[:, 0:n], ACT.Relu).then_inc(*w.up(act_bank_free))
                        act.wait_ge(*w.own())
                        act.sem_inc(*w.up(act_ready_dve))
                act.wait_ge(*w.next(dve_ready_act))
                squares(ACC, streams)
                roots(streams, D)
                for k in range(KC):
                    act.wait_ge(*w.next(dve_ready_act))

            act.wait_ge(s_first, 48)
            act.activation(cvec[:, :, :], cvec[:, :, :], ACT.Silu).then_inc(*w.up(act_ready_pe))
            act.wait_ge(*w.next(dve_ready_act))
            for layer in range(LAYERS):
                layer_program(layer)
            act.wait_ge(s_mem, 16)
            squares(MEM, [(0, TC)])
            roots([(0, TC)], D)
            for m in range(2):
                act.wait_ge(*w.next(pe_tile_for["act"]))
                b = tile()
                act.copy(MK[:, m, :], b[:, 0:TC]).then_inc(*w.up(act_bank_free))
            for m in range(2):
                act.wait_ge(*w.next(pe_tile_for["act"]))
                b = tile()
                act.copy(MV[:, m, :], b[:, 0:TC]).then_inc(*w.up(act_bank_free))
            act.wait_ge(*w.next(dve_ready_act))
            act.wait_ge(*w.next(dve_ready_act))
            act.activation(COS, SIN, ACT.Sin, scale=0.5).then_inc(*w.up())
            act.activation(SIN, SIN, ACT.Sin).then_inc(*w.up(act_ready_dve))
            squares(X, [X_COLS])
            roots([X_COLS], D)

            def into(dst, func=ACT.Copy, n=TX):
                act.wait_ge(*w.next(pe_tile_for["act"]))
                b = tile()
                act.activation(dst, b[:, 0:n], func).then_inc(*w.up(act_bank_free))

            for c in range(4):
                into(Q2[:, c, :])
            for dst in (KRAW, VRAW, KS):
                into(dst)
            act.wait_ge(*w.own())
            act.sem_inc(*w.up(act_ready_dve))
            for i in range(4):
                into(VS[:, i, :], n=P)
            into(KW)
            for i in range(4):
                act.wait_ge(*w.next(pe_tile_for["act"]))
                b = tile()
                act.copy(VW[:, i, :], b[:, 0:P]).then_inc(*w.up())
                act.activation(GATE[:, i, :], b[:, P:P + 24], ACT.Sigmoid).then_inc(*w.up(act_bank_free))
            for c in range(4):
                into(ZN[:, c, :], ACT.Silu)
            for c in range(2):
                into(VP[:, c, :])
            act.wait_ge(*w.own())
            act.sem_inc(*w.up(act_ready_dve))
            for c in range(2):
                into(ZP[:, c, :], ACT.Silu)
            for c in range(2):
                into(QM[:, c, :])
            for c in range(2):
                into(ZM[:, c, :], ACT.Silu)
            for dst in (HIDK, HIDV):
                into(dst, ACT.Gelu_apprx_tanh, NCMP)
            act.wait_ge(*w.own())
            act.sem_inc(*w.up(act_ready_pe))
            into(KCMP, n=NCMP)
            act.wait_ge(*w.next(pe_tile_for["act"]))
            b = tile()
            act.copy(VCMP[0:NCMP, :], b[0:NCMP, 0:P]).then_inc(*w.up(act_bank_free))
            act.wait_ge(*w.own())

            def head_square(i):
                z, n = heads[i][0:2]
                act.activation(tmp[:, (i % 2) * TX:(i % 2) * TX + n], z, ACT.Square).then_inc(*w.up(act_ready_pe))

            head_square(0)
            for i in range(len(heads)):
                if i + 1 < len(heads):
                    head_square(i + 1)
                if i >= 2:
                    act.wait_ge(*w.next(dve_ready_act))
                n = heads[i][1]
                act.wait_ge(*w.next(pe_tile_for["act"]))
                b = tile()
                act.activation((rs, sq)[i % 2][:, 0:n], b[:, 0:n], ACT.Sqrt, bias=eps).then_inc(*w.up(act_bank_free))
                act.wait_ge(*w.own())
                act.sem_inc(*w.up(act_ready_dve))
            act.wait_ge(*w.next(dve_ready_act, 2))
            banks = iter(shared)

            def exps(u):
                o = 16 * (u % 2)
                kind, c, g, tb = UNITS[u]
                act.wait_ge(*w.next(dve_ready_act))
                for j, n in enumerate([TC] if kind == "mem" else [NCMP, (tb + 1) * P, (tb + 1) * P]):
                    at = prob_at(u, j, n)
                    act.activation(PROB[:, u % 2, at:at + n], psum[:, next(banks), 0:n], ACT.Exp, scale=SCALE,
                                        bias=small[:, o + 4 + j:o + 5 + j], accum_out=small[:, o + 8 + j:o + 9 + j]).then_inc(*w.up(act_bank_free))
                act.wait_ge(*w.own())
                act.sem_inc(*w.up(act_ready_dve))

            def turned(u):
                nb = len(prob_blocks(u))
                for i in range(0, nb, 4):
                    m = min(4, nb - i)
                    act.wait_ge(*w.next(pe_tile_for["act"]))
                    b = tile()
                    act.copy(PROBT[:, u % 2, i:i + m, :], b[:, 0:m * P].rearrange("p (i t) -> p i t", t=P)).then_inc(*w.up(act_bank_free))
                act.wait_ge(*w.own())
                act.sem_inc(*w.up(act_ready_pe))

            exps(0)
            for u in range(len(UNITS)):
                if u + 1 < len(UNITS):
                    exps(u + 1)
                turned(u)

        @block.sync
        def _(sp):
            w = Worker(None)
            sp.dma_start(cvec[:, :, :], a["cvec"]).then_inc(s_first, 16)
            sp.dma_start(cols[:, :], a["cols"]).then_inc(s_first, 16)
            sp.dma_start(con[:, :], a["con"]).then_inc(s_first, 16)
            sp.dma_start(X[:, :, 0:TX], a["x"].rearrange("(k p) t -> p k t", p=P)).then_inc(s_x, 16)
            sp.dma_start(X[:, :, TX:T], a["ctx"].rearrange("(k p) t -> p k t", p=P)).then_inc(s_x, 16)
            sp.dma_start(Hc[:, :, 0:TX], a["grid"].rearrange("(k p) t -> p k t", p=P)).then_inc(s_pos, 16)

            def load(n):
                src, kc, width, _ = panels[n]
                if n >= SLOTS:
                    sp.wait_ge(*panels[n - SLOTS][3])
                if kc:
                    dst = part(ring[:, n % SLOTS], 0, kc, width)
                    src = src.rearrange("(k p) n -> p k n", p=P)
                else:
                    dst = ring[:, n % SLOTS, 0:width]
                sp.dma_start(dst, src).then_inc(slot_loaded[n % SLOTS], 16)

            n = 0
            for layer in range(LAYERS):
                stop = rows_after[layer]
                while n < stop:
                    load(n)
                    n += 1
                sp.wait_ge(*w.next(dve_ready_sp))
                for j in range(4):
                    sp.dma_start(ROWS[0:4, j, :], sq[4 * j:4 * j + 4, :]).then_inc(s_rows, 16)
            while n < memory_after[0]:
                load(n)
                n += 1
            sp.wait_ge(*w.next(dve_ready_sp))
            sp.dma_start(MEM, a["mem"].rearrange("(k p) t -> p k t", p=P)).then_inc(s_mem, 16)
            sp.dma_start(COS.bitcast(I32), a["positions"][0, :].partition_broadcast(P)).then_inc(s_tok, 16)
            while n < len(panels):
                load(n)
                n += 1
            sp.wait_ge(*w.next(dve_ready_sp))
            sp.dma_start(a["out"].rearrange("(k p) t -> p k t", p=P), X[:, :, 0:TX]).then_inc(s_out, 16)
            sp.wait_ge(s_out, 16)


def constants():
    i, j = np.arange(P)[:, None], np.arange(P)[None, :]
    c = np.zeros((P, NCONST), np.float32)

    def put(name, v):
        at, n = CONST[name]
        v = np.asarray(v)
        c[:v.shape[0], at:at + v.shape[1]] = v

    put("ident", np.eye(P))
    put("ones", np.ones((P, P)))
    put("ones64", (i // 64 == j // 64) / 64.0)
    turn = np.zeros((P, P))
    for g in (0, 64):
        for k in range(8):
            turn[g + 8 + k, g + k] = -1.0
            turn[g + k, g + 8 + k] = 1.0
    put("rope_turn", turn)
    ang = 2 * np.pi * (np.outer(np.arange(64), np.arange(64)) % 64) / 64
    chan = np.zeros((P, 256))
    for g in (0, 64):
        chan[g:g + 64, g:g + 64] = np.cos(ang) / 8
        chan[g:g + 64, P + g:P + g + 64] = np.sin(ang) / 8
    put("dft_chan", chan)
    put("hide_t_lt_s", np.where(j < i, BIG, 0.0))
    put("hide_t_gt_s", np.where(j > i, BIG, 0.0))
    put("hide_s_gt_t", np.where(j > i, -BIG, 0.0))
    hide = np.zeros((P, 4 * NCMP))
    for tb in range(4):
        hide[:, tb * NCMP:(tb + 1) * NCMP] = np.where(np.arange(NCMP)[None, :] * 16 + 31 > tb * P + i, -BIG, 0.0)
    put("cmp_hide", hide)
    put("head_rows", np.repeat(np.eye(4), P, axis=1))
    freq = np.zeros((P, 1), np.float32)
    inv = np.float32(500000.0) ** (-np.arange(8, dtype=np.float32) / np.float32(8))
    for g in (0, 8, 64, 72):
        freq[g:g + 8, 0] = inv
    put("rope_freq", freq)
    put("eps", np.full((P, 1), EPS))
    win = np.array([[2, 8], [4, 16]], np.float64)[np.arange(P) // 64]
    put("pool_inv", 1 / win)
    t = np.arange(16)
    put("pool_first", (win[:, :, None] / np.minimum(t + 1, win[:, :, None])).reshape(P, 32))
    return c


def dft(n):
    ang = 2 * np.pi * (np.outer(np.arange(n), np.arange(n)) % n) / n
    m = np.stack([np.cos(ang), -np.sin(ang)]) / np.sqrt(n)
    return m.reshape(2, n // P, P, n).transpose(2, 0, 1, 3).reshape(P, -1).astype(np.float32)


def grid():
    rows = TX // 64
    quarter = D // 4
    freq = np.exp(np.float32(-np.log(10000.0)) * np.arange(quarter, dtype=np.float32) / np.float32(quarter))
    freq = freq.astype(np.float32)
    r = np.repeat(np.arange(rows, dtype=np.float32), 64)[:, None] * freq
    c = np.tile(np.arange(64, dtype=np.float32), rows)[:, None] * freq
    return np.ascontiguousarray(np.concatenate([np.sin(r), np.cos(r), np.sin(c), np.cos(c)], -1).T, np.float32)


def columns(inputs):
    out = np.zeros((P, NCOL), np.float32)

    def put(at, v):
        v = np.asarray(v, np.float32).reshape(-1, P).T
        out[:, at:at + v.shape[1]] = v

    for layer in range(LAYERS):
        for name, k in LAYER_COLS:
            v = np.asarray(inputs[name])[layer]
            if name == "b_gate":
                out[:16, COL[name, layer]] = v.reshape(16)
            else:
                put(COL[name, layer], v)
    for name, k in LAST_COLS:
        v = np.asarray(inputs[name])[0]
        if name.startswith("cmp_pos"):
            out[:, COL[name]:COL[name] + 32] = np.tile(v.T, (2, 1))
        elif v.shape[0] == 64:
            out[:, COL[name]] = np.tile(v, 2)
        else:
            put(COL[name], v)
    return out


def twice(w):
    out = np.zeros(w.shape[:-2] + (P, P), np.float32)
    out[..., :64, :64] = w
    out[..., 64:, 64:] = w
    return out


def head_order(n):
    return np.arange(n).reshape(2, 4, 64).transpose(1, 0, 2).reshape(-1)


def arrays_of(inputs):
    f = {k: np.asarray(v) for k, v in inputs.items()}
    perm = head_order(512)
    cols_in = np.arange(W_IN2)
    cols_in[0:512] = perm
    cols_in[1304:1816] = 1304 + perm
    rows_out = np.arange(1024)
    rows_out[0:512] = perm
    wp = f["w_pool_2"][0]
    small_w = np.zeros((P, 4, P), np.float32)
    small_w[:, 0] = twice(f["w_cmp_k2_2"][0])
    small_w[:, 1] = twice(f["w_cmp_v2_2"][0])
    for c in range(2):
        small_w[:64, 2 + c, :64] = wp[2 * c]
        small_w[64:, 2 + c, 64:] = wp[2 * c + 1]
    cmp1 = np.stack([twice(f[n][0]).transpose(1, 0, 2).reshape(P, -1) for n in ("w_cmp_k1_2", "w_cmp_v1_2")])
    cv = np.stack([f["c"][0], f["c_ctx"]])
    return {
        "x": np.ascontiguousarray(f["x"][0].T), "ctx": np.ascontiguousarray(f["ctx"][0].T),
        "mem": np.ascontiguousarray(f["mem_2"][0].T), "positions": f["positions_2"],
        "cvec": np.ascontiguousarray(cv.reshape(2, KC, P).transpose(2, 1, 0)),
        "w_ada": f["w_ada"], "w_in": f["w_in"], "w_out": f["w_out"], "w_mlp1": f["w_mlp1"], "w_mlp2": f["w_mlp2"],
        "w_mem_kv_2": f["w_mem_kv_2"], "w_in_2": np.ascontiguousarray(f["w_in_2"][:, :, cols_in]),
        "w_out_2": np.ascontiguousarray(f["w_out_2"][:, rows_out, :]), "w_cmp1": cmp1,
        "w_small": small_w.reshape(P, -1), "cols": columns(inputs), "con": constants(), "grid": grid(),
        "dft_x": dft(TX), "dft_c": dft(TC),
    }


def declare(nc, arrays):
    a = {}
    for name, v in arrays.items():
        a[name] = nc.dram_tensor(f"in_{name}", v.shape, mybir.dt.from_np(v.dtype), kind="ExternalInput").ap()
    a["out"] = nc.dram_tensor("out", [D, TX], F32, kind="ExternalOutput").ap()
    build(nc, a)


def kernel(**inputs):
    import concourse.bacc as bacc
    from concourse.bass_utils import run_bass_kernel_spmd

    arrays = arrays_of(inputs)
    nc = bacc.Bacc("TRN2", target_bir_lowering=False, num_devices=1)
    declare(nc, arrays)
    r = run_bass_kernel_spmd(nc, [{f"in_{k}": v for k, v in arrays.items()}], core_ids=[0])
    return np.ascontiguousarray(r.results[0]["out"].T)[None]
```

```python
from contextlib import ExitStack

import numpy as np

import concourse.bass as bass
from concourse import mybir

F32 = mybir.dt.float32
I32 = mybir.dt.int32
ALU = mybir.AluOpType
ACT = mybir.ActivationFunctionType
AXX = mybir.AxisListType.X

P = 128
D = 1024
KC = D // P
TX, TC = 512, 256
T = TX + TC
LAYERS = 2
EPS = 1e-6
HEADS = 4
HD = 128
FF = 4096
W_IN = 2832
W_IN2 = 2840
CONV_K = 31
NCMP = (TX - 32) // 16 + 1
SCALE = 64 ** -0.5
UNITS = [("nsa", c, g, tb) for c in range(4) for tb in range(4) for g in range(2)]
UNITS += [("mem", c, g, tb) for c in range(2) for tb in range(4) for g in range(2)]
PAD = CONV_K // 2
BIG = 1e30
TINY = float(np.finfo(np.float32).tiny)
X_COLS, C_COLS = (0, TX), (TX, TC)

LAYER_COLS = [("b_ada", 48), ("g_pre_mix", 8), ("g_post_mix", 8), ("g_pre_mlp", 8), ("g_post_mlp", 8),
              ("g_mlstm_norm", 4), ("w_qk_conv", 24), ("w_dw", 62), ("b_dw", 2), ("g_conv_ln", 2),
              ("b_conv_ln", 2), ("b_gate", 1)]
LAST_COLS = [("g_norm_2", 8), ("g_q_nsa_2", 1), ("g_k_cmp_2", 1), ("g_k_slc_2", 1), ("g_k_win_2", 1),
             ("g_q_mem_2", 1), ("g_k_mem_2", 1), ("pool_scale_2", 2), ("g_mem_2", 8), ("cmp_pos_k_2", 32),
             ("cmp_pos_v_2", 32)]


def column_offsets():
    at, n = {}, 0
    for layer in range(LAYERS):
        for name, k in LAYER_COLS:
            at[name, layer] = n
            n += k
    for name, k in LAST_COLS:
        at[name] = n
        n += k
    return at, n


COL, NCOL = column_offsets()

PANELS = {"conv": (2320, 512), "gates": (2048, 272), "q": (0, 512), "k": (512, 512), "v": (1024, 512),
          "o": (1536, 512)}
PANELS2 = [(0, 512), (512, 512), (1024, 280), (1304, 512), (1816, 512), (2328, 512)]

TWO_PI = 2 * np.pi
ROUND = 1.5 * 2 ** 23
PI_BELOW = 3.1415925


def split_two_pi():
    parts, rest = [], float(TWO_PI)
    for bits in (9, 21):
        part = np.floor(rest * 2.0 ** bits) / 2.0 ** bits
        parts.append(part)
        rest -= part
    return parts + [rest]


TWO_PI_PARTS = split_two_pi()
SLOTS = 3
ADA_AT = [(4, 5), (6, 7), (8, 9), (10, 11)]
SLOT = 4096

CONSTS = [("ident", P), ("ones", P), ("ones64", P), ("rope_turn", P), ("dft_chan", 256), ("hide_t_lt_s", P),
          ("hide_t_gt_s", P), ("hide_s_gt_t", P), ("cmp_hide", 128), ("head_rows", 512), ("rope_freq", 1),
          ("eps", 1), ("pool_inv", 2), ("pool_first", 32), ("cond_pick", 2)]


def const_offsets():
    at, n = {}, 0
    for name, k in CONSTS:
        at[name] = (n, k)
        n += k
    return at, n


CONST, NCONST = const_offsets()


class Signal:

    def __init__(self, sem):
        self.sem, self.made = sem, 0


class Worker:

    def __init__(self, step):
        self.step, self.seen, self.last = step, {}, None

    def up(self, signal=None):
        signal = signal or self.step
        signal.made += 1
        self.last = (signal.sem, signal.made)
        return signal.sem, 1

    def own(self):
        return self.last

    def next(self, signal, n=1):
        self.seen[signal] = self.seen.get(signal, 0) + n
        return signal.sem, self.seen[signal]


def pt_layout():
    at, n = {}, 0
    for d in range(2):
        for s in range(6):
            for group in ((0, 1, 2, 3), (4, 5)):
                for tb in group:
                    if s >= 4 and tb < 4:
                        seen = True
                    elif (s >= 4) != (tb >= 4):
                        seen = False
                    else:
                        seen = tb >= s if d == 0 else tb <= s
                    if seen:
                        at[d, s, tb] = n
                        n += P
    return at, n


PT_AT, PT_SIZE = pt_layout()


def pt_at(d, s, tb):
    return PT_AT.get((d, s, tb))


def pt_blocks(both):
    out = []
    for s in (4, 5, 0, 1, 2, 3):
        for d in range(2):
            first = 0 if d == 1 or s >= 4 else s
            lo, hi = (0, TX) if s >= 4 else ((s * P, TX) if d == 0 else (0, (s + 1) * P))
            out.append((s, d, lo, hi, 0, pt_at(d, s, first)))
    for j in range(2 if both else 0):
        for d in range(2):
            lo, hi = (j * P, TC) if d == 0 else (0, (j + 1) * P)
            out.append((4 + j, d, lo, hi, TX, pt_at(d, 4 + j, 4 if d == 1 else 4 + j)))
    return out


def build(nc, a):
    with ExitStack() as ctx:
        def sb(name, shape, dt=F32):
            return ctx.enter_context(nc.sbuf_tensor(name, shape, dt))

        def signal(name):
            return Signal(ctx.enter_context(nc.semaphore(name)))

        X = sb("X", [P, KC, T])
        H = sb("H", [P, KC * T])
        R = sb("R", [P, 21504])
        ring = sb("ring", [P, SLOTS, SLOT])
        cols = sb("cols", [P, NCOL])
        con = sb("con", [P, NCONST])
        cond = sb("cond", [P, KC, 32])
        adarow = sb("adarow", [P, 2, 512])
        mod = sb("mod", [P, LAYERS, 48, 2])
        gsc = sb("gsc", [P, 4, KC, 2])
        rs = sb("rs", [P, T])
        tmp = sb("tmp", [P, 2 * T])
        sq = sb("sq", [P, T])
        acol = sb("acol", [P, 96])
        small = sb("small", [P, 96])
        psum = ctx.enter_context(nc.psum_tensor("psum", [P, 8, 512], F32))

        def part(buf, at, *shape):
            n = int(np.prod(shape))
            v = buf[:, at:at + n]
            if len(shape) == 2:
                return v.rearrange("p (a b) -> p a b", a=shape[0])
            if len(shape) == 3:
                return v.rearrange("p (a b c) -> p a b c", a=shape[0], b=shape[1])
            if len(shape) == 4:
                return v.rearrange("p (a b c d) -> p a b c d", a=shape[0], b=shape[1], c=shape[2])
            return v

        Hc = part(H, 0, KC, T)
        acol2 = part(R, 20760, 72)
        Q = O = part(R, 0, 4, T)
        K = part(R, 3072, 4, T)
        V = part(R, 6144, 6, 4, 129)
        M2 = part(R, 9240, 4, T)
        ROWS = part(R, 12312, 4, T)
        FZ = part(R, 15384, 2, T)
        PT = part(R, 12312, PT_SIZE)
        HS = part(R, 17688, 6, 4, 128)
        UPAD = part(R, 17688, 2, 828)
        CV = part(R, 19344, 2, T)
        FA = part(R, 17688, 6, 2, 2, 128)

        def mixed(k):
            return K[:, k, :] if k < 4 else M2[:, k - 4, :]

        HID = part(R, 0, 16, T)
        ACC = part(R, 12312, KC, T)
        GR = part(tmp, 0, 2, T)
        Q2, KS, KW = part(R, 0, 4, TX), part(R, 2048, TX), part(R, 2560, TX)
        KRAW, VRAW = part(R, 3072, TX), part(R, 3584, TX)
        VS, VW = part(R, 4096, 4, P), part(R, 4608, 4, P)
        ZN, VP, ZP = part(R, 5120, 4, TX), part(R, 7168, 2, TX), part(R, 8192, 2, TX)
        QM, ZM = part(R, 9216, 2, TX), part(R, 10240, 2, TX)
        MK, MV = part(R, 11264, 2, TC), part(R, 11776, 2, TC)
        MEM = part(R, 12288, KC, TC)
        KWIN, VWIN = part(R, 14336, NCMP, 32), part(R, 15360, NCMP, 32)
        COS, SIN = part(R, 16384, TX), part(R, 16896, TX)
        PROB = part(R, 17408, 2, 1152)
        GATE = part(R, 19712, 4, 24)
        KCMP, VCMP = part(R, 19808, NCMP), part(R, 19840, P)
        HIDK, HIDV = part(R, 19968, NCMP), part(R, 20000, NCMP)
        POOLT = part(R, 20032, 2, TX)
        PROBT = part(R, 12288, 2, 9, P)
        Y = part(H, 0, KC, TX)

        def const(name):
            at, n = CONST[name]
            return con[:, at:at + n]

        def col(name, i=0, layer=None, n=1):
            at = COL[name if layer is None else (name, layer)] + i
            return cols[:, at:at + n]

        ident, ones, ones64, rope_turn = (const(n) for n in ("ident", "ones", "ones64", "rope_turn"))
        eps = const("eps")

        pe_step, dve_step, act_step = signal("pe_step"), signal("dve_step"), signal("act_step")
        pe_tile_for = {"dve": signal("pe_tile_for_dve"), "act": signal("pe_tile_for_act")}
        dve_bank_free, act_bank_free = signal("dve_bank_free"), signal("act_bank_free")
        bank_free = {"dve": dve_bank_free, "act": act_bank_free}
        dve_ready_pe, act_ready_pe = signal("dve_ready_for_pe"), signal("act_ready_for_pe")
        dve_ready_act, act_ready_dve = signal("dve_ready_for_act"), signal("act_ready_for_dve")
        dve_ready_sp = signal("dve_ready_for_sp")
        pe_norm_sum, act_norm_read = signal("pe_norm_sum"), signal("act_norm_read")
        slot_loaded = [ctx.enter_context(nc.semaphore(f"slot{i}_loaded")) for i in range(SLOTS)]
        s_first = ctx.enter_context(nc.semaphore("vectors_loaded"))
        s_x = ctx.enter_context(nc.semaphore("x_loaded"))
        s_pos = ctx.enter_context(nc.semaphore("grid_loaded"))
        s_rows = ctx.enter_context(nc.semaphore("gate_rows_moved"))
        s_mem = ctx.enter_context(nc.semaphore("mem_loaded"))
        s_tok = ctx.enter_context(nc.semaphore("positions_loaded"))
        s_out = ctx.enter_context(nc.semaphore("out_stored"))

        panels = []
        marks = {}
        tiles = {"dve": [], "act": []}
        shared = []
        frees = {"dve": 0, "act": 0}
        bank_turn = [(b, None, 0) for b in range(6)]
        rows_after = {}
        memory_after = []

        block = ctx.enter_context(nc.Block())

        def prob_blocks(u):
            kind, _, _, tb = UNITS[u]
            if kind == "mem":
                return [P, 2 * P]
            n = tb + 1
            return [0] + [P * (1 + i) for i in range(2 * n)]

        heads = [(MK[:, c, :], TC, "g_k_mem_2", None) for c in range(2)]
        heads += [(Q2[:, c, :], TX, "g_q_nsa_2", slice(0, TX)) for c in range(4)]
        heads += [(KS, TX, "g_k_slc_2", slice(0, TX)), (KW, TX, "g_k_win_2", slice(0, TX))]
        heads += [(QM[:, c, :], TX, "g_q_mem_2", None) for c in range(2)]
        heads += [(KCMP, NCMP, "g_k_cmp_2", slice(31, TX, 16))]

        def prob_at(u, j, n):
            return P if UNITS[u][0] == "mem" else (0, P, P + n)[j]

        def Hs_gate(s, n):
            return rs[:, 0:n] if s == 0 else rs[:, TX:TX + n]

        def g_rows(d):
            return sq if d == 1 else rs

        @block.tensor
        def _(pe):
            w = Worker(pe_step)
            norm_reads = [0]

            def panel(src, kc, width):
                n = len(panels)
                panels.append([src, kc, width, None])
                pe.wait_ge(slot_loaded[n % SLOTS], 16 * (n // SLOTS + 1))
                return part(ring[:, n % SLOTS], 0, kc, width)

            def panel_done():
                panels[-1][3] = w.last

            def tile(reader, last=None):
                last = last or reader
                n, who, count = bank_turn.pop(0)
                if who:
                    pe.wait_ge(bank_free[who].sem, count)
                tiles[reader].append(n)
                if last != reader:
                    shared.append(n)
                frees[last] += 1
                bank_turn.append((n, last, frees[last]))
                return psum[:, n]

            def norm_step(k, streams, chunks):
                if k == 0 and norm_reads[0]:
                    pe.wait_ge(act_norm_read.sem, norm_reads[0])
                pe.wait_ge(*w.next(act_ready_pe))
                for i, (c0, n) in enumerate(streams):
                    mm = pe.matmul(psum[:, 6 + i, 0:n], ones, Hc[:, k, c0:c0 + n], start=k == 0, stop=k == chunks - 1)
                    if k == chunks - 1:
                        mm.then_inc(*w.up(pe_norm_sum))
                        norm_reads[0] += 1

            def norm_sum(streams, chunks=KC):
                for k in range(chunks):
                    norm_step(k, streams, chunks)

            def project(wt, chunk, streams, src, order, reader, wait_each=None):
                for i, (c0, n) in enumerate(streams):
                    b = tile(reader)
                    for k in order:
                        if wait_each and i == 0:
                            pe.wait_ge(*w.next(wait_each))
                        mm = pe.matmul(b[:, 0:n], wt[:, k, chunk * P:chunk * P + P], src(k)[:, c0:c0 + n],
                                       start=k == order[0], stop=k == order[-1])
                    mm.then_inc(*w.up(pe_tile_for[reader]))

            def by_token(wt, blocks, w0, width, src, reader):
                for tb in blocks:
                    b = tile(reader)
                    for k in range(KC):
                        mm = pe.matmul(b[:, 0:width], src(k)[:, tb * P:tb * P + P], wt[:, k, w0:w0 + width],
                                       start=k == 0, stop=k == KC - 1)
                    mm.then_inc(*w.up(pe_tile_for[reader]))

            def ada(layer, panels_of):
                for n in panels_of:
                    wt = panel(a["w_ada"][layer, :, n * 512:(n + 1) * 512], KC, 512)
                    b = tile("act")
                    for k in range(KC):
                        g = 32 * (k % 4)
                        mm = pe.matmul(b[g:g + 32, :], cond[:, k, :], wt[:, k, :], start=k < 4, stop=k >= 4)
                    mm.then_inc(*w.up(pe_tile_for["act"]))
                    panel_done()
                for n in panels_of:
                    pe.wait_ge(*w.next(act_ready_pe))
                    b = tile("dve")
                    for j in range(4):
                        mm = pe.matmul(b[:, 2 * j:2 * j + 2], adarow[:, n % 2, j * P:j * P + P], const("cond_pick"),
                                       start=True, stop=True)
                    mm.then_inc(*w.up(pe_tile_for["dve"]))

            def layer_program(layer):
                both = layer < LAYERS - 1
                streams = [X_COLS, C_COLS] if both else [X_COLS]
                all_streams = [X_COLS, C_COLS]
                nb = 6 if both else 4
                w_in = a["w_in"]
                every = list(range(KC))

                def win(name):
                    c0, n = PANELS[name]
                    return panel(w_in[layer, :, c0:c0 + n], KC, n)

                def h(k):
                    return Hc[:, k, :]

                norm_sum(all_streams)
                wt = win("conv")
                for m in (2, 0, 3, 1):
                    project(wt, m, streams, h, every, "act" if m >= 2 else "dve", act_ready_pe if m == 2 else None)
                panel_done()
                wt = win("gates")
                for c0, n in all_streams:
                    b = tile("dve")
                    for k in range(KC):
                        mm = pe.matmul(b[0:16, 0:n], wt[:, k, 0:16], h(k)[:, c0:c0 + n], start=k == 0, stop=k == KC - 1)
                    mm.then_inc(*w.up(pe_tile_for["dve"]))
                for m in range(2):
                    for c0, n in streams:
                        b = tile("act")
                        for k in range(KC):
                            mm = pe.matmul(b[:, 0:n], wt[:, k, 16 + m * P:16 + m * P + P], h(k)[:, c0:c0 + n],
                                           start=k == 0, stop=k == KC - 1)
                        mm.then_inc(*w.up(pe_tile_for["act"]))
                panel_done()
                for name, some in (("k", all_streams), ("q", streams)):
                    wt = win(name)
                    if name == "q":
                        rows_after[layer] = len(panels)
                    for m in range(4):
                        project(wt, m, some, h, every, "dve")
                    panel_done()
                pe.wait_ge(*w.next(dve_ready_pe))
                b = tile("dve")
                for i in range(6):
                    for d in range(2):
                        for e in range(2):
                            o = ((e * 6 + i) * 2 + d) * 4
                            mm = pe.matmul(b[:, o:o + 4], ROWS[0:4, 2 * d + e, i * P:i * P + P], ident[0:4, 0:4],
                                           start=True, stop=True)
                mm.then_inc(*w.up(pe_tile_for["dve"]))
                wt = win("v")
                by_token(wt, range(3), 0, 512, h, "act")
                pe.wait_ge(*w.next(dve_ready_pe))
                for c0, n in streams:
                    b = tile("dve")
                    for k in range(2):
                        mm = pe.matmul(b[:, 0:n], ones, CV[:, k, c0:c0 + n], start=k == 0, stop=k == 1)
                    mm.then_inc(*w.up(pe_tile_for["dve"]))
                by_token(wt, range(3, 6), 0, 512, h, "act")
                panel_done()
                if norm_reads[0]:
                    pe.wait_ge(act_norm_read.sem, norm_reads[0])
                for k in range(2):
                    pe.wait_ge(*w.next(act_ready_pe))
                    for i, (c0, n) in enumerate(streams):
                        mm = pe.matmul(psum[:, 6 + i, 0:n], ones, M2[:, k, c0:c0 + n], start=k == 0, stop=k == 1)
                        if k == 1:
                            mm.then_inc(*w.up(pe_norm_sum))
                            norm_reads[0] += 1
                pe.wait_ge(*w.next(dve_ready_pe))
                for i in range(nb):
                    b = tile("act")
                    for c in range(2):
                        mm = pe.matmul(b[:, c * 256:c * 256 + 256], FZ[:, c, i * P:i * P + P], const("dft_chan"),
                                       start=True, stop=True)
                    mm.then_inc(*w.up(pe_tile_for["act"]))
                pe.wait_ge(*w.next(act_ready_pe))
                for s, (c0, n) in enumerate(streams):
                    blocks = n // P
                    wt = part(panel_raw(a["dft_x" if s == 0 else "dft_c"], 2 * blocks * n), 0, 2, blocks, n)
                    for c in range(2):
                        b = tile("dve")
                        for i in range(blocks):
                            for cs in range(2):
                                mm = pe.matmul(b[:, 0:n], FA[:, c0 // P + i, c, cs, :], wt[:, cs, i, :],
                                               start=i == 0 and cs == 0, stop=i == blocks - 1 and cs == 1)
                        mm.then_inc(*w.up(pe_tile_for["dve"]))
                    panel_done()

                for hd in range(HEADS):
                    for d in range(2):
                        for c0, n in streams:
                            b = tile("act")
                            mm = pe.matmul(b[:, 0:n], const("head_rows")[0:4, hd * P:hd * P + P], GR[0:4, d, c0:c0 + n],
                                           start=True, stop=True)
                            mm.then_inc(*w.up(pe_tile_for["act"]))
                    for s in (4, 5, 0, 1, 2, 3):
                        b = tile("dve")
                        mm = pe.matmul(b[:, 0:TX], K[:, hd, s * P:s * P + P], Q[:, hd, 0:TX], start=True, stop=True)
                        mm.then_inc(*w.up(pe_tile_for["dve"]))
                    if both:
                        b = tile("dve")
                        for j in range(2):
                            mm = pe.matmul(b[:, j * TC:j * TC + TC], K[:, hd, TX + j * P:TX + j * P + P],
                                           Q[:, hd, TX:T], start=True, stop=True)
                        mm.then_inc(*w.up(pe_tile_for["dve"]))
                    o0 = PANELS["o"][0] + hd * P
                    project(panel(w_in[layer, :, o0:o0 + P], KC, P), 0, streams, h, every, "act")
                    panel_done()
                    ada(layer, ADA_AT[hd])
                    pe.wait_ge(*w.next(dve_ready_pe))
                    for d in range(2):
                        for g in ((0, 1, 2), (3, 4, 5)) if both else ((0, 1, 2), (3,)):
                            b = tile("dve")
                            for i, tb in enumerate(g):
                                keys = [s for s in (4, 5, 0, 1, 2, 3) if pt_at(d, s, tb) is not None]
                                for n, s in enumerate(keys):
                                    at = pt_at(d, s, tb)
                                    mm = pe.matmul(b[:, i * 129:i * 129 + 129], PT[:, at:at + P], V[:, s, hd, :],
                                                   start=n == 0, stop=n == len(keys) - 1)
                            mm.then_inc(*w.up(pe_tile_for["dve"]))
                if both:
                    ada(layer + 1, (0, 1))
                    ada(layer + 1, (2, 3))
                for hd in range(HEADS):
                    pe.wait_ge(*w.next(dve_ready_pe))
                    for g in ((0, 1, 2, 3), (4, 5)) if both else ((0, 1, 2, 3),):
                        b = tile("dve")
                        for i, tb in enumerate(g):
                            mm = pe.transpose(b[:, i * P:i * P + P], HS[:, tb, hd, :], ident)
                        mm.then_inc(*w.up(pe_tile_for["dve"]))
                for half in range(2):
                    wt = panel(a["w_out"][layer, :, half * 512:(half + 1) * 512], KC, 512)
                    for m in range(4):
                        if half == m == 0:
                            pe.wait_ge(*w.next(dve_ready_pe))
                        project(wt, m, streams, mixed, every, "dve")
                        if half * 4 + m >= 2:
                            norm_step(half * 4 + m - 2, streams, KC)
                    panel_done()
                norm_step(6, streams, KC)
                norm_step(7, streams, KC)
                norm_sum(streams)
                for half in range(2):
                    for n in range(4):
                        c0 = half * 2048 + n * 512
                        wt = panel(a["w_mlp1"][layer, :, c0:c0 + 512], KC, 512)
                        for m in range(4):
                            project(wt, m, streams, h, every, "act", act_ready_pe if half == n == m == 0 else None)
                        panel_done()
                    for n in range(4):
                        wt = panel(a["w_mlp2"][layer, half * 2048:half * 2048 + 2048, n * 256:n * 256 + 256], 16, 256)
                        for m in range(2):
                            project(wt, m, streams, lambda k: HID[:, k, :], list(range(16)), "dve",
                                    dve_ready_pe if n == m == 0 else None)
                            if half and 2 * n + m >= 2:
                                norm_step(2 * n + m - 2, streams, KC)
                        panel_done()
                    marks["hid_read", layer, half] = w.last
                norm_step(6, streams, KC)
                norm_step(7, streams, KC)

            def panel_raw(src, width):
                n = len(panels)
                panels.append([src, 0, width, None])
                pe.wait_ge(slot_loaded[n % SLOTS], 16 * (n // SLOTS + 1))
                return ring[:, n % SLOTS]

            pe.wait_ge(s_first, 48)
            pe.wait_ge(*w.next(act_ready_pe))
            ada(0, (0, 1))
            ada(0, (2, 3))
            for layer in range(LAYERS):
                layer_program(layer)

            memory_after.append(len(panels))
            for k in range(KC):
                pe.wait_ge(*w.next(act_ready_pe))
                if k == 0:
                    pe.wait_ge(act_norm_read.sem, norm_reads[0])
                mm = pe.matmul(psum[:, 6, 0:TC], ones, Hc[:, k, 0:TC], start=k == 0, stop=k == KC - 1)
            mm.then_inc(*w.up(pe_norm_sum))
            norm_reads[0] += 1
            pe.wait_ge(*w.next(dve_ready_pe, KC))
            wt = panel(a["w_mem_kv_2"][0], KC, 512)
            for m in range(2):
                project(wt, m, [(0, TC)], lambda k: MEM[:, k, :], list(range(KC)), "act")
            by_token(wt, range(2), 256, 256, lambda k: MEM[:, k, :], "act")
            panel_done()
            norm_sum([X_COLS])

            def h(k):
                return Hc[:, k, :]

            for i, (c0, n) in enumerate(PANELS2):
                wt = panel(a["w_in_2"][0, :, c0:c0 + n], KC, n)
                for m in range({1: 3, 2: 1}.get(i, 4)):
                    project(wt, m, [X_COLS], h, list(range(KC)), "act", dve_ready_pe if i == m == 0 else None)
                if i == 1:
                    by_token(wt, range(4), 384, 128, h, "act")
                if i == 2:
                    by_token(wt, range(4), 128, 152, h, "act")
                panel_done()
            for i, win in enumerate((KWIN, VWIN)):
                pe.wait_ge(*w.next(dve_ready_pe))
                wt = part(panel_raw(a["w_cmp1"][i], SLOT), 0, 32, P)
                b = tile("act")
                for j in range(32):
                    mm = pe.matmul(b[:, 0:NCMP], wt[:, j, :], win[:, :, j], start=j == 0, stop=j == 31)
                mm.then_inc(*w.up(pe_tile_for["act"]))
                panel_done()
            wt = part(panel_raw(a["w_small"], 512), 0, 4, P)
            pe.wait_ge(*w.next(act_ready_pe))
            b = tile("act")
            pe.matmul(b[:, 0:NCMP], wt[:, 0, :], HIDK, start=True, stop=True).then_inc(*w.up(pe_tile_for["act"]))
            b = tile("act")
            pe.matmul(b[0:NCMP, 0:P], HIDV, wt[:, 1, :], start=True, stop=True).then_inc(*w.up(pe_tile_for["act"]))
            for c in range(2):
                pe.wait_ge(*w.next(dve_ready_pe))
                b = tile("dve")
                pe.matmul(b[:, 0:TX], wt[:, 2 + c, :], VP[:, c, :], start=True, stop=True).then_inc(*w.up(pe_tile_for["dve"]))
            panel_done()
            for i in range(len(heads) + 1):
                if i < len(heads):
                    pe.wait_ge(*w.next(act_ready_pe))
                    n = heads[i][1]
                    b = tile("act")
                    pe.matmul(b[:, 0:n], ones64, tmp[:, (i % 2) * TX:(i % 2) * TX + n], start=True,
                                        stop=True).then_inc(*w.up(pe_tile_for["act"]))
                if i and heads[i - 1][3]:
                    pe.wait_ge(*w.next(dve_ready_pe))
                    z, n = heads[i - 1][0:2]
                    b = tile("dve")
                    pe.matmul(b[:, 0:n], rope_turn, z, start=True, stop=True).then_inc(*w.up(pe_tile_for["dve"]))

            pe.wait_ge(act_norm_read.sem, norm_reads[0])
            bank_turn[:0] = [(6, None, 0), (7, None, 0)]

            def scores(u):
                kind, c, g, tb = UNITS[u]
                lo, hi = 64 * g, 64 * g + 64
                if kind == "mem":
                    q, keys = QM[lo:hi, c, tb * P:tb * P + P], [MK[lo:hi, c, :]]
                else:
                    n = (tb + 1) * P
                    q, keys = Q2[lo:hi, c, tb * P:tb * P + P], [KCMP[lo:hi, :], KS[lo:hi, 0:n], KW[lo:hi, 0:n]]
                for k in keys:
                    b = tile("dve", "act")
                    pe.matmul(b[:, 0:k.shape[1]], q, k, start=True, stop=True).then_inc(*w.up(pe_tile_for["dve"]))

            def turn(u):
                pe.wait_ge(*w.next(dve_ready_pe))
                blocks = prob_blocks(u)
                for i in range(0, len(blocks), 4):
                    b = tile("act")
                    for j, at in enumerate(blocks[i:i + 4]):
                        mm = pe.transpose(b[:, j * P:j * P + P], PROB[:, u % 2, at:at + P], ident)
                    mm.then_inc(*w.up(pe_tile_for["act"]))

            def values(u):
                pe.wait_ge(*w.next(act_ready_pe))
                kind, c, g, tb = UNITS[u]
                lo, hi = 64 * g, 64 * g + 64
                if kind == "mem":
                    v = [MV[:, i, (2 * c + g) * 64:(2 * c + g) * 64 + 64] for i in range(2)]
                else:
                    v = [VCMP[:, lo:hi]] + [VS[:, i, lo:hi] for i in range(tb + 1)]
                    v += [VW[:, i, lo:hi] for i in range(tb + 1)]
                b = tile("dve")
                for i, vi in enumerate(v):
                    mm = pe.matmul(b[lo:hi, 0:P], vi, PROBT[:, u % 2, i, :], start=i == 0, stop=i == len(v) - 1)
                mm.then_inc(*w.up(pe_tile_for["dve"]))

            pe.wait_ge(*w.next(dve_ready_pe))
            scores(0)
            for u in range(len(UNITS)):
                if u + 1 < len(UNITS):
                    scores(u + 1)
                if u:
                    values(u - 1)
                turn(u)
            values(len(UNITS) - 1)
            pe.wait_ge(*w.next(dve_ready_pe))
            for half in range(2):
                wt = panel(a["w_out_2"][0, :, half * 512:(half + 1) * 512], KC, 512)
                for m in range(4):
                    project(wt, m, [X_COLS], lambda k: Y[:, k, :], list(range(KC)), "dve")
                panel_done()

        @block.vector
        def _(dve):
            w = Worker(dve_step)
            st = iter(tiles["dve"])

            def tile():
                return psum[:, next(st)]

            def recip_rs(c0, n):
                dve.wait_ge(*w.next(act_ready_dve))
                dve.reciprocal(rs[:, c0:c0 + n], rs[:, c0:c0 + n]).then_inc(*w.up())

            def apply_norm(streams, gslot, dst):
                for c0, n in streams:
                    recip_rs(c0, n)
                dve.wait_ge(*w.own())
                for k in range(KC):
                    for s, (c0, n) in enumerate(streams):
                        ins = dve.scalar_tensor_tensor(out=dst[:, k, c0:c0 + n], in0=X[:, k, c0:c0 + n],
                                                       scalar=gsc[:, gslot, k, s:s + 1], in1=rs[:, c0:c0 + n],
                                                       op0=ALU.mult, op1=ALU.mult)
                        ins.then_inc(*w.up(dve_ready_act if s == len(streams) - 1 else None))

            def ada(layer, panels_of):
                for n in panels_of:
                    dve.wait_ge(*w.next(pe_tile_for["dve"]))
                    b = tile()
                    for s in range(2):
                        ins = dve.tensor_tensor(mod[:, layer, 4 * n:4 * n + 4, s],
                                                b[:, 0:8].rearrange("p (j s) -> p j s", s=2)[:, :, s],
                                                col("b_ada", 4 * n, layer, 4), ALU.add)
                        if s == 0:
                            ins.then_inc(*w.up())
                    ins.then_inc(*w.up(dve_bank_free))

            def gains(layer, gslot, name, section, plus_one):
                dve.wait_ge(*w.own())
                for s in range(2):
                    m = mod[:, layer, section * 8:section * 8 + 8, s]
                    dve.scalar_tensor_tensor(out=gsc[:, gslot, :, s], in0=m, scalar=1.0 if plus_one else 0.0,
                                                   in1=col(name, 0, layer, 8), op0=ALU.add, op1=ALU.mult).then_inc(*w.up())
                dve.wait_ge(*w.own())

            def residual(streams, gslot):
                for c0, n in streams:
                    recip_rs(c0, n)
                dve.wait_ge(*w.own())
                for k in range(KC):
                    for s, (c0, n) in enumerate(streams):
                        dve.scalar_tensor_tensor(out=ACC[:, k, c0:c0 + n], in0=ACC[:, k, c0:c0 + n],
                                                       scalar=gsc[:, gslot, k, s:s + 1], in1=rs[:, c0:c0 + n],
                                                       op0=ALU.mult, op1=ALU.mult).then_inc(*w.up())
                    dve.wait_ge(*w.own())
                    n = sum(q[1] for q in streams)
                    dve.tensor_tensor(X[:, k, 0:n], X[:, k, 0:n], ACC[:, k, 0:n], ALU.add).then_inc(*w.up(dve_ready_act))

            def layer_program(layer):
                both = layer < LAYERS - 1
                streams = [X_COLS, C_COLS] if both else [X_COLS]
                all_streams = [X_COLS, C_COLS]
                tn = T if both else TX

                gains(layer, 0, "g_pre_mix", 1, True)
                apply_norm(all_streams, 0, Hc)
                dve.memset(R[:, 17688:17688 + 1656], 0.0).then_inc(*w.up())
                dve.wait_ge(*w.own())
                for m in range(2):
                    for s, (c0, n) in enumerate(streams):
                        u0 = PAD + (0 if s == 0 else TX + 2 * PAD)
                        dve.wait_ge(*w.next(act_ready_dve))
                        dve.wait_ge(*w.next(pe_tile_for["dve"]))
                        b = tile()
                        dve.tensor_tensor(UPAD[:, m, u0:u0 + n], b[:, 0:n], Hs_gate(s, n), ALU.mult).then_inc(*w.up(dve_bank_free))
                        dve.wait_ge(*w.own())
                        dve.wait_ge(*w.own())
                        dve.sem_inc(*w.up(dve_ready_act))
                for c0, n in all_streams:
                    dve.wait_ge(*w.next(pe_tile_for["dve"]))
                    b = tile()
                    dve.tensor_scalar(sq[0:16, c0:c0 + n], b[0:16, 0:n], col("b_gate", 0, layer)[0:16, :], None,
                                      ALU.add).then_inc(*w.up(dve_bank_free))
                dve.wait_ge(*w.own())
                dve.sem_inc(*w.up(dve_ready_sp))

                def taps():
                    for m in range(2):
                        for i in range(CONV_K):
                            tap = col("w_dw", 2 * i + m, layer)
                            dve.wait_ge(*w.own())
                            for s, (c0, n) in enumerate(streams):
                                u0 = 0 if s == 0 else TX + 2 * PAD
                                cv = CV[:, m, c0:c0 + n]
                                u = UPAD[:, m, u0 + i:u0 + i + n]
                                if i == 0:
                                    dve.tensor_scalar(cv, u, tap, col("b_dw", m, layer), ALU.mult,
                                                      ALU.add).then_inc(*w.up())
                                else:
                                    dve.scalar_tensor_tensor(out=cv, in0=u, scalar=tap, in1=cv, op0=ALU.mult,
                                                             op1=ALU.add).then_inc(*w.up())
                            yield

                tap = taps()

                def short_conv(dst, m, j, some):
                    for c0, n in some:
                        dve.wait_ge(*w.next(pe_tile_for["dve"]))
                        b = tile()
                        t = [col("w_qk_conv", 8 * i + j + m, layer) for i in range(3)]
                        dve.tensor_scalar(dst[:, m, c0:c0 + n], b[:, 0:n], t[1], None, ALU.mult).then_inc(*w.up())
                        dve.wait_ge(*w.own())
                        dve.scalar_tensor_tensor(out=dst[:, m, c0 + 1:c0 + n], in0=b[:, 0:n - 1], scalar=t[0],
                                                 in1=dst[:, m, c0 + 1:c0 + n], op0=ALU.mult,
                                                 op1=ALU.add).then_inc(*w.up())
                        dve.wait_ge(*w.own())
                        dve.scalar_tensor_tensor(out=dst[:, m, c0:c0 + n - 1], in0=b[:, 1:n], scalar=t[2],
                                                 in1=dst[:, m, c0:c0 + n - 1], op0=ALU.mult,
                                                 op1=ALU.add).then_inc(*w.up(dve_bank_free))
                    for _ in range(6):
                        next(tap, None)

                dve.memset(V[:, :, :, 128:129], 1.0).then_inc(*w.up())
                for m in range(4):
                    short_conv(K, m, 4, all_streams)
                dve.wait_ge(*w.next(act_ready_dve))
                for d in range(2):
                    i_row, f_row = ROWS[0:4, 2 * d, :], ROWS[0:4, 2 * d + 1, :]
                    ln = (rs if d == 0 else sq)[0:4, :]
                    dve.wait_ge(*w.own())
                    dve.scalar_tensor_tensor(out=f_row, in0=f_row, scalar=0.0, in1=ln, op0=ALU.min,
                                             op1=ALU.subtract).then_inc(*w.up())
                    dve.wait_ge(*w.own())

                    def scan(dst, src, kind):
                        carry = 0.0
                        for lo, hi in ((TX, T), (0, TX)):
                            o, i = dst[:, lo:hi], src[:, lo:hi]
                            if d == 1:
                                o, i = o[:, ::-1], i[:, ::-1]
                            dve.tensor_tensor_scan(o, i, i, carry, kind, ALU.bypass).then_inc(*w.up())
                            dve.wait_ge(*w.own())
                            carry = dst[:, hi - 1:hi] if d == 0 else dst[:, lo:lo + 1]

                    scan(f_row, f_row, ALU.add)
                    dve.tensor_tensor(i_row, i_row, f_row, ALU.subtract).then_inc(*w.up())
                    dve.wait_ge(*w.own())
                    scan(GR[0:4, d, :], i_row, ALU.max)
                    dve.tensor_tensor(f_row, f_row, GR[0:4, d, :],
                                      ALU.add).then_inc(*w.up(dve_ready_act if d == 1 else None))
                for m in range(4):
                    short_conv(Q, m, 0, streams)
                dve.wait_ge(*w.own())
                dve.wait_ge(*w.next(act_ready_dve))
                dve.sem_inc(*w.up(dve_ready_pe))
                for _ in tap:
                    pass
                dve.wait_ge(*w.next(pe_tile_for["dve"]))
                b = tile()
                dve.tensor_copy(acol[:, :], b[:, 0:96]).then_inc(*w.up(dve_bank_free))
                dve.wait_ge(*w.own())
                dve.sem_inc(*w.up(dve_ready_pe))
                for c0, n in streams:
                    dve.wait_ge(*w.next(pe_tile_for["dve"]))
                    b = tile()
                    for k in range(2):
                        cv = CV[:, k, c0:c0 + n]
                        ins = dve.scalar_tensor_tensor(out=cv, in0=b[:, 0:n], scalar=-1.0 / 256, in1=cv, op0=ALU.mult,
                                                       op1=ALU.add)
                        if k == 0:
                            ins.then_inc(*w.up())
                    ins.then_inc(*w.up(dve_bank_free))
                dve.wait_ge(*w.own())
                dve.sem_inc(*w.up(dve_ready_act))
                for c0, n in streams:
                    recip_rs(c0, n)
                dve.wait_ge(*w.own())
                for k in range(2):
                    dve.tensor_tensor(M2[:, 2 + k, 0:tn], CV[:, k, 0:tn], rs[:, 0:tn],
                                      ALU.mult).then_inc(*w.up(dve_ready_act))
                dve.wait_ge(*w.own())
                dve.sem_inc(*w.up(dve_ready_pe))
                for c0, n in streams:
                    for c in range(2):
                        dve.wait_ge(*w.next(pe_tile_for["dve"]))
                        b = tile()
                        dve.tensor_copy(M2[:, c, c0:c0 + n], b[:, 0:n]).then_inc(*w.up(dve_bank_free))

                en = acol[:, 48:96].rearrange("p (i d h) -> p i d h", i=6, d=2)
                av = acol[:, 0:48].rearrange("p (i d h) -> p i d h", i=6, d=2)
                blocks = pt_blocks(both)
                nb = 6 if both else 4
                for hd in range(HEADS):
                    dve.wait_ge(*w.next(act_ready_dve, 2 * len(streams)))
                    for s, d, lo, hi, t0, at in blocks:
                        if t0 == 0 and s >= 4:
                            continue
                        wv = PT[:, at:at + hi - lo]
                        dve.tensor_scalar(wv, g_rows(d)[:, t0 + lo:t0 + hi], av[:, s, d, hd:hd + 1], 0.0, ALU.subtract,
                                          ALU.max).then_inc(*w.up())
                        dve.wait_ge(*w.own())
                        o = 0 if d == 0 else hi - lo - P
                        hide = const("hide_t_lt_s" if d == 0 else "hide_t_gt_s")
                        dve.tensor_tensor(wv[:, o:o + P], wv[:, o:o + P], hide,
                                          ALU.add).then_inc(*w.up(dve_ready_act))
                    for s, d, lo, hi, t0, at in blocks:
                        new = t0 == 0 and d == 0 or t0 and (s, d) == (4, 0)
                        last = t0 == 0 and d == 1 or t0 and (s, d) == (5, 1)
                        if new:
                            dve.wait_ge(*w.next(pe_tile_for["dve"]))
                            b = tile()
                        dve.wait_ge(*w.next(act_ready_dve))
                        wv = PT[:, at:at + hi - lo]
                        c0 = (s - 4) * TC if t0 else 0
                        ins = dve.scalar_tensor_tensor(out=wv, in0=b[:, c0 + lo:c0 + hi], scalar=HD ** -0.5, in1=wv,
                                                       op0=ALU.mult, op1=ALU.mult)
                        ins.then_inc(*w.up(dve_bank_free if last else None))
                    dve.wait_ge(*w.own())
                    dve.sem_inc(*w.up(dve_ready_pe))
                    ada(layer, ADA_AT[hd])
                    for d in range(2):
                        for g in ((0, 1, 2), (3, 4, 5)) if both else ((0, 1, 2), (3,)):
                            dve.wait_ge(*w.next(pe_tile_for["dve"]))
                            b = tile()
                            ng = len(g)
                            bv = b[:, 0:ng * 129].rearrange("p (i e) -> p i e", e=129)
                            den = small[:, 4 * (2 * d + g[0] // 3):4 * (2 * d + g[0] // 3) + ng]
                            dve.tensor_tensor(den, bv[:, :, 128], en[:, g[0]:g[0] + ng, d, hd],
                                              ALU.max).then_inc(*w.up())
                            dve.wait_ge(*w.own())
                            dve.scalar_tensor_tensor(out=den, in0=bv[:, :, 128], scalar=-1.0, in1=den,
                                                     op0=ALU.mult, op1=ALU.max).then_inc(*w.up())
                            dve.wait_ge(*w.own())
                            dve.reciprocal(den, den).then_inc(*w.up())
                            dve.wait_ge(*w.own())
                            for i, tb in enumerate(g):
                                if d == 0:
                                    ins = dve.tensor_scalar(HS[:, tb, hd, :], bv[:, i, 0:128], den[:, i:i + 1], None,
                                                            ALU.mult)
                                else:
                                    ins = dve.scalar_tensor_tensor(out=HS[:, tb, hd, :], in0=bv[:, i, 0:128],
                                                                   scalar=den[:, i:i + 1], in1=HS[:, tb, hd, :],
                                                                   op0=ALU.mult, op1=ALU.add)
                                if i < ng - 1:
                                    ins.then_inc(*w.up())
                            ins.then_inc(*w.up(dve_bank_free))
                    dve.wait_ge(*w.own())
                    dve.sem_inc(*w.up(dve_ready_act))
                    for tb in range(nb):
                        dve.bn_stats(small[:, 16 + 6 * tb:22 + 6 * tb], HS[:, tb, hd, :]).then_inc(*w.up())
                    dve.wait_ge(*w.own())
                    for tb in range(nb):
                        i = 2 * (tb * 4 + hd)
                        dve.bn_aggr(acol2[:, i:i + 2], small[:, 16 + 6 * tb:22 + 6 * tb]).then_inc(*w.up())
                dve.wait_ge(*w.own())
                dve.sem_inc(*w.up(dve_ready_act))
                dve.wait_ge(*w.next(act_ready_dve))
                root = acol2[:, 48:48 + nb * 4]
                dve.reciprocal(root, root).then_inc(*w.up())
                dve.wait_ge(*w.own())
                for hd in range(HEADS):
                    for tb in range(nb):
                        i = tb * 4 + hd
                        dve.tensor_scalar(HS[:, tb, hd, :], HS[:, tb, hd, :], acol2[:, 2 * i:2 * i + 1],
                                          acol2[:, 48 + i:49 + i], ALU.subtract, ALU.mult).then_inc(*w.up())
                    dve.wait_ge(*w.own())
                    dve.sem_inc(*w.up(dve_ready_pe))
                if both:
                    ada(layer + 1, (0, 1))
                    ada(layer + 1, (2, 3))
                dve.wait_ge(*w.next(act_ready_dve))
                for hd in range(HEADS):
                    for c0, n in streams:
                        dve.wait_ge(*w.next(pe_tile_for["dve"]))
                        b = tile()
                        dve.scalar_tensor_tensor(out=mixed(hd)[:, c0:c0 + n], in0=b[:, 0:n],
                                                 scalar=col("g_mlstm_norm", hd, layer), in1=O[:, hd, c0:c0 + n],
                                                 op0=ALU.mult, op1=ALU.mult).then_inc(*w.up(dve_bank_free))
                dve.wait_ge(*w.own())
                dve.sem_inc(*w.up(dve_ready_pe))
                gains(layer, 1, "g_post_mix", 2, False)
                gains(layer, 2, "g_pre_mlp", 4, True)
                gains(layer, 3, "g_post_mlp", 5, False)
                for k in range(KC):
                    for c0, n in streams:
                        dve.wait_ge(*w.next(pe_tile_for["dve"]))
                        b = tile()
                        dve.tensor_copy(ACC[:, k, c0:c0 + n], b[:, 0:n]).then_inc(*w.up(dve_bank_free))
                    marks["acc", layer, 0, k] = w.last
                residual(streams, 1)
                apply_norm(streams, 2, Hc)
                for half in range(2):
                    for k in range(16):
                        dve.wait_ge(*w.next(act_ready_dve))
                        dve.tensor_tensor(HID[:, k, 0:tn], HID[:, k, 0:tn], HID[:, k, 0:tn],
                                          ALU.mult).then_inc(*w.up(dve_ready_pe))
                    for k in range(KC):
                        for c0, n in streams:
                            dve.wait_ge(*w.next(pe_tile_for["dve"]))
                            b = tile()
                            acc = ACC[:, k, c0:c0 + n]
                            if half == 0:
                                dve.tensor_copy(acc, b[:, 0:n]).then_inc(*w.up(dve_bank_free))
                            else:
                                dve.tensor_tensor(acc, b[:, 0:n], acc, ALU.add).then_inc(*w.up(dve_bank_free))
                        marks["acc", layer, 1, k] = w.last
                residual(streams, 3)

            dve.wait_ge(s_first, 48)
            dve.memset(small[:, :], 0.0).then_inc(*w.up())
            dve.wait_ge(*w.own())
            dve.wait_ge(s_x, 32)
            dve.wait_ge(s_pos, 16)
            for k in range(KC):
                dve.tensor_tensor(X[:, k, 0:TX], X[:, k, 0:TX], Hc[:, k, 0:TX], ALU.add).then_inc(*w.up())
            dve.wait_ge(*w.own())
            dve.sem_inc(*w.up(dve_ready_act))
            ada(0, (0, 1))
            ada(0, (2, 3))
            for layer in range(LAYERS):
                layer_program(layer)
            dve.wait_ge(*w.own())
            dve.sem_inc(*w.up(dve_ready_sp))
            recip_rs(0, TC)
            dve.wait_ge(*w.own())
            for k in range(KC):
                dve.scalar_tensor_tensor(out=MEM[:, k, :], in0=MEM[:, k, :], scalar=col("g_mem_2", k),
                                               in1=rs[:, 0:TC], op0=ALU.mult, op1=ALU.mult).then_inc(*w.up(dve_ready_pe))
            dve.wait_ge(*w.own())
            dve.sem_inc(*w.up(dve_ready_act))
            dve.wait_ge(s_tok, 16)
            kk = POOLT[:, 0, :]
            dve.tensor_scalar(SIN, COS.bitcast(I32), const("rope_freq"), None, ALU.mult).then_inc(*w.up())
            dve.wait_ge(*w.own())
            dve.tensor_scalar(kk, SIN, 1.0 / TWO_PI, ROUND, ALU.mult, ALU.add).then_inc(*w.up())
            dve.wait_ge(*w.own())
            dve.tensor_scalar(kk, kk, ROUND, None, ALU.subtract).then_inc(*w.up())
            for c in TWO_PI_PARTS:
                dve.wait_ge(*w.own())
                dve.scalar_tensor_tensor(out=SIN, in0=kk, scalar=-c, in1=SIN, op0=ALU.mult, op1=ALU.add).then_inc(*w.up())
            dve.wait_ge(*w.own())
            dve.tensor_scalar(SIN, SIN, PI_BELOW, -PI_BELOW, ALU.min, ALU.max).then_inc(*w.up(dve_ready_act))
            dve.wait_ge(*w.next(act_ready_dve))
            dve.tensor_tensor(COS, COS, COS, ALU.mult).then_inc(*w.up())
            dve.wait_ge(*w.own())
            dve.tensor_scalar(COS, COS, -2.0, 1.0, ALU.mult, ALU.add).then_inc(*w.up())
            dve.memset(VCMP, 0.0).then_inc(*w.up())
            dve.memset(PROB[:, :, 0:P], 0.0).then_inc(*w.up())
            recip_rs(*X_COLS)
            dve.wait_ge(*w.own())
            for k in range(KC):
                dve.scalar_tensor_tensor(out=Hc[:, k, 0:TX], in0=X[:, k, 0:TX], scalar=col("g_norm_2", k),
                                               in1=rs[:, 0:TX], op0=ALU.mult, op1=ALU.mult).then_inc(*w.up(dve_ready_pe))
            dve.wait_ge(*w.next(act_ready_dve))
            for raw, win, pos in ((KRAW, KWIN, "cmp_pos_k_2"), (VRAW, VWIN, "cmp_pos_v_2")):
                for part_ in range(2):
                    src = raw[:, 16 * part_:16 * part_ + 16 * NCMP].rearrange("p (n j) -> p n j", j=16)
                    dve.tensor_tensor(win[:, :, 16 * part_:16 * part_ + 16], src,
                                            col(pos, 16 * part_, n=16).unsqueeze(1).to_broadcast([P, NCMP, 16]),
                                            ALU.add).then_inc(*w.up())
                dve.wait_ge(*w.own())
                dve.sem_inc(*w.up(dve_ready_pe))
            dve.wait_ge(*w.next(act_ready_dve))
            for c in range(2):
                cur, lo = VP[:, c, :], 0
                where = {0: cur}
                for i, sh in enumerate((1, 2) if c == 0 else (1, 2, 4, 8)):
                    if sh == (2, 8)[c]:
                        where[0], lo = cur, 64
                    nxt = POOLT[:, i % 2, :]
                    dve.wait_ge(*w.own())
                    dve.tensor_tensor(nxt[lo:, sh:TX], cur[lo:, sh:TX], cur[lo:, 0:TX - sh], ALU.add).then_inc(*w.up())
                    dve.tensor_copy(nxt[lo:, 0:sh], cur[lo:, 0:sh]).then_inc(*w.up())
                    cur = nxt
                for lo, res in ((0, where[0]), (64, cur)):
                    r = res[lo:lo + 64, :]
                    dve.wait_ge(*w.own())
                    dve.tensor_tensor(r[:, 0:16], r[:, 0:16], const("pool_first")[lo:lo + 64, 16 * c:16 * c + 16],
                                            ALU.mult).then_inc(*w.up())
                    dve.wait_ge(*w.own())
                    vp = VP[lo:lo + 64, c, :]
                    dve.scalar_tensor_tensor(out=vp, in0=r, scalar=const("pool_inv")[lo:lo + 64, c:c + 1],
                                                   in1=vp, op0=ALU.mult, op1=ALU.subtract).then_inc(*w.up())
                dve.wait_ge(*w.own())
                dve.sem_inc(*w.up(dve_ready_pe))
            for c in range(2):
                dve.wait_ge(*w.next(pe_tile_for["dve"]))
                b = tile()
                dve.scalar_tensor_tensor(out=Y[:, 4 + c, :], in0=b[:, 0:TX], scalar=col("pool_scale_2", c),
                                              in1=ZP[:, c, :], op0=ALU.mult, op1=ALU.mult).then_inc(*w.up(dve_bank_free))
            for i in range(len(heads) + 1):
                if i < len(heads):
                    z, n, gain, _ = heads[i]
                    r = (rs, sq)[i % 2][:, 0:n]
                    dve.wait_ge(*w.next(act_ready_dve))
                    dve.reciprocal(r, r).then_inc(*w.up())
                    dve.wait_ge(*w.own())
                    dve.scalar_tensor_tensor(out=z, in0=z, scalar=col(gain), in1=r, op0=ALU.mult, op1=ALU.mult).then_inc(*w.up())
                    dve.wait_ge(*w.own())
                    dve.sem_inc(*w.up(dve_ready_act))
                    if heads[i][3]:
                        dve.wait_ge(*w.own())
                        dve.sem_inc(*w.up(dve_ready_pe))
                if i and heads[i - 1][3]:
                    z, n, _, sl = heads[i - 1]
                    dve.wait_ge(*w.next(pe_tile_for["dve"]))
                    b = tile()
                    t0, t1 = POOLT[:, 0, 0:n], POOLT[:, 1, 0:n]
                    dve.wait_ge(*w.own())
                    dve.tensor_tensor(t0, z, COS[:, sl], ALU.mult).then_inc(*w.up())
                    dve.tensor_tensor(t1, b[:, 0:n], SIN[:, sl], ALU.mult).then_inc(*w.up(dve_bank_free))
                    dve.wait_ge(*w.own())
                    dve.tensor_tensor(z, t0, t1, ALU.add).then_inc(*w.up())
            dve.wait_ge(*w.own())
            dve.sem_inc(*w.up(dve_ready_pe))

            def parts_of(u):
                kind, c, g, tb = UNITS[u]
                if kind == "mem":
                    return [(TC, 0, None)]
                n = (tb + 1) * P
                return [(NCMP, 0, const("cmp_hide")[:, tb * NCMP:(tb + 1) * NCMP]), (n, tb * P, const("hide_s_gt_t")),
                        (n, tb * P, const("hide_s_gt_t"))]

            def highest(u):
                o = 16 * (u % 2)
                ps = parts_of(u)
                for j, (n, h0, hide) in enumerate(ps):
                    dve.wait_ge(*w.next(pe_tile_for["dve"]))
                    b = tile()
                    if hide is not None:
                        m = hide.shape[1]
                        dve.tensor_tensor(b[:, h0:h0 + m], b[:, h0:h0 + m], hide, ALU.add).then_inc(*w.up())
                        dve.wait_ge(*w.own())
                    dve.tensor_reduce(small[:, o + j:o + j + 1], b[:, 0:n], AXX, ALU.max).then_inc(*w.up())
                dve.wait_ge(*w.own())
                dve.tensor_scalar(small[:, o + 4:o + 4 + len(ps)], small[:, o:o + len(ps)], -BIG / 10, -SCALE,
                                        ALU.max, ALU.mult).then_inc(*w.up(dve_ready_act))

            def normalise(u):
                kind, c, g, tb = UNITS[u]
                o = 16 * (u % 2) + 8
                ps = parts_of(u)
                dve.wait_ge(*w.next(act_ready_dve))
                den = small[:, o:o + len(ps)]
                dve.tensor_scalar(den, den, TINY, None, ALU.max).then_inc(*w.up())
                dve.wait_ge(*w.own())
                dve.reciprocal(den, den).then_inc(*w.up())
                dve.wait_ge(*w.own())
                if kind == "nsa":
                    hd = 4 * g + c
                    dve.tensor_tensor(den, den, GATE[:, tb, 3 * hd:3 * hd + 3], ALU.mult).then_inc(*w.up())
                    dve.wait_ge(*w.own())
                for j, (n, _, _) in enumerate(ps):
                    at = prob_at(u, j, n)
                    pr = PROB[:, u % 2, at:at + n]
                    dve.tensor_scalar(pr, pr, den[:, j:j + 1], None, ALU.mult).then_inc(*w.up())
                dve.wait_ge(*w.own())
                dve.sem_inc(*w.up(dve_ready_pe))

            def gated(u):
                kind, c, g, tb = UNITS[u]
                lo, hi = 64 * g, 64 * g + 64
                z, k = (ZN, c) if kind == "nsa" else (ZM, 6 + c)
                dve.wait_ge(*w.next(pe_tile_for["dve"]))
                b = tile()
                dve.tensor_tensor(Y[lo:hi, k, tb * P:tb * P + P], b[lo:hi, 0:P], z[lo:hi, c, tb * P:tb * P + P],
                                       ALU.mult).then_inc(*w.up(dve_bank_free))

            highest(0)
            for u in range(len(UNITS)):
                normalise(u)
                if u + 1 < len(UNITS):
                    highest(u + 1)
                if u:
                    gated(u - 1)
            gated(len(UNITS) - 1)
            dve.wait_ge(*w.own())
            dve.sem_inc(*w.up(dve_ready_pe))
            for k in range(KC):
                dve.wait_ge(*w.next(pe_tile_for["dve"]))
                b = tile()
                dve.tensor_tensor(X[:, k, 0:TX], b[:, 0:TX], X[:, k, 0:TX], ALU.add).then_inc(*w.up(dve_bank_free))
            dve.wait_ge(*w.own())
            dve.sem_inc(*w.up(dve_ready_sp))

        @block.scalar
        def _(act):
            w = Worker(act_step)
            st = iter(tiles["act"])

            def tile():
                return psum[:, next(st)]

            def squares(src, streams, each=False):
                n = sum(q[1] for q in streams)
                for k in range(KC):
                    if each:
                        act.wait_ge(*w.next(dve_ready_act))
                    act.activation(Hc[:, k, 0:n], src[:, k, 0:n], ACT.Square).then_inc(*w.up(act_ready_pe))

            def squares_of_product(layer, which, streams):
                n = sum(q[1] for q in streams)
                for k in range(KC):
                    act.wait_ge(*marks["acc", layer, which, k])
                    act.activation(Hc[:, k, 0:n], ACC[:, k, 0:n], ACT.Square).then_inc(*w.up(act_ready_pe))

            def roots(streams, count):
                for i, (c0, n) in enumerate(streams):
                    act.wait_ge(*w.next(pe_norm_sum))
                    act.activation(rs[:, c0:c0 + n], psum[:, 6 + i, 0:n], ACT.Sqrt, scale=1.0 / count,
                                   bias=eps).then_inc(*w.up(act_norm_read))
                    act.wait_ge(*w.own())
                    act.sem_inc(*w.up(act_ready_dve))

            def ada(panels_of):
                for n in panels_of:
                    act.wait_ge(*w.next(pe_tile_for["act"]))
                    b = tile()
                    act.copy(adarow[:, n % 2, :], b[:, :]).then_inc(*w.up(act_bank_free))
                    act.wait_ge(*w.own())
                    act.sem_inc(*w.up(act_ready_pe))

            def shifts(streams, layer, section):
                for k in range(KC):
                    act.wait_ge(*w.next(dve_ready_act))
                    for s, (c0, n) in enumerate(streams):
                        m = mod[:, layer, section * 8 + k, s:s + 1]
                        act.activation(Hc[:, k, c0:c0 + n], Hc[:, k, c0:c0 + n], ACT.Identity, bias=m).then_inc(*w.up(act_ready_pe if s == len(streams) - 1 else None))

            def layer_program(layer):
                both = layer < LAYERS - 1
                streams = [X_COLS, C_COLS] if both else [X_COLS]
                all_streams = [X_COLS, C_COLS]
                tn = T if both else TX
                squares(X, all_streams, each=layer > 0)
                roots(all_streams, D)
                shifts(all_streams, layer, 0)
                for m in range(2):
                    for s, (c0, n) in enumerate(streams):
                        if m:
                            act.wait_ge(*w.next(dve_ready_act))
                        act.wait_ge(*w.next(pe_tile_for["act"]))
                        b = tile()
                        act.activation(Hs_gate(s, n), b[:, 0:n], ACT.Sigmoid).then_inc(*w.up(act_bank_free))
                        act.wait_ge(*w.own())
                        act.sem_inc(*w.up(act_ready_dve))
                act.wait_ge(*w.next(dve_ready_act, len(streams)))
                for m in range(2):
                    for c0, n in streams:
                        act.wait_ge(*w.next(pe_tile_for["act"]))
                        b = tile()
                        act.copy(FZ[:, m, c0:c0 + n], b[:, 0:n]).then_inc(*w.up(act_bank_free))
                act.wait_ge(s_rows, 64 * (layer + 1))
                for d in range(2):
                    t = (rs if d == 0 else sq)[0:4, :]
                    act.activation(t, ROWS[0:4, 2 * d + 1, :], ACT.Abs).then_inc(*w.up())
                    act.wait_ge(*w.own())
                    act.activation(t, t, ACT.Exp, scale=-1.0).then_inc(*w.up())
                    act.wait_ge(*w.own())
                    act.activation(t, t, ACT.Ln, bias=1.0).then_inc(*w.up(act_ready_dve if d == 1 else None))
                act.wait_ge(*w.next(dve_ready_act))
                act.activation(ROWS[0:4, 1:4:2, :], ROWS[0:4, 1:4:2, :], ACT.Exp,
                               scale=-1.0).then_inc(*w.up(act_ready_dve))

                def v_blocks(some):
                    for i in some:
                        act.wait_ge(*w.next(pe_tile_for["act"]))
                        b = tile()
                        act.copy(V[:, i, :, 0:128],
                                 b[:, 0:512].rearrange("p (h e) -> p h e", h=4)).then_inc(*w.up(act_bank_free))

                v_blocks(range(6))
                act.wait_ge(*w.next(dve_ready_act))
                for k in range(2):
                    act.activation(M2[:, k, 0:tn], CV[:, k, 0:tn], ACT.Square).then_inc(*w.up(act_ready_pe))
                roots(streams, 256)
                for k in range(2):
                    act.wait_ge(*w.next(dve_ready_act))
                    act.activation(M2[:, 2 + k, 0:tn], M2[:, 2 + k, 0:tn], ACT.Silu,
                                   scale=col("g_conv_ln", k, layer), bias=col("b_conv_ln", k, layer)).then_inc(*w.up())

                def gate_chunk(m):
                    for c0, n in streams:
                        act.wait_ge(*w.next(pe_tile_for["act"]))
                        b = tile()
                        act.copy(O[:, m, c0:c0 + n], b[:, 0:n]).then_inc(*w.up(act_bank_free))

                for i in range(6 if both else 4):
                    act.wait_ge(*w.next(pe_tile_for["act"]))
                    b = tile()
                    act.copy(FA[:, i], b[:, 0:512].rearrange("p (c s e) -> p c s e", c=2,
                                                             s=2)).then_inc(*w.up(act_bank_free))
                act.wait_ge(*w.own())
                act.sem_inc(*w.up(act_ready_pe))
                av = acol[:, 0:48].rearrange("p (i d h) -> p i d h", i=6, d=2)
                for hd in range(HEADS):
                    if hd:
                        act.wait_ge(*w.next(dve_ready_act))
                    for d in range(2):
                        for c0, n in streams:
                            act.wait_ge(*w.next(pe_tile_for["act"]))
                            b = tile()
                            act.copy(g_rows(d)[:, c0:c0 + n], b[:, 0:n]).then_inc(*w.up(act_bank_free))
                            act.wait_ge(*w.own())
                            act.sem_inc(*w.up(act_ready_dve))
                    for s, d, lo, hi, t0, at in pt_blocks(both):
                        wv = PT[:, at:at + hi - lo]
                        if t0 == 0 and s >= 4:
                            act.activation(wv, g_rows(d)[:, lo:hi], ACT.Exp, scale=-1.0,
                                           bias=av[:, s, d, hd:hd + 1]).then_inc(*w.up(act_ready_dve))
                        else:
                            act.wait_ge(*w.next(dve_ready_act))
                            act.activation(wv, wv, ACT.Exp, scale=-1.0).then_inc(*w.up(act_ready_dve))
                    gate_chunk(hd)
                    ada(ADA_AT[hd])
                act.wait_ge(*w.own())
                act.activation(O[:, :, 0:tn], O[:, :, 0:tn], ACT.Sigmoid).then_inc(*w.up())
                act.wait_ge(*w.next(dve_ready_act))
                act.wait_ge(*w.next(dve_ready_act))
                nb = 6 if both else 4
                act.activation(acol2[:, 48:48 + nb * 4], acol2[:, 0:nb * 8].rearrange("p (i t) -> p i t", t=2)[:, :, 1],
                               ACT.Sqrt, bias=eps).then_inc(*w.up(act_ready_dve))
                if both:
                    ada((0, 1))
                    ada((2, 3))
                act.wait_ge(*w.own())
                act.sem_inc(*w.up(act_ready_dve))
                squares_of_product(layer, 0, streams)
                roots(streams, D)
                squares(X, streams, each=True)
                roots(streams, D)
                shifts(streams, layer, 3)
                for half in range(2):
                    if half:
                        act.wait_ge(*marks["hid_read", layer, 0])
                    for k in range(16):
                        for c0, n in streams:
                            act.wait_ge(*w.next(pe_tile_for["act"]))
                            b = tile()
                            act.activation(HID[:, k, c0:c0 + n], b[:, 0:n], ACT.Relu).then_inc(*w.up(act_bank_free))
                        act.wait_ge(*w.own())
                        act.sem_inc(*w.up(act_ready_dve))
                squares_of_product(layer, 1, streams)
                roots(streams, D)

            act.wait_ge(s_first, 48)
            act.activation(cond[:, :, :], cond[:, :, :], ACT.Silu).then_inc(*w.up(act_ready_pe))
            ada((0, 1))
            ada((2, 3))
            act.wait_ge(*w.next(dve_ready_act))
            for layer in range(LAYERS):
                layer_program(layer)
            act.wait_ge(*w.next(dve_ready_act, KC))
            act.wait_ge(s_mem, 16)
            squares(MEM, [(0, TC)])
            roots([(0, TC)], D)
            for m in range(2):
                act.wait_ge(*w.next(pe_tile_for["act"]))
                b = tile()
                act.copy(MK[:, m, :], b[:, 0:TC]).then_inc(*w.up(act_bank_free))
            for m in range(2):
                act.wait_ge(*w.next(pe_tile_for["act"]))
                b = tile()
                act.copy(MV[:, m, :], b[:, 0:TC]).then_inc(*w.up(act_bank_free))
            act.wait_ge(*w.next(dve_ready_act))
            act.wait_ge(*w.next(dve_ready_act))
            act.activation(COS, SIN, ACT.Sin, scale=0.5).then_inc(*w.up())
            act.activation(SIN, SIN, ACT.Sin).then_inc(*w.up(act_ready_dve))
            squares(X, [X_COLS])
            roots([X_COLS], D)

            def into(dst, func=ACT.Copy, n=TX):
                act.wait_ge(*w.next(pe_tile_for["act"]))
                b = tile()
                act.activation(dst, b[:, 0:n], func).then_inc(*w.up(act_bank_free))

            for c in range(4):
                into(Q2[:, c, :])
            for dst in (KRAW, VRAW, KS):
                into(dst)
            act.wait_ge(*w.own())
            act.sem_inc(*w.up(act_ready_dve))
            for i in range(4):
                into(VS[:, i, :], n=P)
            into(KW)
            for i in range(4):
                act.wait_ge(*w.next(pe_tile_for["act"]))
                b = tile()
                act.copy(VW[:, i, :], b[:, 0:P]).then_inc(*w.up())
                act.activation(GATE[:, i, :], b[:, P:P + 24], ACT.Sigmoid).then_inc(*w.up(act_bank_free))
            for c in range(4):
                into(ZN[:, c, :], ACT.Silu)
            for c in range(2):
                into(VP[:, c, :])
            act.wait_ge(*w.own())
            act.sem_inc(*w.up(act_ready_dve))
            for c in range(2):
                into(ZP[:, c, :], ACT.Silu)
            for c in range(2):
                into(QM[:, c, :])
            for c in range(2):
                into(ZM[:, c, :], ACT.Silu)
            for dst in (HIDK, HIDV):
                into(dst, ACT.Gelu_apprx_tanh, NCMP)
            act.wait_ge(*w.own())
            act.sem_inc(*w.up(act_ready_pe))
            into(KCMP, n=NCMP)
            act.wait_ge(*w.next(pe_tile_for["act"]))
            b = tile()
            act.copy(VCMP[0:NCMP, :], b[0:NCMP, 0:P]).then_inc(*w.up(act_bank_free))
            act.wait_ge(*w.own())

            def head_square(i):
                z, n = heads[i][0:2]
                act.activation(tmp[:, (i % 2) * TX:(i % 2) * TX + n], z, ACT.Square).then_inc(*w.up(act_ready_pe))

            head_square(0)
            for i in range(len(heads)):
                if i + 1 < len(heads):
                    head_square(i + 1)
                if i >= 2:
                    act.wait_ge(*w.next(dve_ready_act))
                n = heads[i][1]
                act.wait_ge(*w.next(pe_tile_for["act"]))
                b = tile()
                act.activation((rs, sq)[i % 2][:, 0:n], b[:, 0:n], ACT.Sqrt, bias=eps).then_inc(*w.up(act_bank_free))
                act.wait_ge(*w.own())
                act.sem_inc(*w.up(act_ready_dve))
            act.wait_ge(*w.next(dve_ready_act, 2))
            banks = iter(shared)

            def exps(u):
                o = 16 * (u % 2)
                kind, c, g, tb = UNITS[u]
                act.wait_ge(*w.next(dve_ready_act))
                for j, n in enumerate([TC] if kind == "mem" else [NCMP, (tb + 1) * P, (tb + 1) * P]):
                    at = prob_at(u, j, n)
                    act.activation(PROB[:, u % 2, at:at + n], psum[:, next(banks), 0:n], ACT.Exp, scale=SCALE,
                                        bias=small[:, o + 4 + j:o + 5 + j], accum_out=small[:, o + 8 + j:o + 9 + j]).then_inc(*w.up(act_bank_free))
                act.wait_ge(*w.own())
                act.sem_inc(*w.up(act_ready_dve))

            def turned(u):
                nb = len(prob_blocks(u))
                for i in range(0, nb, 4):
                    m = min(4, nb - i)
                    act.wait_ge(*w.next(pe_tile_for["act"]))
                    b = tile()
                    act.copy(PROBT[:, u % 2, i:i + m, :], b[:, 0:m * P].rearrange("p (i t) -> p i t", t=P)).then_inc(*w.up(act_bank_free))
                act.wait_ge(*w.own())
                act.sem_inc(*w.up(act_ready_pe))

            exps(0)
            for u in range(len(UNITS)):
                if u + 1 < len(UNITS):
                    exps(u + 1)
                turned(u)

        @block.sync
        def _(sp):
            w = Worker(None)
            sp.dma_start(cond[:, :, :], a["cond"]).then_inc(s_first, 16)
            sp.dma_start(cols[:, :], a["cols"]).then_inc(s_first, 16)
            sp.dma_start(con[:, :], a["con"]).then_inc(s_first, 16)
            sp.dma_start(X[:, :, 0:TX], a["x"].rearrange("(k p) t -> p k t", p=P)).then_inc(s_x, 16)
            sp.dma_start(X[:, :, TX:T], a["ctx"].rearrange("(k p) t -> p k t", p=P)).then_inc(s_x, 16)
            sp.dma_start(Hc[:, :, 0:TX], a["grid"].rearrange("(k p) t -> p k t", p=P)).then_inc(s_pos, 16)

            def load(n):
                src, kc, width, _ = panels[n]
                if n >= SLOTS:
                    sp.wait_ge(*panels[n - SLOTS][3])
                if kc:
                    dst = part(ring[:, n % SLOTS], 0, kc, width)
                    src = src.rearrange("(k p) n -> p k n", p=P)
                else:
                    dst = ring[:, n % SLOTS, 0:width]
                sp.dma_start(dst, src).then_inc(slot_loaded[n % SLOTS], 16)

            n = 0
            for layer in range(LAYERS):
                stop = rows_after[layer]
                while n < stop:
                    load(n)
                    n += 1
                sp.wait_ge(*w.next(dve_ready_sp))
                for j in range(4):
                    sp.dma_start(ROWS[0:4, j, :], sq[4 * j:4 * j + 4, :]).then_inc(s_rows, 16)
            while n < memory_after[0]:
                load(n)
                n += 1
            sp.wait_ge(*w.next(dve_ready_sp))
            sp.dma_start(MEM, a["mem"].rearrange("(k p) t -> p k t", p=P)).then_inc(s_mem, 16)
            sp.dma_start(COS.bitcast(I32), a["positions"][0, :].partition_broadcast(P)).then_inc(s_tok, 16)
            while n < len(panels):
                load(n)
                n += 1
            sp.wait_ge(*w.next(dve_ready_sp))
            sp.dma_start(a["out"].rearrange("(k p) t -> p k t", p=P), X[:, :, 0:TX]).then_inc(s_out, 16)
            sp.wait_ge(s_out, 16)


def constants():
    i, j = np.arange(P)[:, None], np.arange(P)[None, :]
    c = np.zeros((P, NCONST), np.float32)

    def put(name, v):
        at, n = CONST[name]
        v = np.asarray(v)
        c[:v.shape[0], at:at + v.shape[1]] = v

    put("ident", np.eye(P))
    put("ones", np.ones((P, P)))
    put("ones64", (i // 64 == j // 64) / 64.0)
    turn = np.zeros((P, P))
    for g in (0, 64):
        for k in range(8):
            turn[g + 8 + k, g + k] = -1.0
            turn[g + k, g + 8 + k] = 1.0
    put("rope_turn", turn)
    ang = 2 * np.pi * (np.outer(np.arange(64), np.arange(64)) % 64) / 64
    chan = np.zeros((P, 256))
    for g in (0, 64):
        chan[g:g + 64, g:g + 64] = np.cos(ang) / 8
        chan[g:g + 64, P + g:P + g + 64] = np.sin(ang) / 8
    put("dft_chan", chan)
    put("hide_t_lt_s", np.where(j < i, BIG, 0.0))
    put("hide_t_gt_s", np.where(j > i, BIG, 0.0))
    put("hide_s_gt_t", np.where(j > i, -BIG, 0.0))
    hide = np.zeros((P, 4 * NCMP))
    for tb in range(4):
        hide[:, tb * NCMP:(tb + 1) * NCMP] = np.where(np.arange(NCMP)[None, :] * 16 + 31 > tb * P + i, -BIG, 0.0)
    put("cmp_hide", hide)
    put("head_rows", np.repeat(np.eye(4), P, axis=1))
    freq = np.zeros((P, 1), np.float32)
    inv = np.float32(500000.0) ** (-np.arange(8, dtype=np.float32) / np.float32(8))
    for g in (0, 8, 64, 72):
        freq[g:g + 8, 0] = inv
    put("rope_freq", freq)
    put("eps", np.full((P, 1), EPS))
    win = np.array([[2, 8], [4, 16]], np.float64)[np.arange(P) // 64]
    put("pool_inv", 1 / win)
    put("cond_pick", np.stack([np.arange(P) % 32 == v for v in range(2)], 1))
    t = np.arange(16)
    put("pool_first", (win[:, :, None] / np.minimum(t + 1, win[:, :, None])).reshape(P, 32))
    return c


def dft(n):
    ang = 2 * np.pi * (np.outer(np.arange(n), np.arange(n)) % n) / n
    m = np.stack([np.cos(ang), -np.sin(ang)]) / np.sqrt(n)
    return m.reshape(2, n // P, P, n).transpose(2, 0, 1, 3).reshape(P, -1).astype(np.float32)


def grid():
    rows = TX // 64
    quarter = D // 4
    freq = np.exp(np.float32(-np.log(10000.0)) * np.arange(quarter, dtype=np.float32) / np.float32(quarter))
    freq = freq.astype(np.float32)
    r = np.repeat(np.arange(rows, dtype=np.float32), 64)[:, None] * freq
    c = np.tile(np.arange(64, dtype=np.float32), rows)[:, None] * freq
    return np.ascontiguousarray(np.concatenate([np.sin(r), np.cos(r), np.sin(c), np.cos(c)], -1).T, np.float32)


def columns(inputs):
    out = np.zeros((P, NCOL), np.float32)

    def put(at, v):
        v = np.asarray(v, np.float32).reshape(-1, P).T
        out[:, at:at + v.shape[1]] = v

    for layer in range(LAYERS):
        for name, k in LAYER_COLS:
            v = np.asarray(inputs[name])[layer]
            if name == "b_gate":
                out[:16, COL[name, layer]] = v.reshape(16)
            else:
                put(COL[name, layer], v)
    for name, k in LAST_COLS:
        v = np.asarray(inputs[name])[0]
        if name.startswith("cmp_pos"):
            out[:, COL[name]:COL[name] + 32] = np.tile(v.T, (2, 1))
        elif v.shape[0] == 64:
            out[:, COL[name]] = np.tile(v, 2)
        else:
            put(COL[name], v)
    return out


def twice(w):
    out = np.zeros(w.shape[:-2] + (P, P), np.float32)
    out[..., :64, :64] = w
    out[..., 64:, 64:] = w
    return out


def head_order(n):
    return np.arange(n).reshape(2, 4, 64).transpose(1, 0, 2).reshape(-1)


def arrays_of(inputs):
    f = {k: np.asarray(v) for k, v in inputs.items()}
    perm = head_order(512)
    cols_in = np.arange(W_IN2)
    cols_in[0:512] = perm
    cols_in[1304:1816] = 1304 + perm
    rows_out = np.arange(1024)
    rows_out[0:512] = perm
    wp = f["w_pool_2"][0]
    small_w = np.zeros((P, 4, P), np.float32)
    small_w[:, 0] = twice(f["w_cmp_k2_2"][0])
    small_w[:, 1] = twice(f["w_cmp_v2_2"][0])
    for c in range(2):
        small_w[:64, 2 + c, :64] = wp[2 * c]
        small_w[64:, 2 + c, 64:] = wp[2 * c + 1]
    cmp1 = np.stack([twice(f[n][0]).transpose(1, 0, 2).reshape(P, -1) for n in ("w_cmp_k1_2", "w_cmp_v1_2")])
    cond = np.zeros((P, KC, 32), np.float32)
    cond[:, :, 0:2] = np.stack([f["c"][0], f["c_ctx"]]).reshape(2, KC, P).transpose(2, 1, 0)
    return {
        "x": np.ascontiguousarray(f["x"][0].T), "ctx": np.ascontiguousarray(f["ctx"][0].T),
        "mem": np.ascontiguousarray(f["mem_2"][0].T), "positions": f["positions_2"],
        "cond": cond,
        "w_ada": f["w_ada"], "w_in": f["w_in"], "w_out": f["w_out"], "w_mlp1": f["w_mlp1"], "w_mlp2": f["w_mlp2"],
        "w_mem_kv_2": f["w_mem_kv_2"], "w_in_2": np.ascontiguousarray(f["w_in_2"][:, :, cols_in]),
        "w_out_2": np.ascontiguousarray(f["w_out_2"][:, rows_out, :]), "w_cmp1": cmp1,
        "w_small": small_w.reshape(P, -1), "cols": columns(inputs), "con": constants(), "grid": grid(),
        "dft_x": dft(TX), "dft_c": dft(TC),
    }


def declare(nc, arrays):
    a = {}
    for name, v in arrays.items():
        a[name] = nc.dram_tensor(f"in_{name}", v.shape, mybir.dt.from_np(v.dtype), kind="ExternalInput").ap()
    a["out"] = nc.dram_tensor("out", [D, TX], F32, kind="ExternalOutput").ap()
    build(nc, a)


def kernel(**inputs):
    import concourse.bacc as bacc
    from concourse.bass_utils import run_bass_kernel_spmd

    arrays = arrays_of(inputs)
    nc = bacc.Bacc("TRN2", target_bir_lowering=False, num_devices=1)
    declare(nc, arrays)
    r = run_bass_kernel_spmd(nc, [{f"in_{k}": v for k, v in arrays.items()}], core_ids=[0])
    return np.ascontiguousarray(r.results[0]["out"].T)[None]
```

```python
from contextlib import ExitStack

import numpy as np

import concourse.bass as bass
from concourse import mybir

F32 = mybir.dt.float32
F32R = mybir.dt.float32r
I32 = mybir.dt.int32
ALU = mybir.AluOpType
ACT = mybir.ActivationFunctionType
AXX = mybir.AxisListType.X

P = 128
D = 1024
KC = D // P
TX, TC = 512, 256
T = TX + TC
LAYERS = 2
EPS = 1e-6
HEADS = 4
HD = 128
FF = 4096
W_IN2 = 2840
CONV_K = 31
NCMP = (TX - 32) // 16 + 1
SCALE = 64 ** -0.5
UNITS = [("nsa", c, g, tb) for c in range(4) for tb in range(4) for g in range(2)]
UNITS += [("mem", c, g, tb) for c in range(2) for tb in range(4) for g in range(2)]
PAD = CONV_K // 2
BIG = 1e30
TINY = float(np.finfo(np.float32).tiny)
X_COLS, C_COLS = (0, TX), (TX, TC)

LAYER_COLS = [("b_ada", 48), ("g_pre_mix", 8), ("g_post_mix", 8), ("g_pre_mlp", 8), ("g_post_mlp", 8),
              ("g_mlstm_norm", 4), ("w_qk_conv", 24), ("w_dw", 62), ("b_dw", 2), ("g_conv_ln", 2),
              ("b_conv_ln", 2), ("b_gate", 1)]
LAST_COLS = [("g_norm_2", 8), ("g_q_nsa_2", 1), ("g_k_cmp_2", 1), ("g_k_slc_2", 1), ("g_k_win_2", 1),
             ("g_q_mem_2", 1), ("g_k_mem_2", 1), ("pool_scale_2", 2), ("g_mem_2", 8), ("cmp_pos_k_2", 32),
             ("cmp_pos_v_2", 32)]


def column_offsets():
    at, n = {}, 0
    for layer in range(LAYERS):
        for name, k in LAYER_COLS:
            at[name, layer] = n
            n += k
    for name, k in LAST_COLS:
        at[name] = n
        n += k
    return at, n


COL, NCOL = column_offsets()

W_IN_AT = {"q": 0, "k": 512, "v": 1024, "o": 1536, "gates": 2048, "f": 2064, "conv": 2320}
W_IN2_AT = {"q": 0, "k_raw": 512, "v_raw": 640, "ks": 768, "kw": 896, "v": 1024, "gate": 1280, "z": 1304, "vp": 1816,
            "zp": 2072, "qm": 2328, "zm": 2584}
SPLIT_AT = {35: 0, 36: 1, 37: 2, 38: 3, 39: 4, 40: 5, 43: 6}

TWO_PI = 2 * np.pi
ROUND = 1.5 * 2 ** 23
PI_BELOW = 3.1415925


def split_two_pi():
    parts, rest = [], float(TWO_PI)
    for bits in (9, 21):
        part = np.floor(rest * 2.0 ** bits) / 2.0 ** bits
        parts.append(part)
        rest -= part
    return parts + [rest]


TWO_PI_PARTS = split_two_pi()
SLOTS = 3
SECTIONS = 6
ADA_STEPS = [(layer, j) for layer in range(LAYERS) for j in range(SECTIONS * KC)]
ADA_START, ADA_W_OUT = 2 * KC, 6
GRID = 64
SLOT = 4096
UNIT = KC * P
RAWS, SPLITS = 2, 4
QUARTERS = FF // D

CONSTS = [("ident", P), ("ones", P), ("ones64", P), ("rope_turn", P), ("dft_chan", 256), ("hide_t_lt_s", P),
          ("hide_t_gt_s", P), ("hide_s_gt_t", P), ("cmp_hide", 128), ("head_rows", 512), ("rope_freq", 1),
          ("eps", 1), ("pool_inv", 2), ("pool_first", 32), ("cond_pick", 2)]


def const_offsets():
    at, n = {}, 0
    for name, k in CONSTS:
        at[name] = (n, k)
        n += k
    return at, n


CONST, NCONST = const_offsets()


class Signal:

    def __init__(self, sem):
        self.sem, self.made = sem, 0


class Worker:

    def __init__(self, step):
        self.step, self.seen, self.last = step, {}, None

    def up(self, signal=None):
        signal = signal or self.step
        signal.made += 1
        self.last = (signal.sem, signal.made)
        return signal.sem, 1

    def own(self):
        return self.last

    def next(self, signal, n=1):
        self.seen[signal] = self.seen.get(signal, 0) + n
        return signal.sem, self.seen[signal]


def pt_layout():
    at, n = {}, 0
    for d in range(2):
        for s in range(6):
            for group in ((0, 1, 2, 3), (4, 5)):
                for tb in group:
                    if s >= 4 and tb < 4:
                        seen = True
                    elif (s >= 4) != (tb >= 4):
                        seen = False
                    else:
                        seen = tb >= s if d == 0 else tb <= s
                    if seen:
                        at[d, s, tb] = n
                        n += P
    return at, n


PT_AT, PT_SIZE = pt_layout()


def pt_at(d, s, tb):
    return PT_AT.get((d, s, tb))


def pt_blocks(both):
    out = []
    for s in (4, 5, 0, 1, 2, 3):
        for d in range(2):
            first = 0 if d == 1 or s >= 4 else s
            lo, hi = (0, TX) if s >= 4 else ((s * P, TX) if d == 0 else (0, (s + 1) * P))
            out.append((s, d, lo, hi, 0, pt_at(d, s, first)))
    for j in range(2 if both else 0):
        for d in range(2):
            lo, hi = (j * P, TC) if d == 0 else (0, (j + 1) * P)
            out.append((4 + j, d, lo, hi, TX, pt_at(d, 4 + j, 4 if d == 1 else 4 + j)))
    return out


def build(nc, a):
    with ExitStack() as ctx:
        def sb(name, shape, dt=F32):
            return ctx.enter_context(nc.sbuf_tensor(name, shape, dt))

        def signal(name):
            return Signal(ctx.enter_context(nc.semaphore(name)))

        cols = sb("cols", [P, NCOL])
        con = sb("con", [P, NCONST])
        cond = sb("cond", [P, KC, 32])
        mod = sb("mod", [P, LAYERS, 48, 2])
        gsc = sb("gsc", [P, 4, KC, 2])
        rs = sb("rs", [P, T])
        acol = sb("acol", [P, 96])
        small = sb("small", [P, 96])
        with nc.sbuf_tensor("X", [P, KC, T], F32) as X, nc.sbuf_tensor("H", [P, KC * T], F32) as H, \
                nc.sbuf_tensor("R", [P, 21528], F32) as R, nc.sbuf_tensor("ring", [P, SLOTS * SLOT], F32) as ring, \
                nc.sbuf_tensor("tmp", [P, 2 * T], F32) as tmp, nc.sbuf_tensor("sq", [P, T], F32) as sq, \
                nc.sbuf_tensor("adarow", [P, 2, P], F32) as adarow, \
                nc.sbuf_tensor("spare", [P, T], F32) as spare:
            pass
        rounded = [("X", 0, 2 * KC * T), ("R", 0, KC * T), ("R", KC * T, 24 + KC * T),
                   ("R", 24 + 2 * KC * T, KC * T), ("R", 24 + 3 * KC * T, 4 * T), ("ring", 0, SLOT),
                   ("ring", SLOT, 2 * SLOT), ("tmp", 0, 2 * T), ("sq", 0, T), ("adarow", 0, 2 * P),
                   ("spare", 0, T)]
        rounded = {(name, at): sb(f"{name}_rounded_{at}", [P, n], F32R) for name, at, n in rounded}
        psum = ctx.enter_context(nc.psum_tensor("psum", [P, 8, 512], F32))

        def part(buf, at, *shape):
            n = int(np.prod(shape))
            v = buf[:, at:at + n]
            if len(shape) == 2:
                return v.rearrange("p (a b) -> p a b", a=shape[0])
            if len(shape) == 3:
                return v.rearrange("p (a b c) -> p a b c", a=shape[0], b=shape[1])
            if len(shape) == 4:
                return v.rearrange("p (a b c d) -> p a b c d", a=shape[0], b=shape[1], c=shape[2])
            return v

        def rounded_part(name, at, *shape):
            first = max(a for n, a in rounded if n == name and a <= at)
            return part(rounded[name, first], at - first, *shape)

        Hc = part(H, 0, KC, T)
        acol2 = part(R, 20760, 72)
        Q = O = part(R, 0, 4, T)
        K = part(R, 3072, 4, T)
        V = part(R, 6144, 6, 4, 129)
        M2 = part(R, 9240, 4, T)
        ROWS = part(R, 12312, 4, T)
        FZ = part(R, 15384, 2, T)
        PT = part(R, 12312, PT_SIZE)
        HS = part(R, 17688, 6, 4, 128)
        UPAD = part(R, 17688, 2, 828)
        CV = part(R, 19344, 2, T)
        FA = part(R, 17688, 6, 2, 2, 128)

        def mixed(k):
            return K[:, k, :] if k < 4 else M2[:, k - 4, :]

        WHOLE = [ring[:, i * UNIT:(i + 1) * UNIT] for i in range(RAWS)]
        FIRST = [part(R, i * SLOT, KC, 512) for i in range(ADA_START // 4)]
        GRID_ROWS, GRID_COLS = part(H, 0, KC // 2, TX // GRID), part(H, 64, KC // 2, GRID)
        DIRECT = [ring[:, (RAWS + i) * UNIT:(RAWS + i + 1) * UNIT] for i in range(RAWS)]
        W_R = rounded_part("ring", SLOT, SPLITS, 2, UNIT)
        HID_HI_R = rounded_part("R", 0, KC, T)
        HID_LO, HID_LO_R = part(R, KC * T, KC, T), rounded_part("R", KC * T, KC, T)
        H_HI_R = rounded_part("X", KC * T, KC, T)
        X_R = rounded_part("X", 0, KC, T)
        MIX_LO, MIX_LO_R = [X[:, k, :] for k in range(KC)], [X_R[:, k, :] for k in range(KC)]
        MLP_LO = [part(R, 18456 + k * T, T) for k in range(4)] + [part(tmp, k * T, T) for k in range(2)]
        MLP_LO += [sq[:, :], spare[:, :]]
        MLP_LO_R = [rounded_part("R", 18456 + k * T, T) for k in range(4)]
        MLP_LO_R += [rounded_part("tmp", k * T, T) for k in range(2)]
        MLP_LO_R += [rounded_part("sq", 0, T), rounded_part("spare", 0, T)]
        LAST_LO = [[buf[:, k, TX:T] for buf in (X, Hc)] for k in range(KC)]
        both_rounded = rounded_part("X", 0, 2, KC, T)
        LAST_LO_R = [both_rounded[:, :, k, TX:T] for k in range(KC)]
        Y_HI_R, Y_LO_R = rounded_part("R", 0, KC, TX), rounded_part("X", KC * T, KC, TX)
        OUT_SQ = [part(R, k * T, T) for k in range(4)] + [part(R, 6144 + k * T, T) for k in range(4)]
        ACC = part(R, 12312, KC, T)
        GR = part(tmp, 0, 2, T)
        Q2, KS, KW = part(R, 0, 4, TX), part(R, 2048, TX), part(R, 2560, TX)
        KRAW, VRAW = part(R, 3072, TX), part(R, 3584, TX)
        VS, VW = part(R, 4096, 4, P), part(R, 4608, 4, P)
        ZN, VP, ZP = part(R, 5120, 4, TX), part(R, 7168, 2, TX), part(R, 8192, 2, TX)
        QM, ZM = part(R, 9216, 2, TX), part(R, 10240, 2, TX)
        MK, MV = part(R, 11264, 2, TC), part(R, 11776, 2, TC)
        MEM = part(R, 12288, KC, TC)
        MEM_SQ = part(R, 17408, KC, TC)
        KWIN, VWIN = part(R, 14336, NCMP, 32), part(R, 15360, NCMP, 32)
        COS, SIN = part(R, 16384, TX), part(R, 16896, TX)
        PROB = part(R, 17408, 2, 2, TX)
        GATE = part(R, 19712, 4, 24)
        KCMP = part(R, 19808, NCMP)
        HIDK, HIDV = part(R, 19968, NCMP), part(R, 20000, NCMP)
        POOLT = part(R, 20032, 2, TX)
        PROBT = part(R, 12288, 2, 8, P)
        VCMP, DIAG = part(R, 14336, 4, P), part(R, 15360, 2, 2, P)
        CMP, CMPT = part(H, 4096, 2, 4, 4, 32), part(H, 5120, 8, P)
        Y = part(H, 0, KC, TX)

        def mixed_low(k):
            return rounded_part("R", 3072 + k * T if k < 4 else 9240 + (k - 4) * T, T)

        def const(name):
            at, n = CONST[name]
            return con[:, at:at + n]

        def col(name, i=0, layer=None, n=1):
            at = COL[name if layer is None else (name, layer)] + i
            return cols[:, at:at + n]

        ident, ones, ones64, rope_turn = (const(n) for n in ("ident", "ones", "ones64", "rope_turn"))
        eps = const("eps")

        pe_step, dve_step, act_step = signal("pe_step"), signal("dve_step"), signal("act_step")
        pe_tile_for = {"dve": signal("pe_tile_for_dve"), "act": signal("pe_tile_for_act")}
        dve_bank_free, act_bank_free = signal("dve_bank_free"), signal("act_bank_free")
        bank_free = {"dve": dve_bank_free, "act": act_bank_free}
        dve_ready_pe, act_ready_pe = signal("dve_ready_for_pe"), signal("act_ready_for_pe")
        dve_ready_act, act_ready_dve = signal("dve_ready_for_act"), signal("act_ready_for_dve")
        dve_ready_sp = signal("dve_ready_for_sp")
        act_ready_pool, pool_ready_pe = signal("act_ready_for_pool"), signal("pool_ready_for_pe")
        whole_loaded = [ctx.enter_context(nc.semaphore(f"whole{i}_loaded")) for i in range(RAWS)]
        first_loaded = [ctx.enter_context(nc.semaphore(f"first_modulation{i}_loaded")) for i in range(ADA_START // 4)]
        direct_loaded = [ctx.enter_context(nc.semaphore(f"direct{i}_loaded")) for i in range(RAWS)]
        dve_head_ready, act_head_square = signal("dve_head_ready_for_pe"), signal("act_head_square_ready")
        dve_y_ready, act_y_upper, dve_y_lower = (signal(n) for n in ("dve_y_ready", "act_y_upper_ready",
                                                                     "dve_y_lower_ready"))
        act_row_ready = signal("act_modulation_row_ready")
        act_scores_read = signal("act_scores_read")
        pe_norm_sum, act_norm_read = signal("pe_norm_sum"), signal("act_norm_read")
        s_first = ctx.enter_context(nc.semaphore("vectors_loaded"))
        s_kept = ctx.enter_context(nc.semaphore("x_kept"))
        s_back = ctx.enter_context(nc.semaphore("x_back"))
        s_x = ctx.enter_context(nc.semaphore("x_loaded"))
        s_pos = ctx.enter_context(nc.semaphore("grid_loaded"))
        s_rows = ctx.enter_context(nc.semaphore("gate_rows_moved"))
        s_mem = ctx.enter_context(nc.semaphore("mem_loaded"))
        s_tok = ctx.enter_context(nc.semaphore("positions_loaded"))
        s_out = ctx.enter_context(nc.semaphore("out_stored"))

        marks = {}
        tiles = {"dve": [], "act": []}
        frees = {"dve": 0, "act": 0}
        bank_turn = [(b, None, 0) for b in range(6)]
        direct = []
        units = []
        turns = [0]
        loads = []

        block = ctx.enter_context(nc.Block())

        def keys_seen(u):
            kind, _, _, tb = UNITS[u]
            return (TC, 1) if kind == "mem" else ((tb + 1) * P, 2)

        heads = [(Q2[:, c, :], TX, "g_q_nsa_2", slice(0, TX)) for c in range(4)]
        heads += [(KS, TX, "g_k_slc_2", slice(0, TX)), (KW, TX, "g_k_win_2", slice(0, TX))]
        heads += [(MK[:, c, :], TC, "g_k_mem_2", None) for c in range(2)]
        heads += [(KCMP, NCMP, "g_k_cmp_2", slice(31, TX, 16))]
        heads += [(QM[:, c, :], TX, "g_q_mem_2", None) for c in range(2)]
        step_after = ["k_raw", "v_raw", "ks", "kw", "v", "gate", "mem", "zn", "k_cmp", "zm0", "zm1"]

        def Hs_gate(s, n):
            return rs[:, 0:n] if s == 0 else rs[:, TX:TX + n]

        def g_rows(d):
            return sq if d == 1 else rs

        @block.tensor
        def _(pe):
            w = Worker(pe_step)
            norm_reads = [0]

            def raw(src):
                n = len(direct)
                direct.append([src, None])
                pe.wait_ge(direct_loaded[n % RAWS], 16 * (n // RAWS + 1))
                return DIRECT[n % RAWS]

            def unit(src):
                units.append([src, None, turns[0]])
                turns[0] += 1
                pe.wait_ge(*w.next(pool_ready_pe))
                return units[-1][2] % SPLITS

            def tile(reader, turn=bank_turn):
                n, who, count = turn.pop(0)
                if who:
                    pe.wait_ge(bank_free[who].sem, count)
                tiles[reader].append(n)
                frees[reader] += 1
                turn.append((n, reader, frees[reader]))
                return psum[:, n]

            def norm_step(k, streams, chunks, src=None):
                if k == 0 and norm_reads[0]:
                    pe.wait_ge(act_norm_read.sem, norm_reads[0])
                pe.wait_ge(*w.next(act_ready_pe))
                squares = Hc[:, k, :] if src is None else src
                for i, (c0, n) in enumerate(streams):
                    mm = pe.matmul(psum[:, 6 + i, 0:n], ones, squares[:, c0:c0 + n], start=k == 0, stop=k == chunks - 1)
                    if k == chunks - 1:
                        mm.then_inc(*w.up(pe_norm_sum))
                        norm_reads[0] += 1

            def norm_sum(streams, chunks=KC):
                for k in range(chunks):
                    norm_step(k, streams, chunks)

            def project_split(src, streams, upper, lower, reader, wait_each=None, m=P, order=range(KC)):
                slot = unit(src)
                for i, (c0, n) in enumerate(streams):
                    b = tile(reader)
                    for k in order:
                        if wait_each and i == 0:
                            pe.wait_ge(*w.next(wait_each))
                        up, low = upper(k)[:, c0:c0 + n], lower(k)[:, c0:c0 + n]
                        w_up, w_low = W_R[:, slot, 0, k * P:k * P + m], W_R[:, slot, 1, k * P:k * P + m]
                        pe.matmul(b[0:m, 0:n], w_up, up, start=k == order[0], stop=False)
                        pe.matmul(b[0:m, 0:n], w_up, low, start=False, stop=False)
                        mm = pe.matmul(b[0:m, 0:n], w_low, up, start=False, stop=k == order[-1])
                    mm.then_inc(*w.up(pe_tile_for[reader]))
                units[-1][1] = w.last

            def by_token_split(slot, blocks, upper, lower):
                for tb in blocks:
                    b = tile("act")[:, 0:2 * P].rearrange("p (a e) -> p a e", a=2)
                    for k in range(KC):
                        up, low = upper(k)[:, tb * P:tb * P + P], lower(k)[:, tb * P:tb * P + P]
                        w_up, w_low = (W_R[:, slot:slot + 2, i, k * P:k * P + P] for i in range(2))
                        pe.matmul(b, up, w_up, start=k == 0, stop=False)
                        pe.matmul(b, low, w_up, start=False, stop=False)
                        mm = pe.matmul(b, up, w_low, start=False, stop=k == KC - 1)
                    mm.then_inc(*w.up(pe_tile_for["act"]))
                units[-2][1] = units[-1][1] = w.last

            steps, rows = iter(ADA_STEPS), []

            def ada_step(more=True):
                if rows:
                    pe.wait_ge(*w.next(act_row_ready))
                    pe.matmul(tile("dve")[:, 0:2], adarow[:, rows.pop() % 2, :], const("cond_pick"), start=True,
                              stop=True).then_inc(*w.up(pe_tile_for["dve"]))
                if more:
                    layer, j = next(steps)
                    b = tile("act")
                    first = layer == 0 and j < ADA_START
                    if first:
                        pe.wait_ge(first_loaded[j // 4], 16)
                        wt = FIRST[j // 4][:, :, j % 4 * P:(j % 4 + 1) * P]
                    else:
                        wt = raw(a["w_ada"][layer, :, j * P:j * P + P]).rearrange("p (k n) -> p k n", k=KC)
                    for k in range(KC):
                        g = 32 * (k % 4)
                        mm = pe.matmul(b[g:g + 32, 0:P], cond[:, k, :], wt[:, k, :], start=k < 4, stop=k >= 4)
                    mm.then_inc(*w.up(pe_tile_for["act"]))
                    if not first:
                        direct[-1][1] = w.last
                    rows.append(j)

            def layer_program(layer):
                both = layer < LAYERS - 1
                streams = [X_COLS, C_COLS] if both else [X_COLS]
                all_streams = [X_COLS, C_COLS]
                nb = 6 if both else 4
                w_in = a["w_in"]

                def win(name, m=0):
                    c0 = W_IN_AT[name] + m * P
                    return w_in[layer, :, c0:c0 + P]

                def up(k):
                    return H_HI_R[:, k, :]

                def low(k):
                    return MIX_LO_R[k]

                norm_sum(all_streams)
                if layer == 0:
                    for _ in range(ADA_START):
                        ada_step()
                    ada_step(more=False)
                for m in (2, 0, 3, 1):
                    project_split(win("conv", m), streams, up, low, "act" if m >= 2 else "dve",
                                  dve_ready_pe if m == 2 else None)
                project_split(win("gates"), all_streams, up, low, "dve", m=16)
                for m in range(2):
                    project_split(win("f", m), streams, up, low, "act")
                    if layer == 0:
                        ada_step()
                for name, some in (("k", all_streams), ("q", streams)):
                    for m in range(4):
                        project_split(win(name, m), some, up, low, "dve")
                        if layer == 0:
                            ada_step()
                turns[0] += turns[0] % 2
                slot = unit(win("v", 0))
                unit(win("v", 1))
                by_token_split(slot, range(6), up, low)
                slot = unit(win("v", 2))
                unit(win("v", 3))
                by_token_split(slot, range(4), up, low)
                pe.wait_ge(*w.next(dve_ready_pe))
                b = tile("dve")
                for i in range(6):
                    for d in range(2):
                        for e in range(2):
                            o = ((e * 6 + i) * 2 + d) * 4
                            mm = pe.matmul(b[:, o:o + 4], ROWS[0:4, 2 * d + e, i * P:i * P + P], ident[0:4, 0:4],
                                           start=True, stop=True)
                mm.then_inc(*w.up(pe_tile_for["dve"]))
                pe.wait_ge(*w.next(dve_ready_pe))
                for c0, n in streams:
                    b = tile("dve")
                    for k in range(2):
                        mm = pe.matmul(b[:, 0:n], ones, CV[:, k, c0:c0 + n], start=k == 0, stop=k == 1)
                    mm.then_inc(*w.up(pe_tile_for["dve"]))
                by_token_split(slot, range(4, 6), up, low)
                if norm_reads[0]:
                    pe.wait_ge(act_norm_read.sem, norm_reads[0])
                for k in range(2):
                    pe.wait_ge(*w.next(act_ready_pe))
                    for i, (c0, n) in enumerate(streams):
                        mm = pe.matmul(psum[:, 6 + i, 0:n], ones, M2[:, k, c0:c0 + n], start=k == 0, stop=k == 1)
                        if k == 1:
                            mm.then_inc(*w.up(pe_norm_sum))
                            norm_reads[0] += 1
                pe.wait_ge(*w.next(dve_ready_pe))
                for i in range(nb):
                    b = tile("act")
                    for c in range(2):
                        mm = pe.matmul(b[:, c * 256:c * 256 + 256], FZ[:, c, i * P:i * P + P], const("dft_chan"),
                                       start=True, stop=True)
                    mm.then_inc(*w.up(pe_tile_for["act"]))
                pe.wait_ge(*w.next(act_ready_pe))
                banks = [tile("dve") for _ in range(2)]
                for i in range(4):
                    wt = raw(a["dft_x"][:, i * UNIT:(i + 1) * UNIT])
                    for c in range(2):
                        for cs in range(2):
                            mm = pe.matmul(banks[c][:, 0:TX], FA[:, i, c, cs, :], wt[:, cs * TX:(cs + 1) * TX],
                                           start=i == 0 and cs == 0, stop=i == 3 and cs == 1)
                        mm.then_inc(*w.up(pe_tile_for["dve"] if i == 3 else None))
                    direct[-1][1] = w.last
                if both:
                    wt = raw(a["dft_c"])
                    for c in range(2):
                        b = tile("dve")
                        for i in range(2):
                            for cs in range(2):
                                o = (2 * i + cs) * TC
                                mm = pe.matmul(b[:, 0:TC], FA[:, 4 + i, c, cs, :], wt[:, o:o + TC],
                                               start=i == 0 and cs == 0, stop=i == 1 and cs == 1)
                        mm.then_inc(*w.up(pe_tile_for["dve"]))
                    direct[-1][1] = w.last

                for hd in range(HEADS):
                    for d in range(2):
                        for c0, n in streams:
                            b = tile("act")
                            mm = pe.matmul(b[:, 0:n], const("head_rows")[0:4, hd * P:hd * P + P], GR[0:4, d, c0:c0 + n],
                                           start=True, stop=True)
                            mm.then_inc(*w.up(pe_tile_for["act"]))
                    for s in (4, 5, 0, 1, 2, 3):
                        b = tile("dve")
                        mm = pe.matmul(b[:, 0:TX], K[:, hd, s * P:s * P + P], Q[:, hd, 0:TX], start=True, stop=True)
                        mm.then_inc(*w.up(pe_tile_for["dve"]))
                    if both:
                        b = tile("dve")
                        for j in range(2):
                            mm = pe.matmul(b[:, j * TC:j * TC + TC], K[:, hd, TX + j * P:TX + j * P + P],
                                           Q[:, hd, TX:T], start=True, stop=True)
                        mm.then_inc(*w.up(pe_tile_for["dve"]))
                    project_split(win("o", hd), streams, up, low, "act")
                    marks["h_read", layer] = w.last
                    if layer == 0:
                        ada_step()
                    pe.wait_ge(*w.next(dve_ready_pe))
                    for d in range(2):
                        for g in ((0, 1, 2), (3, 4, 5)) if both else ((0, 1, 2), (3,)):
                            b = tile("dve")
                            for i, tb in enumerate(g):
                                keys = [s for s in (4, 5, 0, 1, 2, 3) if pt_at(d, s, tb) is not None]
                                for n, s in enumerate(keys):
                                    at = pt_at(d, s, tb)
                                    mm = pe.matmul(b[:, i * 129:i * 129 + 129], PT[:, at:at + P], V[:, s, hd, :],
                                                   start=n == 0, stop=n == len(keys) - 1)
                            mm.then_inc(*w.up(pe_tile_for["dve"]))
                    if layer == 0:
                        ada_step()
                for hd in range(HEADS):
                    pe.wait_ge(*w.next(dve_ready_pe))
                    for g in ((0, 1, 2, 3), (4, 5)) if both else ((0, 1, 2, 3),):
                        b = tile("dve")
                        for i, tb in enumerate(g):
                            mm = pe.transpose(b[:, i * P:i * P + P], HS[:, tb, hd, :], ident)
                        mm.then_inc(*w.up(pe_tile_for["dve"]))
                for m in range(KC):
                    project_split(a["w_out"][layer, :, m * P:m * P + P], streams, up, mixed_low, "dve",
                                  dve_ready_pe if m == 0 else None, order=[4, 5, 6, 7, 0, 1, 2, 3])
                    if m >= 2:
                        norm_step(m - 2, streams, KC, OUT_SQ[m - 2])
                    if layer == 0 and m <= ADA_W_OUT:
                        ada_step(more=m < ADA_W_OUT)
                norm_step(6, streams, KC, OUT_SQ[6])
                norm_step(7, streams, KC, OUT_SQ[7])
                norm_sum(streams)
                for q in range(QUARTERS):
                    for m in range(KC):
                        c0 = (q * KC + m) * P
                        project_split(a["w_mlp1"][layer, :, c0:c0 + P], streams, up,
                                      lambda k: MLP_LO_R[k], "act",
                                      dve_ready_pe if q == m == 0 else None)
                        if both:
                            ada_step()
                    for m in range(KC):
                        project_split(a["w_mlp2"][layer, q * D:(q + 1) * D, m * P:m * P + P], streams,
                                      lambda k: HID_HI_R[:, k, :], lambda k: HID_LO_R[:, k, :], "dve",
                                      dve_ready_pe if m == 0 else None)
                        if both and (q < QUARTERS - 1 or m == 0):
                            ada_step(more=q < QUARTERS - 1)
                        if q == QUARTERS - 1 and m >= 2:
                            norm_step(m - 2, streams, KC)
                    marks["hid_read", layer, q] = units[-1][1]
                marks["mlp", layer] = units[-1][1]
                norm_step(6, streams, KC)
                norm_step(7, streams, KC)

            pe.wait_ge(s_first, 48)
            pe.wait_ge(*w.next(act_ready_pe))
            for layer in range(LAYERS):
                layer_program(layer)

            norm_sum([X_COLS])

            def project_last(src, wait_each=None):
                slot = unit(src)
                b = tile("act")
                halves = b[:, :].rearrange("p (a n) -> p a n", a=2)
                for k in range(KC):
                    if wait_each:
                        pe.wait_ge(*w.next(wait_each))
                    w_up, w_low = (W_R[:, slot, i, k * P:(k + 1) * P] for i in range(2))
                    pe.matmul(b, w_up, H_HI_R[:, k, 0:TX], start=k == 0, stop=False)
                    pe.matmul(halves, w_up, LAST_LO_R[k], start=False, stop=False)
                    mm = pe.matmul(b, w_low, H_HI_R[:, k, 0:TX], start=False, stop=k == KC - 1)
                mm.then_inc(*w.up(pe_tile_for["act"]))
                units[-1][1] = w.last

            def by_token_last(slot, slots, width):
                for tb in range(TX // P):
                    b = tile("act")[:, 0:slots * width].rearrange("p (a e) -> p a e", a=slots)
                    for k in range(KC):
                        up = H_HI_R[:, k, tb * P:tb * P + P]
                        low = LAST_LO_R[k][:, tb // 2, tb % 2 * P:(tb % 2 + 1) * P]
                        w_up, w_low = (W_R[:, slot:slot + slots, i, k * P:k * P + width] for i in range(2))
                        pe.matmul(b, up, w_up, start=k == 0, stop=False)
                        pe.matmul(b, low, w_up, start=False, stop=False)
                        mm = pe.matmul(b, up, w_low, start=False, stop=k == KC - 1)
                    mm.then_inc(*w.up(pe_tile_for["act"]))
                for done in units[-slots:]:
                    done[1] = w.last

            def head_step(i):
                if 1 <= i <= len(heads):
                    pe.wait_ge(*w.next(act_head_square))
                    n, at = heads[i - 1][1], (i - 1) % 2 * TX
                    pe.matmul(tile("act")[:, 0:n], ones64, tmp[:, at:at + n], start=True,
                              stop=True).then_inc(*w.up(pe_tile_for["act"]))
                if i >= 2 and heads[i - 2][3]:
                    pe.wait_ge(*w.next(dve_head_ready))
                    z, n = heads[i - 2][0:2]
                    pe.matmul(tile("dve")[:, 0:n], rope_turn, z, start=True,
                              stop=True).then_inc(*w.up(pe_tile_for["dve"]))

            def after(what):
                if what in step_after:
                    head_step(step_after.index(what))

            def win2(name, m=0):
                c0 = W_IN2_AT[name] + m * P
                return a["w_in_2"][0, :, c0:c0 + P]

            for m in range(4):
                project_last(win2("q", m), dve_ready_pe if m == 0 else None)
            for k in range(KC):
                pe.wait_ge(*w.next(act_ready_pe))
                if k == 0:
                    pe.wait_ge(act_norm_read.sem, norm_reads[0])
                mm = pe.matmul(psum[:, 6, 0:TC], ones, MEM_SQ[:, k, :], start=k == 0, stop=k == KC - 1)
            mm.then_inc(*w.up(pe_norm_sum))
            norm_reads[0] += 1
            for name in ("k_raw", "v_raw", "ks", "kw"):
                project_last(win2(name))
                after(name)
            turns[0] += turns[0] % 2
            slot = unit(win2("v", 0))
            unit(win2("v", 1))
            by_token_last(slot, 2, P)
            after("v")
            by_token_last(unit(win2("gate")), 1, 24)
            after("gate")
            pe.wait_ge(*w.next(dve_ready_pe, KC))
            for m in range(4):
                wt = raw(a["w_mem_kv_2"][0][:, m * P:m * P + P])
                b = tile("act")
                if m < 2:
                    for k in range(KC):
                        mm = pe.matmul(b[:, 0:TC], wt[:, k * P:k * P + P], MEM[:, k, :], start=k == 0, stop=k == KC - 1)
                else:
                    for i in range(2):
                        for k in range(KC):
                            mm = pe.matmul(b[:, i * P:i * P + P], MEM[:, k, i * P:i * P + P], wt[:, k * P:k * P + P],
                                           start=k == 0, stop=k == KC - 1)
                mm.then_inc(*w.up(pe_tile_for["act"]))
                direct[-1][1] = w.last
            after("mem")

            def compress(i, quarter):
                win, b = (KWIN, VWIN)[i], psum[:, 7 - i]
                if quarter == 0:
                    pe.wait_ge(*w.next(dve_ready_pe))
                    pe.wait_ge(act_norm_read.sem, norm_reads[0])
                wt = raw(a["w_cmp1"][i][:, quarter * UNIT:(quarter + 1) * UNIT])
                for j in range(KC):
                    place = quarter * KC + j
                    mm = pe.matmul(b[:, 0:NCMP], wt[:, j * P:(j + 1) * P], win[:, :, place], start=place == 0,
                                   stop=place == 31)
                mm.then_inc(*w.up(pe_tile_for["act"] if quarter == 3 else None))
                direct[-1][1] = w.last
                if quarter == 3:
                    tiles["act"].append(7 - i)
                    frees["act"] += 1

            for m in range(4):
                project_last(win2("z", m))
                if m == 0:
                    after("zn")
                compress(0, m)
            for m in range(4):
                project_last(win2("vp", m) if m < 2 else win2("zp", m - 2))
                compress(1, m)
            for m in range(2):
                project_last(win2("qm", m))
            wt = raw(a["w_small"])[:, 0:4 * P].rearrange("p (k n) -> p k n", k=4)
            pe.wait_ge(*w.next(act_ready_pe))
            b = tile("act")
            pe.matmul(b[:, 0:NCMP], wt[:, 0, :], HIDK, start=True, stop=True).then_inc(*w.up(pe_tile_for["act"]))
            b = tile("act")
            for i in range(4):
                mm = pe.matmul(b[32 * i:32 * i + NCMP, 0:P], HIDV, wt[:, 1, :], start=True, stop=True)
            mm.then_inc(*w.up(pe_tile_for["act"]))
            after("k_cmp")
            for m in range(2):
                project_last(win2("zm", m))
                after(f"zm{m}")
            for c in range(2):
                pe.wait_ge(*w.next(dve_ready_pe))
                b = tile("dve")
                pe.matmul(b[:, 0:TX], wt[:, 2 + c, :], VP[:, c, :], start=True,
                          stop=True).then_inc(*w.up(pe_tile_for["dve"]))
            direct[-1][1] = w.last
            for i in range(len(step_after), len(heads) + 2):
                head_step(i)

            pe.wait_ge(act_norm_read.sem, norm_reads[0])
            for _, who, count in bank_turn:
                if who:
                    pe.wait_ge(bank_free[who].sem, count)
            turned_banks, result_banks = [(4, None, 0), (5, None, 0)], [(6, None, 0), (7, None, 0)]

            def scores(u):
                kind, c, g, tb = UNITS[u]
                lo, hi = 64 * g, 64 * g + 64
                n, _ = keys_seen(u)
                if kind == "mem":
                    q, keys = QM[lo:hi, c, tb * P:tb * P + P], [MK[lo:hi, c, :]]
                else:
                    q, keys = Q2[lo:hi, c, tb * P:tb * P + P], [KS[lo:hi, 0:n], KW[lo:hi, 0:n]]
                if u >= 2:
                    pe.wait_ge(*w.next(act_scores_read))
                first = 2 * (u % 2)
                tiles["dve"].append(first)
                for j, k in enumerate(keys):
                    mm = pe.matmul(psum[:, first + j, 0:n], q, k, start=True, stop=True)
                mm.then_inc(*w.up(pe_tile_for["dve"]))

            def turn(u):
                pe.wait_ge(*w.next(dve_ready_pe))
                n, branches = keys_seen(u)
                for j in range(branches):
                    b = tile("act", turn=turned_banks)
                    for i in range(n // P):
                        mm = pe.matmul(b[:, i * P:i * P + P], PROB[:, u % 2, j, i * P:i * P + P], DIAG[:, u % 2, j, :],
                                       start=True, stop=True)
                    mm.then_inc(*w.up(pe_tile_for["act"]))

            def values(u):
                pe.wait_ge(*w.next(act_ready_pe))
                kind, c, g, tb = UNITS[u]
                lo, hi = 64 * g, 64 * g + 64
                if kind == "mem":
                    v = [(MV[:, i, (2 * c + g) * 64:(2 * c + g) * 64 + 64], PROBT[:, u % 2, i, :]) for i in range(2)]
                else:
                    v = [(VCMP[:, tb, lo:hi], CMPT[:, 4 * g + c, :])]
                    v += [(VS[:, i, lo:hi], PROBT[:, u % 2, i, :]) for i in range(tb + 1)]
                    v += [(VW[:, i, lo:hi], PROBT[:, u % 2, 4 + i, :]) for i in range(tb + 1)]
                b = tile("dve", turn=result_banks)
                for i, (vi, probs) in enumerate(v):
                    mm = pe.matmul(b[lo:hi, 0:P], vi, probs, start=i == 0, stop=i == len(v) - 1)
                mm.then_inc(*w.up(pe_tile_for["dve"]))

            pe.wait_ge(*w.next(dve_ready_pe))
            for g in range(2):
                b = tile("dve", turn=result_banks)
                for c in range(4):
                    for tb in range(4):
                        o = 32 * (4 * c + tb)
                        mm = pe.matmul(b[:, o:o + NCMP], Q2[64 * g:64 * g + 64, c, tb * P:tb * P + P],
                                       KCMP[64 * g:64 * g + 64, :], start=True, stop=True)
                mm.then_inc(*w.up(pe_tile_for["dve"]))
            pe.wait_ge(*w.next(dve_ready_pe))
            for g in range(2):
                b = tile("act", turn=turned_banks)
                for c in range(4):
                    mm = pe.transpose(b[:, c * P:c * P + P], CMP[:, g, c, :, :].rearrange("p t n -> p (t n)"), ident)
                mm.then_inc(*w.up(pe_tile_for["act"]))
            for u in range(len(UNITS) + 3):
                if u < len(UNITS):
                    scores(u)
                if 0 <= u - 2 < len(UNITS):
                    turn(u - 2)
                if 0 <= u - 3:
                    values(u - 3)
            pe.wait_ge(dve_y_ready.sem, KC)
            bank_turn[:] = [(b, None, 0) for b in range(8)]
            for m in range(KC):
                project_split(a["w_out_2"][0, :, m * P:m * P + P], [X_COLS], lambda k: Y_HI_R[:, k, :],
                              lambda k: Y_LO_R[:, k, :], "dve", dve_y_lower if m == 0 else None)

        @block.vector
        def _(dve):
            w = Worker(dve_step)
            st = iter(tiles["dve"])

            def tile():
                return psum[:, next(st)]

            def recip_rs(c0, n):
                dve.wait_ge(*w.next(act_ready_dve))
                dve.reciprocal(rs[:, c0:c0 + n], rs[:, c0:c0 + n]).then_inc(*w.up())

            def apply_norm_split(streams, layer, gslot, section, low, low_rounded):
                for c0, n in streams:
                    recip_rs(c0, n)
                dve.wait_ge(*w.own())
                for k in range(KC + 1):
                    if k < KC:
                        for s, (c0, n) in enumerate(streams):
                            ins = dve.scalar_tensor_tensor(out=low[k][:, c0:c0 + n], in0=X[:, k, c0:c0 + n],
                                                           scalar=gsc[:, gslot, k, s:s + 1], in1=rs[:, c0:c0 + n],
                                                           op0=ALU.mult, op1=ALU.mult)
                            ins.then_inc(*w.up(dve_ready_act if s == len(streams) - 1 else None))
                    if k:
                        dve.wait_ge(*w.next(act_ready_dve))
                        for s, (c0, n) in enumerate(streams):
                            ins = dve.scalar_tensor_tensor(out=low_rounded[k - 1][:, c0:c0 + n],
                                                           in0=low[k - 1][:, c0:c0 + n],
                                                           scalar=mod[:, layer, section * 8 + k - 1, s:s + 1],
                                                           in1=H_HI_R[:, k - 1, c0:c0 + n].bitcast(F32),
                                                           op0=ALU.add, op1=ALU.subtract)
                            ins.then_inc(*w.up(dve_ready_pe if s == len(streams) - 1 else None))

            steps, rows = iter(ADA_STEPS), []

            def ada_step(more=True):
                if rows:
                    layer, j = rows.pop()
                    dve.wait_ge(*w.next(pe_tile_for["dve"]))
                    b = tile()
                    dve.tensor_scalar(mod[:, layer, j, :], b[:, 0:2], col("b_ada", j, layer), None,
                                      ALU.add).then_inc(*w.up(dve_bank_free))
                if more:
                    rows.append(next(steps))

            def gains(layer, gslot, name, section, plus_one):
                dve.wait_ge(*w.own())
                for s in range(2):
                    m = mod[:, layer, section * 8:section * 8 + 8, s]
                    dve.scalar_tensor_tensor(out=gsc[:, gslot, :, s], in0=m, scalar=1.0 if plus_one else 0.0,
                                                   in1=col(name, 0, layer, 8), op0=ALU.add, op1=ALU.mult).then_inc(*w.up())
                dve.wait_ge(*w.own())

            def residual(streams, gslot, of_layer=None):
                for c0, n in streams:
                    recip_rs(c0, n)
                dve.wait_ge(*w.own())
                for k in range(KC):
                    for s, (c0, n) in enumerate(streams):
                        dve.scalar_tensor_tensor(out=ACC[:, k, c0:c0 + n], in0=ACC[:, k, c0:c0 + n],
                                                       scalar=gsc[:, gslot, k, s:s + 1], in1=rs[:, c0:c0 + n],
                                                       op0=ALU.mult, op1=ALU.mult).then_inc(*w.up())
                    dve.wait_ge(*w.own())
                    n = sum(q[1] for q in streams)
                    dve.tensor_tensor(X[:, k, 0:n], X[:, k, 0:n], ACC[:, k, 0:n], ALU.add).then_inc(*w.up(dve_ready_act))
                    marks["x", of_layer, k] = w.last

            def layer_program(layer):
                both = layer < LAYERS - 1
                streams = [X_COLS, C_COLS] if both else [X_COLS]
                all_streams = [X_COLS, C_COLS]
                tn = T if both else TX

                if layer == 0:
                    for _ in range(ADA_START):
                        ada_step()
                    ada_step(more=False)
                gains(layer, 0, "g_pre_mix", 1, True)
                dve.wait_ge(s_kept, 64 * (layer + 1))
                apply_norm_split(all_streams, layer, 0, 0, MIX_LO, MIX_LO_R)
                dve.memset(R[:, 17688:17688 + 1656], 0.0).then_inc(*w.up())
                dve.wait_ge(*w.own())
                for m in range(2):
                    for s, (c0, n) in enumerate(streams):
                        u0 = PAD + (0 if s == 0 else TX + 2 * PAD)
                        dve.wait_ge(*w.next(act_ready_dve))
                        dve.wait_ge(*w.next(pe_tile_for["dve"]))
                        b = tile()
                        dve.tensor_tensor(UPAD[:, m, u0:u0 + n], b[:, 0:n], Hs_gate(s, n), ALU.mult).then_inc(*w.up(dve_bank_free))
                        dve.wait_ge(*w.own())
                        dve.wait_ge(*w.own())
                        dve.sem_inc(*w.up(dve_ready_act))
                for c0, n in all_streams:
                    dve.wait_ge(*w.next(pe_tile_for["dve"]))
                    b = tile()
                    dve.tensor_scalar(sq[0:16, c0:c0 + n], b[0:16, 0:n], col("b_gate", 0, layer)[0:16, :], None,
                                      ALU.add).then_inc(*w.up(dve_bank_free))
                dve.wait_ge(*w.own())
                dve.sem_inc(*w.up(dve_ready_sp))

                def taps():
                    for m in range(2):
                        for i in range(CONV_K):
                            tap = col("w_dw", 2 * i + m, layer)
                            dve.wait_ge(*w.own())
                            for s, (c0, n) in enumerate(streams):
                                u0 = 0 if s == 0 else TX + 2 * PAD
                                cv = CV[:, m, c0:c0 + n]
                                u = UPAD[:, m, u0 + i:u0 + i + n]
                                if i == 0:
                                    dve.tensor_scalar(cv, u, tap, col("b_dw", m, layer), ALU.mult,
                                                      ALU.add).then_inc(*w.up())
                                else:
                                    dve.scalar_tensor_tensor(out=cv, in0=u, scalar=tap, in1=cv, op0=ALU.mult,
                                                             op1=ALU.add).then_inc(*w.up())
                            yield

                tap = taps()

                def short_conv(dst, m, j, some):
                    for c0, n in some:
                        dve.wait_ge(*w.next(pe_tile_for["dve"]))
                        b = tile()
                        t = [col("w_qk_conv", 8 * i + j + m, layer) for i in range(3)]
                        dve.tensor_scalar(dst[:, m, c0:c0 + n], b[:, 0:n], t[1], None, ALU.mult).then_inc(*w.up())
                        dve.wait_ge(*w.own())
                        dve.scalar_tensor_tensor(out=dst[:, m, c0 + 1:c0 + n], in0=b[:, 0:n - 1], scalar=t[0],
                                                 in1=dst[:, m, c0 + 1:c0 + n], op0=ALU.mult,
                                                 op1=ALU.add).then_inc(*w.up())
                        dve.wait_ge(*w.own())
                        dve.scalar_tensor_tensor(out=dst[:, m, c0:c0 + n - 1], in0=b[:, 1:n], scalar=t[2],
                                                 in1=dst[:, m, c0:c0 + n - 1], op0=ALU.mult,
                                                 op1=ALU.add).then_inc(*w.up(dve_bank_free))
                    for _ in range(6):
                        next(tap, None)

                dve.memset(V[:, :, :, 128:129], 1.0).then_inc(*w.up())
                if layer == 0:
                    ada_step()
                    ada_step()
                for m in range(4):
                    short_conv(K, m, 4, all_streams)
                    if layer == 0:
                        ada_step()
                dve.wait_ge(*w.next(act_ready_dve))
                for d in range(2):
                    i_row, f_row = ROWS[0:4, 2 * d, :], ROWS[0:4, 2 * d + 1, :]
                    ln = (rs if d == 0 else sq)[0:4, :]
                    dve.wait_ge(*w.own())
                    dve.scalar_tensor_tensor(out=f_row, in0=f_row, scalar=0.0, in1=ln, op0=ALU.min,
                                             op1=ALU.subtract).then_inc(*w.up())
                    dve.wait_ge(*w.own())

                    def scan(dst, src, kind):
                        carry = 0.0
                        for lo, hi in ((TX, T), (0, TX)):
                            o, i = dst[:, lo:hi], src[:, lo:hi]
                            if d == 1:
                                o, i = o[:, ::-1], i[:, ::-1]
                            dve.tensor_tensor_scan(o, i, i, carry, kind, ALU.bypass).then_inc(*w.up())
                            dve.wait_ge(*w.own())
                            carry = dst[:, hi - 1:hi] if d == 0 else dst[:, lo:lo + 1]

                    scan(f_row, f_row, ALU.add)
                    dve.tensor_tensor(i_row, i_row, f_row, ALU.subtract).then_inc(*w.up())
                    dve.wait_ge(*w.own())
                    scan(GR[0:4, d, :], i_row, ALU.max)
                    dve.tensor_tensor(f_row, f_row, GR[0:4, d, :],
                                      ALU.add).then_inc(*w.up(dve_ready_act if d == 1 else None))
                for m in range(4):
                    short_conv(Q, m, 0, streams)
                    if layer == 0:
                        ada_step()
                dve.wait_ge(*w.own())
                dve.wait_ge(*w.next(act_ready_dve))
                dve.sem_inc(*w.up(dve_ready_pe))
                for _ in tap:
                    pass
                dve.wait_ge(*w.next(pe_tile_for["dve"]))
                b = tile()
                dve.tensor_copy(acol[:, :], b[:, 0:96]).then_inc(*w.up(dve_bank_free))
                dve.wait_ge(*w.own())
                dve.sem_inc(*w.up(dve_ready_pe))
                for c0, n in streams:
                    dve.wait_ge(*w.next(pe_tile_for["dve"]))
                    b = tile()
                    for k in range(2):
                        cv = CV[:, k, c0:c0 + n]
                        ins = dve.scalar_tensor_tensor(out=cv, in0=b[:, 0:n], scalar=-1.0 / 256, in1=cv, op0=ALU.mult,
                                                       op1=ALU.add)
                        if k == 0:
                            ins.then_inc(*w.up())
                    ins.then_inc(*w.up(dve_bank_free))
                dve.wait_ge(*w.own())
                dve.sem_inc(*w.up(dve_ready_act))
                for c0, n in streams:
                    recip_rs(c0, n)
                dve.wait_ge(*w.own())
                for k in range(2):
                    dve.tensor_tensor(M2[:, 2 + k, 0:tn], CV[:, k, 0:tn], rs[:, 0:tn],
                                      ALU.mult).then_inc(*w.up(dve_ready_act))
                dve.wait_ge(*w.own())
                dve.sem_inc(*w.up(dve_ready_pe))
                for c0, n in streams:
                    for c in range(2):
                        dve.wait_ge(*w.next(pe_tile_for["dve"]))
                        b = tile()
                        dve.tensor_copy(M2[:, c, c0:c0 + n], b[:, 0:n]).then_inc(*w.up(dve_bank_free))

                en = acol[:, 48:96].rearrange("p (i d h) -> p i d h", i=6, d=2)
                av = acol[:, 0:48].rearrange("p (i d h) -> p i d h", i=6, d=2)
                blocks = pt_blocks(both)
                nb = 6 if both else 4
                for hd in range(HEADS):
                    dve.wait_ge(*w.next(act_ready_dve, 2 * len(streams)))
                    for s, d, lo, hi, t0, at in blocks:
                        if t0 == 0 and s >= 4:
                            continue
                        wv = PT[:, at:at + hi - lo]
                        dve.tensor_scalar(wv, g_rows(d)[:, t0 + lo:t0 + hi], av[:, s, d, hd:hd + 1], 0.0, ALU.subtract,
                                          ALU.max).then_inc(*w.up())
                        dve.wait_ge(*w.own())
                        o = 0 if d == 0 else hi - lo - P
                        hide = const("hide_t_lt_s" if d == 0 else "hide_t_gt_s")
                        dve.tensor_tensor(wv[:, o:o + P], wv[:, o:o + P], hide,
                                          ALU.add).then_inc(*w.up(dve_ready_act))
                    for s, d, lo, hi, t0, at in blocks:
                        new = t0 == 0 and d == 0 or t0 and (s, d) == (4, 0)
                        last = t0 == 0 and d == 1 or t0 and (s, d) == (5, 1)
                        if new:
                            dve.wait_ge(*w.next(pe_tile_for["dve"]))
                            b = tile()
                        dve.wait_ge(*w.next(act_ready_dve))
                        wv = PT[:, at:at + hi - lo]
                        c0 = (s - 4) * TC if t0 else 0
                        ins = dve.scalar_tensor_tensor(out=wv, in0=b[:, c0 + lo:c0 + hi], scalar=HD ** -0.5, in1=wv,
                                                       op0=ALU.mult, op1=ALU.mult)
                        ins.then_inc(*w.up(dve_bank_free if last else None))
                    dve.wait_ge(*w.own())
                    dve.sem_inc(*w.up(dve_ready_pe))
                    if layer == 0:
                        ada_step()
                    for d in range(2):
                        for g in ((0, 1, 2), (3, 4, 5)) if both else ((0, 1, 2), (3,)):
                            dve.wait_ge(*w.next(pe_tile_for["dve"]))
                            b = tile()
                            ng = len(g)
                            bv = b[:, 0:ng * 129].rearrange("p (i e) -> p i e", e=129)
                            den = small[:, 4 * (2 * d + g[0] // 3):4 * (2 * d + g[0] // 3) + ng]
                            dve.tensor_tensor(den, bv[:, :, 128], en[:, g[0]:g[0] + ng, d, hd],
                                              ALU.max).then_inc(*w.up())
                            dve.wait_ge(*w.own())
                            dve.scalar_tensor_tensor(out=den, in0=bv[:, :, 128], scalar=-1.0, in1=den,
                                                     op0=ALU.mult, op1=ALU.max).then_inc(*w.up())
                            dve.wait_ge(*w.own())
                            dve.reciprocal(den, den).then_inc(*w.up())
                            dve.wait_ge(*w.own())
                            for i, tb in enumerate(g):
                                if d == 0:
                                    ins = dve.tensor_scalar(HS[:, tb, hd, :], bv[:, i, 0:128], den[:, i:i + 1], None,
                                                            ALU.mult)
                                else:
                                    ins = dve.scalar_tensor_tensor(out=HS[:, tb, hd, :], in0=bv[:, i, 0:128],
                                                                   scalar=den[:, i:i + 1], in1=HS[:, tb, hd, :],
                                                                   op0=ALU.mult, op1=ALU.add)
                                if i < ng - 1:
                                    ins.then_inc(*w.up())
                            ins.then_inc(*w.up(dve_bank_free))
                    dve.wait_ge(*w.own())
                    dve.sem_inc(*w.up(dve_ready_act))
                    if layer == 0:
                        ada_step()
                    for tb in range(nb):
                        dve.bn_stats(small[:, 16 + 6 * tb:22 + 6 * tb], HS[:, tb, hd, :]).then_inc(*w.up())
                    dve.wait_ge(*w.own())
                    for tb in range(nb):
                        i = 2 * (tb * 4 + hd)
                        dve.bn_aggr(acol2[:, i:i + 2], small[:, 16 + 6 * tb:22 + 6 * tb]).then_inc(*w.up())
                dve.wait_ge(*w.own())
                dve.sem_inc(*w.up(dve_ready_act))
                dve.wait_ge(*w.next(act_ready_dve))
                root = acol2[:, 48:48 + nb * 4]
                dve.reciprocal(root, root).then_inc(*w.up())
                dve.wait_ge(*w.own())
                for hd in range(HEADS):
                    for tb in range(nb):
                        i = tb * 4 + hd
                        dve.tensor_scalar(HS[:, tb, hd, :], HS[:, tb, hd, :], acol2[:, 2 * i:2 * i + 1],
                                          acol2[:, 48 + i:49 + i], ALU.subtract, ALU.mult).then_inc(*w.up())
                    dve.wait_ge(*w.own())
                    dve.sem_inc(*w.up(dve_ready_pe))
                dve.wait_ge(*w.next(act_ready_dve))

                def lower(k):
                    dve.wait_ge(*w.next(act_ready_dve))
                    dve.tensor_tensor(mixed_low(k)[:, 0:tn], mixed(k)[:, 0:tn], H_HI_R[:, k, 0:tn].bitcast(F32),
                                      ALU.subtract).then_inc(*w.up(dve_ready_pe))

                for k in range(4, KC):
                    lower(k)
                for hd in range(HEADS + 1):
                    if hd < HEADS:
                        for s, (c0, n) in enumerate(streams):
                            dve.wait_ge(*w.next(pe_tile_for["dve"]))
                            b = tile()
                            dve.scalar_tensor_tensor(out=mixed(hd)[:, c0:c0 + n], in0=b[:, 0:n],
                                                     scalar=col("g_mlstm_norm", hd, layer), in1=O[:, hd, c0:c0 + n],
                                                     op0=ALU.mult, op1=ALU.mult).then_inc(*w.up(dve_bank_free))
                        dve.wait_ge(*w.own())
                        dve.sem_inc(*w.up(dve_ready_act))
                    if hd:
                        lower(hd - 1)
                for k in range(KC):
                    for c0, n in streams:
                        dve.wait_ge(*w.next(pe_tile_for["dve"]))
                        b = tile()
                        dve.tensor_copy(ACC[:, k, c0:c0 + n], b[:, 0:n]).then_inc(*w.up(dve_bank_free))
                    marks["acc", layer, 0, k] = w.last
                    if layer == 0 and k <= ADA_W_OUT:
                        ada_step(more=k < ADA_W_OUT)
                gains(layer, 1, "g_post_mix", 2, False)
                gains(layer, 2, "g_pre_mlp", 4, True)
                dve.wait_ge(s_back, 16 * (layer + 1))
                residual(streams, 1)
                apply_norm_split(streams, layer, 2, 3, MLP_LO, MLP_LO_R)
                for q in range(QUARTERS):
                    for k in range(KC):
                        hi, low = HID_HI_R[:, k, 0:tn], HID_LO[:, k, 0:tn]
                        dve.wait_ge(*w.next(act_ready_dve))
                        dve.tensor_tensor(low, low, low, ALU.mult).then_inc(*w.up())
                        dve.wait_ge(*w.own())
                        dve.tensor_copy(hi, low).then_inc(*w.up())
                        dve.wait_ge(*w.own())
                        dve.tensor_tensor(HID_LO_R[:, k, 0:tn], low, hi.bitcast(F32),
                                          ALU.subtract).then_inc(*w.up(dve_ready_pe))
                        if both:
                            ada_step()
                    for k in range(KC):
                        for c0, n in streams:
                            dve.wait_ge(*w.next(pe_tile_for["dve"]))
                            b = tile()
                            acc = ACC[:, k, c0:c0 + n]
                            if q == 0:
                                dve.tensor_copy(acc, b[:, 0:n]).then_inc(*w.up(dve_bank_free))
                            else:
                                dve.tensor_tensor(acc, b[:, 0:n], acc, ALU.add).then_inc(*w.up(dve_bank_free))
                        marks["acc", layer, 1, k] = w.last
                        if both and (q < QUARTERS - 1 or k == 0):
                            ada_step(more=q < QUARTERS - 1)
                gains(layer, 3, "g_post_mlp", 5, False)
                residual(streams, 3, layer + 1)

            dve.wait_ge(s_first, 48)
            dve.memset(small[:, :], 0.0).then_inc(*w.up())
            dve.wait_ge(*w.own())
            dve.wait_ge(s_x, 32)
            dve.wait_ge(s_pos, 32)
            shape = [P, TX // GRID, GRID]
            for k in range(KC):
                if k < KC // 2:
                    table = GRID_ROWS[:, k, :].unsqueeze(2).to_broadcast(shape)
                else:
                    table = GRID_COLS[:, k - KC // 2, :].unsqueeze(1).to_broadcast(shape)
                x = X[:, k, 0:TX].rearrange("p (r c) -> p r c", c=GRID)
                dve.tensor_tensor(x, x, table, ALU.add).then_inc(*w.up())
            dve.wait_ge(*w.own())
            dve.sem_inc(*w.up(dve_ready_act))
            for k in range(KC):
                marks["x", 0, k] = w.last
            for layer in range(LAYERS):
                layer_program(layer)
            dve.wait_ge(*w.own())
            dve.sem_inc(*w.up(dve_ready_sp))
            recip_rs(*X_COLS)
            dve.wait_ge(*w.own())
            halves = (slice(0, TX // 2), slice(TX // 2, TX))
            for k in range(KC + 1):
                if k < KC:
                    for i, half in enumerate(halves):
                        dve.scalar_tensor_tensor(out=LAST_LO[k][i], in0=X[:, k, half], scalar=col("g_norm_2", k),
                                                 in1=rs[:, half], op0=ALU.mult,
                                                 op1=ALU.mult).then_inc(*w.up(dve_ready_act if i else None))
                if k:
                    dve.wait_ge(*w.next(act_ready_dve))
                    for i, half in enumerate(halves):
                        dve.tensor_tensor(LAST_LO_R[k - 1][:, i, :], LAST_LO[k - 1][i],
                                          H_HI_R[:, k - 1, half].bitcast(F32),
                                          ALU.subtract).then_inc(*w.up(dve_ready_pe if i else None))
            dve.wait_ge(s_tok, 16)
            kk = POOLT[:, 0, :]
            dve.tensor_scalar(SIN, COS.bitcast(I32), const("rope_freq"), None, ALU.mult).then_inc(*w.up())
            dve.wait_ge(*w.own())
            dve.tensor_scalar(kk, SIN, 1.0 / TWO_PI, ROUND, ALU.mult, ALU.add).then_inc(*w.up())
            dve.wait_ge(*w.own())
            dve.tensor_scalar(kk, kk, ROUND, None, ALU.subtract).then_inc(*w.up())
            for c in TWO_PI_PARTS:
                dve.wait_ge(*w.own())
                dve.scalar_tensor_tensor(out=SIN, in0=kk, scalar=-c, in1=SIN, op0=ALU.mult, op1=ALU.add).then_inc(*w.up())
            dve.wait_ge(*w.own())
            dve.tensor_scalar(SIN, SIN, PI_BELOW, -PI_BELOW, ALU.min, ALU.max).then_inc(*w.up(dve_ready_act))
            recip_rs(TX, TC)
            dve.wait_ge(*w.own())
            for k in range(KC):
                dve.scalar_tensor_tensor(out=MEM[:, k, :], in0=MEM[:, k, :], scalar=col("g_mem_2", k),
                                               in1=rs[:, TX:T], op0=ALU.mult, op1=ALU.mult).then_inc(*w.up(dve_ready_pe))
            dve.wait_ge(*w.next(act_ready_dve))
            dve.tensor_tensor(COS, COS, COS, ALU.mult).then_inc(*w.up())
            dve.wait_ge(*w.own())
            dve.tensor_scalar(COS, COS, -2.0, 1.0, ALU.mult, ALU.add).then_inc(*w.up())

            def head_step(i):
                if 1 <= i <= len(heads):
                    z, n, gain, rotary = heads[i - 1]
                    root = (rs, sq)[(i - 1) % 2][:, 0:n]
                    dve.wait_ge(*w.next(act_ready_dve))
                    dve.reciprocal(root, root).then_inc(*w.up())
                    dve.wait_ge(*w.own())
                    dve.scalar_tensor_tensor(out=z, in0=z, scalar=col(gain), in1=root, op0=ALU.mult,
                                             op1=ALU.mult).then_inc(*w.up())
                    dve.wait_ge(*w.own())
                    dve.sem_inc(*w.up(dve_ready_act))
                    if rotary:
                        dve.sem_inc(*w.up(dve_head_ready))
                if i >= 2 and heads[i - 2][3]:
                    z, n, _, sl = heads[i - 2]
                    dve.wait_ge(*w.next(pe_tile_for["dve"]))
                    b = tile()
                    t0, t1 = POOLT[:, 0, 0:n], POOLT[:, 1, 0:n]
                    dve.tensor_tensor(t0, z, COS[:, sl], ALU.mult).then_inc(*w.up())
                    dve.tensor_tensor(t1, b[:, 0:n], SIN[:, sl], ALU.mult).then_inc(*w.up(dve_bank_free))
                    dve.wait_ge(*w.own())
                    dve.tensor_tensor(z, t0, t1, ALU.add).then_inc(*w.up())

            head_step(0)
            head_step(1)
            dve.wait_ge(*w.next(act_ready_dve))
            for raw, win, pos in ((KRAW, KWIN, "cmp_pos_k_2"), (VRAW, VWIN, "cmp_pos_v_2")):
                for part_ in range(2):
                    src = raw[:, 16 * part_:16 * part_ + 16 * NCMP].rearrange("p (n j) -> p n j", j=16)
                    dve.tensor_tensor(win[:, :, 16 * part_:16 * part_ + 16], src,
                                            col(pos, 16 * part_, n=16).unsqueeze(1).to_broadcast([P, NCMP, 16]),
                                            ALU.add).then_inc(*w.up())
                dve.wait_ge(*w.own())
                dve.sem_inc(*w.up(dve_ready_pe))
            for i in range(2, 8):
                head_step(i)
            dve.wait_ge(*w.next(act_ready_dve))
            for c in range(2):
                cur, lo = VP[:, c, :], 0
                where = {0: cur}
                for i, sh in enumerate((1, 2) if c == 0 else (1, 2, 4, 8)):
                    if sh == (2, 8)[c]:
                        where[0], lo = cur, 64
                    nxt = POOLT[:, i % 2, :]
                    dve.wait_ge(*w.own())
                    dve.tensor_tensor(nxt[lo:, sh:TX], cur[lo:, sh:TX], cur[lo:, 0:TX - sh], ALU.add).then_inc(*w.up())
                    dve.tensor_copy(nxt[lo:, 0:sh], cur[lo:, 0:sh]).then_inc(*w.up())
                    cur = nxt
                for lo, res in ((0, where[0]), (64, cur)):
                    r = res[lo:lo + 64, :]
                    dve.wait_ge(*w.own())
                    dve.tensor_tensor(r[:, 0:16], r[:, 0:16], const("pool_first")[lo:lo + 64, 16 * c:16 * c + 16],
                                            ALU.mult).then_inc(*w.up())
                    dve.wait_ge(*w.own())
                    vp = VP[lo:lo + 64, c, :]
                    dve.scalar_tensor_tensor(out=vp, in0=r, scalar=const("pool_inv")[lo:lo + 64, c:c + 1],
                                                   in1=vp, op0=ALU.mult, op1=ALU.subtract).then_inc(*w.up())
                dve.wait_ge(*w.own())
                dve.sem_inc(*w.up(dve_ready_pe))
            for i in range(8, len(step_after)):
                head_step(i)
            for c in range(2):
                dve.wait_ge(*w.next(pe_tile_for["dve"]))
                b = tile()
                dve.scalar_tensor_tensor(out=Y[:, 4 + c, :], in0=b[:, 0:TX], scalar=col("pool_scale_2", c),
                                              in1=ZP[:, c, :], op0=ALU.mult, op1=ALU.mult).then_inc(*w.up(dve_bank_free))
            for i in range(len(step_after), len(heads) + 2):
                head_step(i)
            dve.wait_ge(*w.own())
            dve.sem_inc(*w.up(dve_ready_pe))

            total = small[:, 64:96].rearrange("p (g c t) -> p g c t", g=2, c=4)
            gates = GATE.rearrange("p t (g c j) -> p g c t j", g=2, c=4)
            hidden = const("cmp_hide")[:, 0:4 * NCMP].rearrange("p (t n) -> p t n", t=4)
            dve.memset(CMP.rearrange("p g c t n -> p (g c t n)"), 0.0).then_inc(*w.up())
            dve.wait_ge(*w.own())
            for g in range(2):
                dve.wait_ge(*w.next(pe_tile_for["dve"]))
                b = tile().rearrange("p (c t n) -> p c t n", c=4, t=4)
                for c in range(4):
                    ins = dve.tensor_tensor(CMP[:, g, c, :, 0:NCMP], b[:, c, :, 0:NCMP], hidden, ALU.add)
                    if c < 3:
                        ins.then_inc(*w.up())
                ins.then_inc(*w.up(dve_bank_free))
            seen = CMP.rearrange("p g c t n -> p (g c t) n")[:, :, 0:NCMP]
            dve.wait_ge(*w.own())
            dve.tensor_reduce(small[:, 32:64], seen, AXX, ALU.max).then_inc(*w.up())
            dve.wait_ge(*w.own())
            dve.tensor_scalar(small[:, 32:64], small[:, 32:64], -BIG / 10, None, ALU.max).then_inc(*w.up())
            dve.wait_ge(*w.own())
            dve.tensor_tensor(seen, seen, small[:, 32:64].unsqueeze(2).to_broadcast([P, 32, NCMP]),
                              ALU.subtract).then_inc(*w.up(dve_ready_act))
            dve.wait_ge(*w.next(act_ready_dve))
            dve.tensor_reduce(small[:, 64:96], seen, AXX, ALU.add).then_inc(*w.up())
            dve.wait_ge(*w.own())
            dve.tensor_scalar(small[:, 64:96], small[:, 64:96], TINY, None, ALU.max).then_inc(*w.up())
            dve.wait_ge(*w.own())
            dve.reciprocal(small[:, 64:96], small[:, 64:96]).then_inc(*w.up())
            dve.wait_ge(*w.own())
            for g in range(2):
                dve.tensor_tensor(total[:, g], total[:, g], gates[:, g, :, :, 0], ALU.mult).then_inc(*w.up())
            dve.wait_ge(*w.own())
            dve.tensor_tensor(seen, seen, small[:, 64:96].unsqueeze(2).to_broadcast([P, 32, NCMP]),
                              ALU.mult).then_inc(*w.up(dve_ready_pe))

            def y_lower(k):
                dve.wait_ge(*w.next(act_y_upper))
                dve.tensor_tensor(Y_LO_R[:, k, :], Y[:, k, :], Y_HI_R[:, k, :].bitcast(F32),
                                  ALU.subtract).then_inc(*w.up(dve_y_lower))

            def highest(u):
                n, branches = keys_seen(u)
                o = 16 * (u % 2)
                dve.wait_ge(*w.next(pe_tile_for["dve"]))
                first = next(st)
                if branches == 2:
                    for j in range(2):
                        b = psum[:, first + j, n - P:n]
                        dve.tensor_tensor(b, b, const("hide_s_gt_t"), ALU.add).then_inc(*w.up())
                    dve.wait_ge(*w.own())
                dve.tensor_reduce(small[:, o:o + branches], psum[:, first:first + branches, 0:n], AXX,
                                  ALU.max).then_inc(*w.up())
                dve.wait_ge(*w.own())
                dve.tensor_scalar(small[:, o + 4:o + 4 + branches], small[:, o:o + branches], -SCALE, None,
                                  ALU.mult).then_inc(*w.up(dve_ready_act))

            def over_sums(u):
                kind, c, g, tb = UNITS[u]
                n, branches = keys_seen(u)
                o = 16 * (u % 2) + 8
                dve.wait_ge(*w.next(act_ready_dve))
                den = small[:, o:o + branches]
                dve.reciprocal(den, den).then_inc(*w.up())
                dve.wait_ge(*w.own())
                if kind == "nsa":
                    hd = 4 * g + c
                    dve.tensor_tensor(den, den, GATE[:, tb, 3 * hd + 1:3 * hd + 3], ALU.mult).then_inc(*w.up())
                    dve.wait_ge(*w.own())
                for j in range(branches):
                    dve.tensor_scalar(DIAG[:, u % 2, j, :], ident, den[:, j:j + 1], None,
                                      ALU.mult).then_inc(*w.up(dve_ready_pe if j == branches - 1 else None))

            def gated(u):
                kind, c, g, tb = UNITS[u]
                lo, hi = 64 * g, 64 * g + 64
                z, k = (ZN, c) if kind == "nsa" else (ZM, 6 + c)
                dve.wait_ge(*w.next(pe_tile_for["dve"]))
                b = tile()
                dve.tensor_tensor(Y[lo:hi, k, tb * P:tb * P + P], b[lo:hi, 0:P], z[lo:hi, c, tb * P:tb * P + P],
                                       ALU.mult).then_inc(*w.up(dve_bank_free))

            for u in range(len(UNITS) + 3):
                if u < len(UNITS):
                    highest(u)
                if 0 <= u - 1 < len(UNITS):
                    over_sums(u - 1)
                if 0 <= u - 3:
                    gated(u - 3)
                if u in SPLIT_AT:
                    dve.wait_ge(*w.own())
                    dve.sem_inc(*w.up(dve_y_ready))
                if u - 2 in SPLIT_AT:
                    y_lower(SPLIT_AT[u - 2])
            dve.wait_ge(*w.own())
            dve.sem_inc(*w.up(dve_y_ready))
            y_lower(KC - 1)
            for k in range(KC):
                dve.wait_ge(*w.next(pe_tile_for["dve"]))
                b = tile()
                dve.tensor_tensor(X[:, k, 0:TX], b[:, 0:TX], X[:, k, 0:TX], ALU.add).then_inc(*w.up(dve_bank_free))
            dve.wait_ge(*w.own())
            dve.sem_inc(*w.up(dve_ready_sp))

        @block.scalar
        def _(act):
            w = Worker(act_step)
            st = iter(tiles["act"])

            def tile():
                return psum[:, next(st)]

            def squares(src, streams, each=False, rounding=False):
                n = sum(q[1] for q in streams)
                for k in range(KC):
                    if each:
                        act.wait_ge(*w.next(dve_ready_act))
                    act.activation(Hc[:, k, 0:n], src[:, k, 0:n], ACT.Square).then_inc(*w.up(act_ready_pe))
                    if rounding and k < SPLITS:
                        round_unit()

            def square_of_product(layer, which, streams, k):
                n = sum(q[1] for q in streams)
                dst = (OUT_SQ[k] if which == 0 else Hc[:, k, :])[:, 0:n]
                act.wait_ge(*marks["acc", layer, which, k])
                act.activation(dst, ACC[:, k, 0:n], ACT.Square).then_inc(*w.up(act_ready_pe))

            def roots(streams, count):
                for i, (c0, n) in enumerate(streams):
                    act.wait_ge(*w.next(pe_norm_sum))
                    act.activation(rs[:, c0:c0 + n], psum[:, 6 + i, 0:n], ACT.Sqrt, scale=1.0 / count,
                                   bias=eps).then_inc(*w.up(act_norm_read))
                    act.wait_ge(*w.own())
                    act.sem_inc(*w.up(act_ready_dve))

            steps = iter(ADA_STEPS)

            def ada_step():
                layer, j = next(steps)
                if layer or j >= ADA_START:
                    loads.append(("direct", next(direct_turns)))
                act.wait_ge(*w.next(pe_tile_for["act"]))
                b = tile()
                act.copy(adarow[:, j % 2, :], b[:, 0:P]).then_inc(*w.up(act_bank_free))
                act.wait_ge(*w.own())
                act.sem_inc(*w.up(act_row_ready))

            def uppers(streams, layer, section, low):
                for k in range(KC):
                    if layer == section == 0 and 1 <= k < SPLITS:
                        round_unit()
                    act.wait_ge(*w.next(dve_ready_act))
                    for s, (c0, n) in enumerate(streams):
                        m = mod[:, layer, section * 8 + k, s:s + 1]
                        ins = act.activation(H_HI_R[:, k, c0:c0 + n], low[k][:, c0:c0 + n], ACT.Identity, bias=m)
                        ins.then_inc(*w.up(act_ready_dve if s == len(streams) - 1 else None))

            held = {}
            rounded_units = iter(range(len(units)))
            direct_turns = iter(range(len(direct)))

            def round_unit():
                n = next(rounded_units)
                loads.append(("whole", n))
                slot = units[n][2] % SPLITS
                act.wait_ge(whole_loaded[n % RAWS], 16 * (n // RAWS + 1))
                if slot in held:
                    act.wait_ge(*units[held[slot]][1])
                held[slot] = n
                act.copy(W_R[:, slot, 0, :], WHOLE[n % RAWS]).then_inc(*w.up(act_ready_pool))

            def layer_program(layer):
                both = layer < LAYERS - 1
                streams = [X_COLS, C_COLS] if both else [X_COLS]
                all_streams = [X_COLS, C_COLS]
                tn = T if both else TX
                squares(X, all_streams, each=layer > 0, rounding=layer > 0)
                if layer:
                    loads.append(("keep", layer))
                roots(all_streams, D)
                if layer == 0:
                    for _ in range(ADA_START):
                        ada_step()
                    round_unit()
                uppers(all_streams, layer, 0, MIX_LO)
                for m in range(2):
                    for s, (c0, n) in enumerate(streams):
                        if m:
                            act.wait_ge(*w.next(dve_ready_act))
                        act.wait_ge(*w.next(pe_tile_for["act"]))
                        b = tile()
                        act.activation(Hs_gate(s, n), b[:, 0:n], ACT.Sigmoid).then_inc(*w.up(act_bank_free))
                        act.wait_ge(*w.own())
                        act.sem_inc(*w.up(act_ready_dve))
                    round_unit()
                    round_unit()
                act.wait_ge(*w.next(dve_ready_act, len(streams)))
                round_unit()
                for m in range(2):
                    for c0, n in streams:
                        act.wait_ge(*w.next(pe_tile_for["act"]))
                        b = tile()
                        act.copy(FZ[:, m, c0:c0 + n], b[:, 0:n]).then_inc(*w.up(act_bank_free))
                    round_unit()
                    if layer == 0:
                        ada_step()
                loads.append(("rows", layer))
                act.wait_ge(s_rows, 64 * (layer + 1))
                for d in range(2):
                    t = (rs if d == 0 else sq)[0:4, :]
                    act.activation(t, ROWS[0:4, 2 * d + 1, :], ACT.Abs).then_inc(*w.up())
                    act.wait_ge(*w.own())
                    act.activation(t, t, ACT.Exp, scale=-1.0).then_inc(*w.up())
                    act.wait_ge(*w.own())
                    act.activation(t, t, ACT.Ln, bias=1.0).then_inc(*w.up(act_ready_dve if d == 1 else None))
                for _ in range(4):
                    round_unit()
                    if layer == 0:
                        ada_step()
                act.wait_ge(*w.next(dve_ready_act))
                act.activation(ROWS[0:4, 1:4:2, :], ROWS[0:4, 1:4:2, :], ACT.Exp,
                               scale=-1.0).then_inc(*w.up(act_ready_dve))

                for _ in range(4):
                    round_unit()
                    if layer == 0:
                        ada_step()
                for i in range(2):
                    for tb in range(6):
                        act.wait_ge(*w.next(pe_tile_for["act"]))
                        b = tile()
                        act.copy(V[:, tb, 2 * i:2 * i + 2, 0:128],
                                 b[:, 0:256].rearrange("p (h e) -> p h e", h=2)).then_inc(*w.up(act_bank_free))
                act.wait_ge(*w.next(dve_ready_act))
                for k in range(2):
                    act.activation(M2[:, k, 0:tn], CV[:, k, 0:tn], ACT.Square).then_inc(*w.up(act_ready_pe))
                roots(streams, 256)
                for k in range(2):
                    act.wait_ge(*w.next(dve_ready_act))
                    act.activation(M2[:, 2 + k, 0:tn], M2[:, 2 + k, 0:tn], ACT.Silu,
                                   scale=col("g_conv_ln", k, layer), bias=col("b_conv_ln", k, layer)).then_inc(*w.up())

                def gate_chunk(m):
                    for c0, n in streams:
                        act.wait_ge(*w.next(pe_tile_for["act"]))
                        b = tile()
                        act.copy(O[:, m, c0:c0 + n], b[:, 0:n]).then_inc(*w.up(act_bank_free))

                loads.extend(("direct", next(direct_turns)) for _ in range(5 if both else 4))
                for i in range(6 if both else 4):
                    act.wait_ge(*w.next(pe_tile_for["act"]))
                    b = tile()
                    act.copy(FA[:, i], b[:, 0:512].rearrange("p (c s e) -> p c s e", c=2,
                                                             s=2)).then_inc(*w.up(act_bank_free))
                act.wait_ge(*w.own())
                act.sem_inc(*w.up(act_ready_pe))
                round_unit()
                av = acol[:, 0:48].rearrange("p (i d h) -> p i d h", i=6, d=2)
                for hd in range(HEADS):
                    if hd:
                        act.wait_ge(*w.next(dve_ready_act))
                    for d in range(2):
                        for c0, n in streams:
                            act.wait_ge(*w.next(pe_tile_for["act"]))
                            b = tile()
                            act.copy(g_rows(d)[:, c0:c0 + n], b[:, 0:n]).then_inc(*w.up(act_bank_free))
                            act.wait_ge(*w.own())
                            act.sem_inc(*w.up(act_ready_dve))
                    for s, d, lo, hi, t0, at in pt_blocks(both):
                        wv = PT[:, at:at + hi - lo]
                        if t0 == 0 and s >= 4:
                            act.activation(wv, g_rows(d)[:, lo:hi], ACT.Exp, scale=-1.0,
                                           bias=av[:, s, d, hd:hd + 1]).then_inc(*w.up(act_ready_dve))
                        else:
                            act.wait_ge(*w.next(dve_ready_act))
                            act.activation(wv, wv, ACT.Exp, scale=-1.0).then_inc(*w.up(act_ready_dve))
                    gate_chunk(hd)
                    if layer == 0:
                        ada_step()
                        ada_step()
                    if hd < HEADS - 1:
                        round_unit()
                act.wait_ge(*w.own())
                act.activation(O[:, :, 0:tn], O[:, :, 0:tn], ACT.Sigmoid).then_inc(*w.up())
                act.wait_ge(*w.next(dve_ready_act))
                act.wait_ge(*w.next(dve_ready_act))
                nb = 6 if both else 4
                act.activation(acol2[:, 48:48 + nb * 4], acol2[:, 0:nb * 8].rearrange("p (i t) -> p i t", t=2)[:, :, 1],
                               ACT.Sqrt, bias=eps).then_inc(*w.up(act_ready_dve))
                act.wait_ge(*w.own())
                act.sem_inc(*w.up(act_ready_dve))
                for k in range(4, KC):
                    act.copy(H_HI_R[:, k, 0:tn], mixed(k)[:, 0:tn]).then_inc(*w.up(act_ready_dve))
                loads.append(("back", layer))
                for _ in range(SPLITS):
                    round_unit()
                for hd in range(HEADS):
                    act.wait_ge(*w.next(dve_ready_act))
                    act.copy(H_HI_R[:, hd, 0:tn], mixed(hd)[:, 0:tn]).then_inc(*w.up(act_ready_dve))
                for k in range(KC):
                    round_unit()
                    square_of_product(layer, 0, streams, k)
                    if layer == 0 and k < ADA_W_OUT:
                        ada_step()
                roots(streams, D)
                squares(X, streams, each=True)
                roots(streams, D)
                uppers(streams, layer, 3, MLP_LO)
                for q in range(QUARTERS):
                    if q:
                        act.wait_ge(*marks["hid_read", layer, q - 1])
                    for k in range(2 * KC):
                        if k < KC:
                            for c0, cn in streams:
                                act.wait_ge(*w.next(pe_tile_for["act"]))
                                b = tile()
                                act.activation(HID_LO[:, k, c0:c0 + cn], b[:, 0:cn],
                                               ACT.Relu).then_inc(*w.up(act_bank_free))
                            act.wait_ge(*w.own())
                            act.sem_inc(*w.up(act_ready_dve))
                        if q < QUARTERS - 1 or k < 2 * KC - SPLITS:
                            round_unit()
                        if both and (q < QUARTERS - 1 or k < KC):
                            ada_step()
                        if q == QUARTERS - 1 and k >= KC:
                            square_of_product(layer, 1, streams, k - KC)
                roots(streams, D)

            act.wait_ge(s_first, 48)
            act.activation(cond[:, :, :], cond[:, :, :], ACT.Silu).then_inc(*w.up(act_ready_pe))
            act.wait_ge(*w.next(dve_ready_act))
            for layer in range(LAYERS):
                layer_program(layer)
            squares(X, [X_COLS], each=True, rounding=True)
            loads.append(("memory", 0))
            roots([X_COLS], D)
            for k in range(KC):
                act.wait_ge(*w.next(dve_ready_act))
                for i, half in enumerate((slice(0, TX // 2), slice(TX // 2, TX))):
                    act.copy(H_HI_R[:, k, half], LAST_LO[k][i]).then_inc(*w.up(act_ready_dve if i else None))
            act.wait_ge(s_mem, 16)
            for k in range(KC):
                act.activation(MEM_SQ[:, k, :], MEM[:, k, :], ACT.Square).then_inc(*w.up(act_ready_pe))

            def head_step(i):
                if i < len(heads):
                    z, n = heads[i][0:2]
                    act.wait_ge(*w.own())
                    act.activation(tmp[:, (i % 2) * TX:(i % 2) * TX + n], z, ACT.Square).then_inc(*w.up(act_head_square))
                if 1 <= i <= len(heads):
                    if i >= 3:
                        act.wait_ge(*w.next(dve_ready_act))
                    n = heads[i - 1][1]
                    act.wait_ge(*w.next(pe_tile_for["act"]))
                    b = tile()
                    act.activation((rs, sq)[(i - 1) % 2][:, 0:n], b[:, 0:n], ACT.Sqrt,
                                   bias=eps).then_inc(*w.up(act_bank_free))
                    act.wait_ge(*w.own())
                    act.sem_inc(*w.up(act_ready_dve))

            def after(what):
                if what in step_after:
                    head_step(step_after.index(what))

            def into(dst, func=ACT.Copy, n=TX):
                act.wait_ge(*w.next(pe_tile_for["act"]))
                b = tile()
                act.activation(dst, b[:, 0:n], func).then_inc(*w.up(act_bank_free))

            for c in range(4):
                into(Q2[:, c, :])
                round_unit()
            roots([(TX, TC)], D)
            act.wait_ge(*w.next(dve_ready_act))
            act.activation(COS, SIN, ACT.Sin, scale=0.5).then_inc(*w.up())
            act.activation(SIN, SIN, ACT.Sin).then_inc(*w.up(act_ready_dve))
            for name, dst in (("k_raw", KRAW), ("v_raw", VRAW), ("ks", KS), ("kw", KW)):
                into(dst)
                round_unit()
                if name == "ks":
                    act.wait_ge(*w.own())
                    act.sem_inc(*w.up(act_ready_dve))
                after(name)
            for i in range(4):
                act.wait_ge(*w.next(pe_tile_for["act"]))
                b = tile()
                act.copy(VS[:, i, :], b[:, 0:P]).then_inc(*w.up())
                act.copy(VW[:, i, :], b[:, P:2 * P]).then_inc(*w.up(act_bank_free))
            round_unit()
            round_unit()
            after("v")
            for i in range(4):
                into(GATE[:, i, :], ACT.Sigmoid, 24)
            round_unit()
            after("gate")
            for m in range(4):
                loads.append(("direct", next(direct_turns)))
                if m < 2:
                    into(MK[:, m, :], n=TC)
                else:
                    act.wait_ge(*w.next(pe_tile_for["act"]))
                    b = tile()
                    act.copy(MV[:, :, (m - 2) * P:(m - 1) * P],
                             b[:, 0:2 * P].rearrange("p (i e) -> p i e", i=2)).then_inc(*w.up(act_bank_free))
            after("mem")
            for c in range(4):
                into(ZN[:, c, :], ACT.Silu)
                round_unit()
                if c == 0:
                    after("zn")
                loads.append(("direct", next(direct_turns)))
            into(HIDK, ACT.Gelu_apprx_tanh, NCMP)
            for c in range(2):
                into(VP[:, c, :])
                round_unit()
                loads.append(("direct", next(direct_turns)))
            act.wait_ge(*w.own())
            act.sem_inc(*w.up(act_ready_dve))
            for c in range(2):
                into(ZP[:, c, :], ACT.Silu)
                round_unit()
                loads.append(("direct", next(direct_turns)))
            into(HIDV, ACT.Gelu_apprx_tanh, NCMP)
            act.wait_ge(*w.own())
            act.sem_inc(*w.up(act_ready_pe))
            loads.append(("direct", next(direct_turns)))
            for c in range(2):
                into(QM[:, c, :])
                round_unit()
            into(KCMP, n=NCMP)
            act.wait_ge(*w.next(pe_tile_for["act"]))
            b = tile()
            act.activation(VCMP, ident.unsqueeze(1).to_broadcast([P, 4, P]), ACT.Copy,
                           scale=0.0).then_inc(*w.up())
            act.wait_ge(*w.own())
            for i in range(4):
                rows = slice(32 * i, 32 * i + NCMP)
                ins = act.copy(VCMP[rows, i, :], b[rows, 0:P])
                if i < 3:
                    ins.then_inc(*w.up())
            ins.then_inc(*w.up(act_bank_free))
            act.wait_ge(*w.own())
            after("k_cmp")
            for c in range(2):
                into(ZM[:, c, :], ACT.Silu)
                round_unit()
                after(f"zm{c}")
            for i in range(len(step_after), len(heads) + 2):
                head_step(i)
            act.wait_ge(*w.next(dve_ready_act, 2))
            act.wait_ge(*w.next(dve_ready_act))
            seen = CMP.rearrange("p g c t n -> p (g c t) n")[:, :, 0:NCMP]
            act.activation(seen, seen, ACT.Exp, scale=SCALE).then_inc(*w.up(act_ready_dve))
            for g in range(2):
                act.wait_ge(*w.next(pe_tile_for["act"]))
                b = tile()
                act.copy(CMPT[:, 4 * g:4 * g + 4, :], b[:, :].rearrange("p (c t) -> p c t", c=4)).then_inc(*w.up(act_bank_free))

            def exps(u):
                n, branches = keys_seen(u)
                o = 16 * (u % 2)
                act.wait_ge(*w.next(dve_ready_act))
                first = 2 * (u % 2)
                for j in range(branches):
                    act.activation(PROB[:, u % 2, j, 0:n], psum[:, first + j, 0:n], ACT.Exp, scale=SCALE,
                                   bias=small[:, o + 4 + j:o + 5 + j],
                                   accum_out=small[:, o + 8 + j:o + 9 + j]).then_inc(*w.up(act_scores_read if j == branches - 1 else None))
                act.wait_ge(*w.own())
                act.sem_inc(*w.up(act_ready_dve))

            def turned(u):
                n, branches = keys_seen(u)
                for j in range(branches):
                    act.wait_ge(*w.next(pe_tile_for["act"]))
                    b = tile()
                    act.copy(PROBT[:, u % 2, 4 * j:4 * j + n // P, :],
                             b[:, 0:n].rearrange("p (i t) -> p i t", t=P)).then_inc(*w.up(act_bank_free))
                act.wait_ge(*w.own())
                act.sem_inc(*w.up(act_ready_pe))

            def y_upper(k):
                act.wait_ge(*w.next(dve_y_ready))
                act.copy(Y_HI_R[:, k, :], Y[:, k, :]).then_inc(*w.up(act_y_upper))

            for u in range(len(UNITS) + 2):
                if 0 <= u - 2:
                    turned(u - 2)
                if u < len(UNITS):
                    exps(u)
                if u - 1 in SPLIT_AT:
                    y_upper(SPLIT_AT[u - 1])
            y_upper(KC - 1)
            for _ in range(KC - SPLITS):
                round_unit()

        @block.gpsimd
        def _(pool):
            w = Worker(None)
            for n in range(len(units)):
                pool.wait_ge(*w.next(act_ready_pool))
                slot = units[n][2] % SPLITS
                pool.tensor_tensor(W_R[:, slot, 1, :], WHOLE[n % RAWS],
                                   W_R[:, slot, 0, :].bitcast(F32), ALU.subtract).then_inc(*w.up(pool_ready_pe))

        @block.sync
        def _(sp):
            w = Worker(None)
            sp.dma_start(cond[:, :, :], a["cond"]).then_inc(s_first, 16)
            sp.dma_start(cols[:, :], a["cols"]).then_inc(s_first, 16)
            sp.dma_start(con[:, :], a["con"]).then_inc(s_first, 16)
            sp.dma_start(X[:, :, 0:TX], a["x"].rearrange("(k p) t -> p k t", p=P)).then_inc(s_x, 16)
            sp.dma_start(X[:, :, TX:T], a["ctx"].rearrange("(k p) t -> p k t", p=P)).then_inc(s_x, 16)
            sp.dma_start(GRID_ROWS, a["grid_rows"]).then_inc(s_pos, 16)
            sp.dma_start(GRID_COLS, a["grid_cols"]).then_inc(s_pos, 16)

            def load_whole(n):
                if n >= RAWS:
                    sp.wait_ge(pool_ready_pe.sem, n - RAWS + 1)
                dst = WHOLE[n % RAWS].rearrange("p (k n) -> p k n", k=KC)
                sp.dma_start(dst, units[n][0].rearrange("(k p) n -> p k n", p=P)).then_inc(whole_loaded[n % RAWS], 16)

            def load_direct(n):
                if n >= RAWS:
                    sp.wait_ge(*direct[n - RAWS][1])
                dst, src = DIRECT[n % RAWS], direct[n][0]
                if src.shape[1] < UNIT and src.shape[0] == P:
                    dst = dst[:, 0:src.shape[1]]
                if src.shape[0] == D:
                    dst, src = dst.rearrange("p (k n) -> p k n", k=KC), src.rearrange("(k p) n -> p k n", p=P)
                sp.dma_start(dst, src).then_inc(direct_loaded[n % RAWS], 16)

            kept = a["kept"].rearrange("(k p) t -> p k t", p=P)

            def keep(layer):
                tn = T if layer < LAYERS - 1 else TX
                for k in range(0, KC, 2):
                    sp.wait_ge(*marks["x", layer, k + 1])
                    sp.dma_start(kept[:, k:k + 2, 0:tn], X[:, k:k + 2, 0:tn]).then_inc(s_kept, 16)

            for i, place in enumerate(FIRST):
                if i == 2:
                    keep(0)
                sp.dma_start(place, a["w_ada"][0, :, i * 512:(i + 1) * 512].rearrange("(k p) n -> p k n",
                                                                                     p=P)).then_inc(first_loaded[i], 16)
            for what, n in loads:
                tn = T if n < LAYERS - 1 else TX
                if what == "memory":
                    sp.wait_ge(*w.next(dve_ready_sp))
                    sp.dma_start(MEM, a["mem"].rearrange("(k p) t -> p k t", p=P)).then_inc(s_mem, 16)
                    sp.dma_start(COS.bitcast(I32), a["positions"][0, :].partition_broadcast(P)).then_inc(s_tok, 16)
                elif what == "whole":
                    load_whole(n)
                elif what == "direct":
                    load_direct(n)
                elif what == "keep":
                    keep(n)
                elif what == "rows":
                    sp.wait_ge(*w.next(dve_ready_sp))
                    for j in range(4):
                        sp.dma_start(ROWS[0:4, j, :], sq[4 * j:4 * j + 4, :]).then_inc(s_rows, 16)
                else:
                    sp.wait_ge(*marks["h_read", n])
                    sp.wait_ge(s_kept, 64 * (n + 1))
                    sp.dma_start(X[:, :, 0:tn], kept[:, :, 0:tn]).then_inc(s_back, 16)
            sp.wait_ge(*w.next(dve_ready_sp))
            sp.dma_start(a["out"].rearrange("(k p) t -> p k t", p=P), X[:, :, 0:TX]).then_inc(s_out, 16)
            sp.wait_ge(s_out, 16)


def constants():
    i, j = np.arange(P)[:, None], np.arange(P)[None, :]
    c = np.zeros((P, NCONST), np.float32)

    def put(name, v):
        at, n = CONST[name]
        v = np.asarray(v)
        c[:v.shape[0], at:at + v.shape[1]] = v

    put("ident", np.eye(P))
    put("ones", np.ones((P, P)))
    put("ones64", (i // 64 == j // 64) / 64.0)
    turn = np.zeros((P, P))
    for g in (0, 64):
        for k in range(8):
            turn[g + 8 + k, g + k] = -1.0
            turn[g + k, g + 8 + k] = 1.0
    put("rope_turn", turn)
    ang = 2 * np.pi * (np.outer(np.arange(64), np.arange(64)) % 64) / 64
    chan = np.zeros((P, 256))
    for g in (0, 64):
        chan[g:g + 64, g:g + 64] = np.cos(ang) / 8
        chan[g:g + 64, P + g:P + g + 64] = np.sin(ang) / 8
    put("dft_chan", chan)
    put("hide_t_lt_s", np.where(j < i, BIG, 0.0))
    put("hide_t_gt_s", np.where(j > i, BIG, 0.0))
    put("hide_s_gt_t", np.where(j > i, -BIG, 0.0))
    hide = np.zeros((P, 4 * NCMP))
    for tb in range(4):
        hide[:, tb * NCMP:(tb + 1) * NCMP] = np.where(np.arange(NCMP)[None, :] * 16 + 31 > tb * P + i, -BIG, 0.0)
    put("cmp_hide", hide)
    put("head_rows", np.repeat(np.eye(4), P, axis=1))
    freq = np.zeros((P, 1), np.float32)
    inv = np.float32(500000.0) ** (-np.arange(8, dtype=np.float32) / np.float32(8))
    for g in (0, 8, 64, 72):
        freq[g:g + 8, 0] = inv
    put("rope_freq", freq)
    put("eps", np.full((P, 1), EPS))
    win = np.array([[2, 8], [4, 16]], np.float64)[np.arange(P) // 64]
    put("pool_inv", 1 / win)
    put("cond_pick", np.stack([np.arange(P) % 32 == v for v in range(2)], 1))
    t = np.arange(16)
    put("pool_first", (win[:, :, None] / np.minimum(t + 1, win[:, :, None])).reshape(P, 32))
    return c


def dft(n):
    ang = 2 * np.pi * (np.outer(np.arange(n), np.arange(n)) % n) / n
    m = np.stack([np.cos(ang), -np.sin(ang)]) / np.sqrt(n)
    return m.reshape(2, n // P, P, n).transpose(2, 1, 0, 3).reshape(P, -1).astype(np.float32)


def grid():
    quarter = D // 4
    freq = np.exp(np.float32(-np.log(10000.0)) * np.arange(quarter, dtype=np.float32) / np.float32(quarter))
    freq = freq.astype(np.float32)
    tables = []
    for n in (TX // GRID, GRID):
        angle = np.arange(n, dtype=np.float32)[:, None] * freq
        table = np.concatenate([np.sin(angle), np.cos(angle)], -1).T
        tables.append(np.ascontiguousarray(table.reshape(KC // 2, P, n).transpose(1, 0, 2), np.float32))
    return tables


def columns(inputs):
    out = np.zeros((P, NCOL), np.float32)

    def put(at, v):
        v = np.asarray(v, np.float32).reshape(-1, P).T
        out[:, at:at + v.shape[1]] = v

    for layer in range(LAYERS):
        for name, k in LAYER_COLS:
            v = np.asarray(inputs[name])[layer]
            if name == "b_gate":
                out[:16, COL[name, layer]] = v.reshape(16)
            else:
                put(COL[name, layer], v)
    for name, k in LAST_COLS:
        v = np.asarray(inputs[name])[0]
        if name.startswith("cmp_pos"):
            out[:, COL[name]:COL[name] + 32] = np.tile(v.T, (2, 1))
        elif v.shape[0] == 64:
            out[:, COL[name]] = np.tile(v, 2)
        else:
            put(COL[name], v)
    return out


def twice(w):
    out = np.zeros(w.shape[:-2] + (P, P), np.float32)
    out[..., :64, :64] = w
    out[..., 64:, 64:] = w
    return out


def head_order(n):
    return np.arange(n).reshape(2, 4, 64).transpose(1, 0, 2).reshape(-1)


def arrays_of(inputs):
    f = {k: np.asarray(v) for k, v in inputs.items()}
    perm = head_order(512)
    cols_in = np.arange(W_IN2)
    cols_in[0:512] = perm
    cols_in[1304:1816] = 1304 + perm
    cols_in[896:1024], cols_in[1024:1152] = cols_in[1024:1152].copy(), cols_in[896:1024].copy()
    rows_out = np.arange(1024)
    rows_out[0:512] = perm
    wp = f["w_pool_2"][0]
    small_w = np.zeros((P, 4, P), np.float32)
    small_w[:, 0] = twice(f["w_cmp_k2_2"][0])
    small_w[:, 1] = twice(f["w_cmp_v2_2"][0])
    for c in range(2):
        small_w[:64, 2 + c, :64] = wp[2 * c]
        small_w[64:, 2 + c, 64:] = wp[2 * c + 1]
    cmp1 = np.stack([twice(f[n][0]).transpose(1, 0, 2).reshape(P, -1) for n in ("w_cmp_k1_2", "w_cmp_v1_2")])
    cond = np.zeros((P, KC, 32), np.float32)
    cond[:, :, 0:2] = np.stack([f["c"][0], f["c_ctx"]]).reshape(2, KC, P).transpose(2, 1, 0)
    return {
        "x": np.ascontiguousarray(f["x"][0].T), "ctx": np.ascontiguousarray(f["ctx"][0].T),
        "mem": np.ascontiguousarray(f["mem_2"][0].T), "positions": f["positions_2"],
        "cond": cond,
        "w_ada": f["w_ada"], "w_in": f["w_in"], "w_out": f["w_out"], "w_mlp1": f["w_mlp1"], "w_mlp2": f["w_mlp2"],
        "w_mem_kv_2": f["w_mem_kv_2"], "w_in_2": np.ascontiguousarray(f["w_in_2"][:, :, cols_in]),
        "w_out_2": np.ascontiguousarray(f["w_out_2"][:, rows_out, :]), "w_cmp1": cmp1,
        "w_small": small_w.reshape(P, -1), "cols": columns(inputs), "con": constants(),
        "grid_rows": grid()[0], "grid_cols": grid()[1],
        "dft_x": dft(TX), "dft_c": dft(TC),
    }


def declare(nc, arrays):
    a = {}
    for name, v in arrays.items():
        a[name] = nc.dram_tensor(f"in_{name}", v.shape, mybir.dt.from_np(v.dtype), kind="ExternalInput").ap()
    a["kept"] = nc.dram_tensor("kept", [D, T], F32, kind="Internal").ap()
    a["out"] = nc.dram_tensor("out", [D, TX], F32, kind="ExternalOutput").ap()
    build(nc, a)


def kernel(**inputs):
    import concourse.bacc as bacc
    from concourse.bass_utils import run_bass_kernel_spmd

    arrays = arrays_of(inputs)
    nc = bacc.Bacc("TRN2", target_bir_lowering=False, num_devices=1)
    declare(nc, arrays)
    r = run_bass_kernel_spmd(nc, [{f"in_{k}": v for k, v in arrays.items()}], core_ids=[0])
    return np.ascontiguousarray(r.results[0]["out"].T)[None]
```
